# Optimizing a Trainium2 kernel written in Bass

```python
import jax, jax.numpy as jnp
from jax import lax
import numpy as np
import functools

D_MODEL = 1024
BATCH = 1
SEQ = 256
DEPTH = 2

NSA_HEADS = 8
NSA_KV_GROUPS = 2
NSA_HPG = NSA_HEADS // NSA_KV_GROUPS
NSA_HEAD_DIM = 64
NSA_WIDTH = NSA_HEADS * NSA_HEAD_DIM
NSA_KV_WIDTH = NSA_KV_GROUPS * NSA_HEAD_DIM
NSA_N_KV = 6
CMP_BLOCK = 32
CMP_STRIDE = 16
SEL_BLOCK = 64
SEL_TOP_N = 16
WINDOW = 512
NSA_QBLOCK = 64
POOL_WINDOWS = (2, 4, 8, 16)
POOL_GROUPS = len(POOL_WINDOWS)
POOL_WIDTH = D_MODEL - NSA_WIDTH
POOL_GROUP_DIM = POOL_WIDTH // POOL_GROUPS
A_IN = NSA_WIDTH + NSA_N_KV * NSA_KV_WIDTH + 3 * NSA_HEADS + POOL_WIDTH
GLA_HEADS = 4
GLA_KEY_WIDTH = D_MODEL // 2
GLA_VAL_WIDTH = D_MODEL
GLA_DK = GLA_KEY_WIDTH // GLA_HEADS
GLA_DV = GLA_VAL_WIDTH // GLA_HEADS
GLA_GATE_RANK = 16
GLA_TAU = 16.0
GLA_CHUNK = 64
C_IN = 2 * GLA_KEY_WIDTH + 2 * GLA_VAL_WIDTH + GLA_GATE_RANK
D_FF = 4 * D_MODEL
N_EVEN = (DEPTH + 1) // 2
N_ODD = DEPTH // 2
ALPHA = (2 * DEPTH) ** 0.25
BETA = (8 * DEPTH) ** -0.25
LN_EPS = 1e-5
MASK_VALUE = -1e30
FORCE_SCORE = 1e4


def layer_norm(x, g, b):
    xf = x.astype(jnp.float32)
    mu = jnp.mean(xf, axis=-1, keepdims=True)
    var = jnp.mean(jnp.square(xf - mu), axis=-1, keepdims=True)
    return ((xf - mu) * lax.rsqrt(var + LN_EPS) * g + b).astype(x.dtype)

def masked_softmax(s, mask):
    s = jnp.where(mask, s.astype(jnp.float32), MASK_VALUE)
    m = jnp.max(s, axis=-1, keepdims=True)
    e = jnp.where(mask, jnp.exp(s - m), 0.0)
    return e / jnp.maximum(jnp.sum(e, axis=-1, keepdims=True), 1e-30)

def compress_blocks(k, pos, w1, b1, w2):
    S = k.shape[2]
    n_cmp = (S - CMP_BLOCK) // CMP_STRIDE + 1
    idx = np.arange(n_cmp)[:, None] * CMP_STRIDE + np.arange(CMP_BLOCK)[None, :]
    blocks = k[:, :, idx, :] + pos
    flat = blocks.reshape(blocks.shape[:3] + (CMP_BLOCK * NSA_HEAD_DIM,))
    return jax.nn.gelu(flat @ w1 + b1) @ w2

def selection_map(n_cmp, n_sel):
    sub = np.arange(n_cmp)[:, None] + np.arange(CMP_BLOCK // CMP_STRIDE)[None, :]
    owner = sub // (SEL_BLOCK // CMP_STRIDE)
    return (owner[:, :, None] == np.arange(n_sel)[None, None, :]).sum(1).astype(np.float32)

def pool_mixer(u, pool_w, pool_scale):
    B, S, _ = u.shape
    uf = u.astype(jnp.float32).reshape(B, S, POOL_GROUPS, POOL_GROUP_DIM)
    cs = jnp.pad(jnp.cumsum(uf, axis=1), ((0, 0), (1, 0), (0, 0), (0, 0)))
    count_base = jnp.arange(1, S + 1, dtype=jnp.float32)
    outs = []
    for g, w in enumerate(POOL_WINDOWS):
        c = cs[:, :, g]
        lower = jnp.pad(c[:, :S + 1 - w], ((0, 0), (w - 1, 0), (0, 0)))
        mean = (c[:, 1:] - lower) / jnp.minimum(count_base, float(w))[None, :, None]
        outs.append(mean - uf[:, :, g])
    r = jnp.stack(outs, axis=2)
    y = jnp.einsum('bsgc,gcd->bsgd', r, pool_w.astype(jnp.float32))
    return (y.reshape(B, S, POOL_WIDTH) * pool_scale).astype(u.dtype)

def nsa_pool_mixer(x, w_in, cmp_pos, cmp_w1, cmp_b1, cmp_w2, pool_w, pool_scale, w_out):
    B, S, _ = x.shape
    G, HPG, DH = NSA_KV_GROUPS, NSA_HPG, NSA_HEAD_DIM
    h = x @ w_in
    o1 = NSA_WIDTH
    o2 = o1 + NSA_N_KV * NSA_KV_WIDTH
    o3 = o2 + 3 * NSA_HEADS
    q = h[..., :o1].reshape(B, S, G, HPG, DH).transpose(0, 2, 3, 1, 4)
    kv = h[..., o1:o2].reshape(B, S, NSA_N_KV, G, DH).transpose(2, 0, 3, 1, 4)
    gates = jax.nn.sigmoid(h[..., o2:o3].astype(jnp.float32))
    gates = gates.reshape(B, S, G, HPG, 3).transpose(0, 2, 3, 1, 4)
    u = h[..., o3:]
    k_cmp, v_cmp, k_slc, v_slc, k_win, v_win = kv[0], kv[1], kv[2], kv[3], kv[4], kv[5]

    kc = compress_blocks(k_cmp, cmp_pos[0], cmp_w1[0], cmp_b1[0], cmp_w2[0])
    vc = compress_blocks(v_cmp, cmp_pos[1], cmp_w1[1], cmp_b1[1], cmp_w2[1])
    n_cmp = kc.shape[2]
    n_sel = S // SEL_BLOCK
    top_n = min(SEL_TOP_N, n_sel)
    sel_map = jnp.asarray(selection_map(n_cmp, n_sel))
    cmp_end = jnp.arange(n_cmp) * CMP_STRIDE + CMP_BLOCK - 1
    ks_b = k_slc.reshape(B, G, n_sel, SEL_BLOCK, DH)
    vs_b = v_slc.reshape(B, G, n_sel, SEL_BLOCK, DH)
    kw = jnp.pad(k_win, ((0, 0), (0, 0), (WINDOW, 0), (0, 0)))
    vw = jnp.pad(v_win, ((0, 0), (0, 0), (WINDOW, 0), (0, 0)))
    bi = jnp.arange(B)[:, None, None, None]
    gi = jnp.arange(G)[None, :, None, None]
    scale = DH ** -0.5

    def query_block(i):
        t0 = i * NSA_QBLOCK
        t = t0 + jnp.arange(NSA_QBLOCK)
        qb = lax.dynamic_slice_in_dim(q, t0, NSA_QBLOCK, axis=3) * scale
        gb = lax.dynamic_slice_in_dim(gates, t0, NSA_QBLOCK, axis=3)
        s_c = jnp.einsum('bghqd,bgcd->bghqc', qb, kc)
        p_c = masked_softmax(s_c, cmp_end[None, :] <= t[:, None])
        o_c = jnp.einsum('bghqc,bgcd->bghqd', p_c.astype(vc.dtype), vc)
        imp = jnp.einsum('bghqc,cj->bgqj', p_c, sel_map)
        blk = jnp.arange(n_sel)[None, :]
        cur = (t // SEL_BLOCK)[:, None]
        forced = (blk == 0) | (blk == cur) | (blk == cur - 1)
        imp = jnp.where(forced, FORCE_SCORE, jnp.where(blk > cur, -FORCE_SCORE, imp))
        _, sel = lax.top_k(imp, top_n)
        k_sel = ks_b[bi, gi, sel].reshape(B, G, NSA_QBLOCK, top_n * SEL_BLOCK, DH)
        v_sel = vs_b[bi, gi, sel].reshape(B, G, NSA_QBLOCK, top_n * SEL_BLOCK, DH)
        kpos = (sel[..., None] * SEL_BLOCK + jnp.arange(SEL_BLOCK)).reshape(
            B, G, NSA_QBLOCK, top_n * SEL_BLOCK)
        s_s = jnp.einsum('bghqd,bgqnd->bghqn', qb, k_sel)
        p_s = masked_softmax(s_s, (kpos <= t[:, None])[:, :, None])
        o_s = jnp.einsum('bghqn,bgqnd->bghqd', p_s.astype(v_sel.dtype), v_sel)
        k_w = lax.dynamic_slice_in_dim(kw, t0, WINDOW + NSA_QBLOCK, axis=2)
        v_w = lax.dynamic_slice_in_dim(vw, t0, WINDOW + NSA_QBLOCK, axis=2)
        wpos = t0 - WINDOW + jnp.arange(WINDOW + NSA_QBLOCK)
        wmask = ((wpos[None, :] <= t[:, None]) & (wpos[None, :] > t[:, None] - WINDOW)
                 & (wpos[None, :] >= 0))
        s_w = jnp.einsum('bghqd,bgkd->bghqk', qb, k_w)
        p_w = masked_softmax(s_w, wmask)
        o_w = jnp.einsum('bghqk,bgkd->bghqd', p_w.astype(v_w.dtype), v_w)
        o = gb[..., 0:1] * o_c + gb[..., 1:2] * o_s + gb[..., 2:3] * o_w
        return o.astype(x.dtype)

    ob = lax.map(query_block, jnp.arange(S // NSA_QBLOCK))
    o_nsa = ob.transpose(1, 0, 4, 2, 3, 5).reshape(B, S, NSA_WIDTH)
    o_pool = pool_mixer(u, pool_w, pool_scale)
    return jnp.concatenate([o_nsa, o_pool], axis=-1) @ w_out

def gla_mixer(x, w_in, gate_w2, gate_b, norm_g, w_out):
    B, S, _ = x.shape
    N, C, H = S // GLA_CHUNK, GLA_CHUNK, GLA_HEADS
    h = x @ w_in
    o1 = GLA_KEY_WIDTH
    o2 = o1 + GLA_KEY_WIDTH
    o3 = o2 + GLA_VAL_WIDTH
    o4 = o3 + GLA_VAL_WIDTH
    q_, k_, v_, r, a = h[..., :o1], h[..., o1:o2], h[..., o2:o3], h[..., o3:o4], h[..., o4:]
    loga = jax.nn.log_sigmoid((a @ gate_w2 + gate_b).astype(jnp.float32)) / GLA_TAU

    def heads(t, d):
        return t.reshape(B, N, C, H, d).transpose(0, 3, 1, 2, 4).astype(jnp.float32)

    q = heads(q_, GLA_DK) * GLA_DK ** -0.5
    k = heads(k_, GLA_DK)
    v = heads(v_, GLA_DV)
    b = jnp.cumsum(heads(loga, GLA_DK), axis=3)
    q_t = q * jnp.exp(b)
    k_t = k * jnp.exp(-b)
    causal = jnp.tril(jnp.ones((C, C), dtype=bool))
    att = jnp.where(causal, jnp.einsum('bhncd,bhnjd->bhncj', q_t, k_t), 0.0)
    o_intra = jnp.einsum('bhncj,bhnje->bhnce', att, v)
    b_last = b[:, :, :, -1:, :]
    upd = jnp.einsum('bhncd,bhnce->bhnde', k * jnp.exp(b_last - b), v)
    decay = jnp.exp(b_last[:, :, :, 0])

    def step(state, inp):
        d, u = inp
        return d[..., None] * state + u, state

    s0 = jnp.zeros((B, H, GLA_DK, GLA_DV), jnp.float32)
    _, s_prev = lax.scan(step, s0, (jnp.moveaxis(decay, 2, 0), jnp.moveaxis(upd, 2, 0)))
    s_prev = jnp.moveaxis(s_prev, 0, 2)
    o = o_intra + jnp.einsum('bhncd,bhnde->bhnce', q_t, s_prev)
    o = o * lax.rsqrt(jnp.mean(jnp.square(o), axis=-1, keepdims=True) + LN_EPS) * norm_g
    o = o.transpose(0, 2, 3, 1, 4).reshape(B, S, GLA_VAL_WIDTH).astype(x.dtype)
    return (o * jax.nn.silu(r)) @ w_out

def sqrelu_mlp(x, w1, w2):
    return jnp.square(jax.nn.relu(x @ w1)) @ w2

def first_inputs(seed: int = 0) -> dict:
    key = jax.random.key(seed)
    ks = jax.random.split(key, 24)

    def nrm(k, shape, scale):
        return jax.random.normal(k, shape, jnp.float32) * scale

    DH = NSA_HEAD_DIM
    return {
        "x": nrm(ks[0], (BATCH, SEQ, D_MODEL), 1.0),
        "a_w_in": nrm(ks[1], (N_EVEN, D_MODEL, A_IN), D_MODEL ** -0.5),
        "a_cmp_pos": nrm(ks[2], (N_EVEN, 2, CMP_BLOCK, DH), 0.1),
        "a_cmp_w1": nrm(ks[3], (N_EVEN, 2, CMP_BLOCK * DH, DH), (CMP_BLOCK * DH) ** -0.5),
        "a_cmp_b1": nrm(ks[4], (N_EVEN, 2, DH), 0.02),
        "a_cmp_w2": nrm(ks[5], (N_EVEN, 2, DH, DH), DH ** -0.5),
        "a_pool_w": nrm(ks[6], (N_EVEN, POOL_GROUPS, POOL_GROUP_DIM, POOL_GROUP_DIM), POOL_GROUP_DIM ** -0.5),
        "a_pool_scale": 1.0 + nrm(ks[7], (N_EVEN, POOL_WIDTH), 0.1),
        "a_w_out": nrm(ks[8], (N_EVEN, D_MODEL, D_MODEL), BETA * D_MODEL ** -0.5),
        "c_w_in": nrm(ks[9], (N_ODD, D_MODEL, C_IN), D_MODEL ** -0.5),
        "c_gate_w2": nrm(ks[10], (N_ODD, GLA_GATE_RANK, GLA_KEY_WIDTH), GLA_GATE_RANK ** -0.5),
        "c_gate_b": nrm(ks[11], (N_ODD, GLA_KEY_WIDTH), 0.1),
        "c_norm_g": 1.0 + nrm(ks[12], (N_ODD, GLA_DV), 0.1),
        "c_w_out": nrm(ks[13], (N_ODD, D_MODEL, D_MODEL), BETA * D_MODEL ** -0.5),
        "ln1_g": 1.0 + nrm(ks[14], (DEPTH, D_MODEL), 0.05),
        "ln1_b": nrm(ks[15], (DEPTH, D_MODEL), 0.02),
        "ln2_g": 1.0 + nrm(ks[16], (DEPTH, D_MODEL), 0.05),
        "ln2_b": nrm(ks[17], (DEPTH, D_MODEL), 0.02),
        "mlp_w1": nrm(ks[18], (DEPTH, D_MODEL, D_FF), D_MODEL ** -0.5),
        "mlp_w2": nrm(ks[19], (DEPTH, D_FF, D_MODEL), BETA * D_FF ** -0.5),
    }

def first_block(x, a_w_in, a_cmp_pos, a_cmp_w1, a_cmp_b1, a_cmp_w2, a_pool_w, a_pool_scale,
              a_w_out, c_w_in, c_gate_w2, c_gate_b, c_norm_g, c_w_out,
              ln1_g, ln1_b, ln2_g, ln2_b, mlp_w1, mlp_w2):
    for i in range(DEPTH):
        j = i // 2
        if i % 2 == 0:
            mix = nsa_pool_mixer(x, a_w_in[j], a_cmp_pos[j], a_cmp_w1[j], a_cmp_b1[j],
                                 a_cmp_w2[j], a_pool_w[j], a_pool_scale[j], a_w_out[j])
        else:
            mix = gla_mixer(x, c_w_in[j], c_gate_w2[j], c_gate_b[j], c_norm_g[j], c_w_out[j])
        x = layer_norm(ALPHA * x + mix, ln1_g[i], ln1_b[i])
        x = layer_norm(ALPHA * x + sqrelu_mlp(x, mlp_w1[i], mlp_w2[i]), ln2_g[i], ln2_b[i])
    return x


DEPTH_2 = 1

DN_HEADS = 8
DN_HEAD_DIM = 128
DN_DIM = DN_HEADS * DN_HEAD_DIM
DN_CHUNK = 64
CONV_WIDTH = 4
SGU_GROUPS = 8
SGU_GROUP_DIM = 128
SGU_DIM = SGU_GROUPS * SGU_GROUP_DIM
SGU_CHUNK = 128
N_GROUPS = 4
EXPERTS_PER_GROUP = 4
N_EXPERTS = N_GROUPS * EXPERTS_PER_GROUP
TOP_K_IN_GROUP = 2
EXPERT_FF = 256
DEEPNORM_ALPHA = (2.0 * DEPTH_2) ** 0.25
DEEPNORM_BETA = (8.0 * DEPTH_2) ** -0.25
NORM_EPS = 1e-6
PROJ_SIZES = (3 * DN_DIM, DN_DIM, DN_HEADS, DN_HEADS, 2 * SGU_DIM, D_MODEL, D_MODEL)
PROJ_DIM = sum(PROJ_SIZES)


def layer_norm_2(x, g, b):
    xf = x.astype(jnp.float32)
    xc = xf - jnp.mean(xf, axis=-1, keepdims=True)
    var = jnp.mean(xc * xc, axis=-1, keepdims=True)
    return (xc * lax.rsqrt(var + LN_EPS) * g + b).astype(x.dtype)

def l2_normalize(x):
    return x * lax.rsqrt(jnp.sum(x * x, axis=-1, keepdims=True) + NORM_EPS)

def causal_depthwise_conv(x, w):
    k = w.shape[0]
    return lax.conv_general_dilated(
        x, w[:, None, :], window_strides=(1,), padding=[(k - 1, 0)],
        dimension_numbers=("NWC", "WIO", "NWC"), feature_group_count=x.shape[-1])

def gated_delta_rule(q, k, v, g, beta):
    bsz, seq, heads, dk = q.shape
    dv = v.shape[-1]
    n = seq // DN_CHUNK

    def to_chunks(t):
        return jnp.swapaxes(t.reshape(bsz, n, DN_CHUNK, heads, *t.shape[3:]), 2, 3)

    q, k, v, g, beta = (to_chunks(t) for t in (q, k, v, g, beta))
    g_cum = jnp.cumsum(g, axis=-1)
    idx = jnp.arange(DN_CHUNK)
    causal = idx[:, None] >= idx[None, :]
    strict = idx[:, None] > idx[None, :]
    diff = g_cum[..., :, None] - g_cum[..., None, :]
    decay = jnp.where(causal, jnp.exp(jnp.where(causal, diff, 0.0)), 0.0)
    k_beta = k * beta[..., None]
    v_beta = v * beta[..., None]
    a_mat = jnp.where(strict, jnp.einsum("bnhtk,bnhsk->bnhts", k_beta, k) * decay, 0.0) \
        + jnp.eye(DN_CHUNK, dtype=q.dtype)
    solve = functools.partial(lax.linalg.triangular_solve, left_side=True, lower=True,
                              unit_diagonal=True)
    u = solve(a_mat, v_beta)
    w = solve(a_mat, k_beta * jnp.exp(g_cum)[..., None])
    qk = jnp.einsum("bnhtk,bnhsk->bnhts", q, k) * decay
    q_dec = q * jnp.exp(g_cum)[..., None]
    k_dec = k * jnp.exp(g_cum[..., -1:] - g_cum)[..., None]
    g_last = jnp.exp(g_cum[..., -1])

    def step(state, inp):
        qk_c, u_c, w_c, q_c, k_c, gl_c = inp
        v_new = u_c - jnp.einsum("bhtk,bhkv->bhtv", w_c, state)
        out = jnp.einsum("bhtk,bhkv->bhtv", q_c, state) + jnp.einsum("bhts,bhsv->bhtv", qk_c, v_new)
        state = state * gl_c[..., None, None] + jnp.einsum("bhsk,bhsv->bhkv", k_c, v_new)
        return state, out

    xs = tuple(jnp.moveaxis(t, 1, 0) for t in (qk, u, w, q_dec, k_dec, g_last))
    state0 = jnp.zeros((bsz, heads, dk, dv), jnp.float32)
    _, out = lax.scan(step, state0, xs)
    return jnp.transpose(out, (1, 0, 3, 2, 4)).reshape(bsz, seq, heads, dv)

def spatial_gating(uv, ln_g, ln_b, spatial_w, spatial_b, w_sgu_out):
    bsz, seq, _ = uv.shape
    n = seq // SGU_CHUNK
    u, v = jnp.split(jax.nn.gelu(uv, approximate=False), 2, axis=-1)
    v = layer_norm_2(v, ln_g, ln_b)
    v = v.reshape(bsz, n, SGU_CHUNK, SGU_GROUPS, SGU_GROUP_DIM)
    idx = jnp.arange(SGU_CHUNK)
    causal = idx[:, None] >= idx[None, :]
    w_causal = jnp.where(causal, spatial_w, 0)
    v = jnp.einsum("gts,bnsgc->bntgc", w_causal, v) + spatial_b.T[:, :, None]
    gated = u * v.reshape(bsz, seq, SGU_DIM)
    return jnp.einsum("blc,cd->bld", gated, w_sgu_out)

def hybrid_mixer(x, w_in, conv_w, a_log, dt_bias, dn_norm_g, w_dn_out,
                 sgu_ln_g, sgu_ln_b, spatial_w, spatial_b, w_sgu_out, w_out):
    bsz, seq, _ = x.shape
    f32 = jnp.float32
    proj = jnp.einsum("bld,dp->blp", x, w_in)
    offsets = np.cumsum(PROJ_SIZES)[:-1].tolist()
    qkv, z, a, b, uv, gate_dn, gate_sgu = jnp.split(proj, offsets, axis=-1)

    qkv = jax.nn.silu(causal_depthwise_conv(qkv, conv_w)).astype(f32)
    q, k, v = jnp.split(qkv, 3, axis=-1)
    to_heads = lambda t: t.reshape(bsz, seq, DN_HEADS, DN_HEAD_DIM)
    q = l2_normalize(to_heads(q)) * (DN_HEAD_DIM ** -0.5)
    k = l2_normalize(to_heads(k))
    v = to_heads(v)
    beta = jax.nn.sigmoid(b.astype(f32))
    g = -jnp.exp(a_log.astype(f32)) * jax.nn.softplus(a.astype(f32) + dt_bias.astype(f32))
    o = gated_delta_rule(q, k, v, g, beta)
    o = o * lax.rsqrt(jnp.mean(o * o, axis=-1, keepdims=True) + NORM_EPS) * dn_norm_g.astype(f32)
    o = o * jax.nn.silu(to_heads(z).astype(f32))
    y_dn = jnp.einsum("blc,cd->bld", o.reshape(bsz, seq, DN_DIM).astype(x.dtype), w_dn_out)

    y_sgu = spatial_gating(uv, sgu_ln_g, sgu_ln_b, spatial_w, spatial_b, w_sgu_out)

    y = jax.nn.sigmoid(gate_dn) * y_dn + jax.nn.sigmoid(gate_sgu) * y_sgu
    return jnp.einsum("bld,de->ble", y, w_out)

def hierarchical_moe(x, router_group_w, router_group_b, router_expert_w, router_expert_b,
                     expert_w_gate, expert_w_up, expert_w_down):
    bsz, seq, d = x.shape
    f32 = jnp.float32
    t = x.reshape(bsz * seq, d)
    n_tok = t.shape[0]
    group_logits = (t @ router_group_w + router_group_b).astype(f32)
    group_p, group_idx = lax.top_k(jax.nn.softmax(group_logits, axis=-1), 1)
    group_p, group_idx = group_p[:, 0], group_idx[:, 0]
    expert_logits = (t @ router_expert_w + router_expert_b).astype(f32)
    expert_logits = expert_logits.reshape(n_tok, N_GROUPS, EXPERTS_PER_GROUP)
    in_group = expert_logits[jnp.arange(n_tok), group_idx]
    exp_p, exp_idx = lax.top_k(jax.nn.softmax(in_group, axis=-1), TOP_K_IN_GROUP)
    exp_p = exp_p / jnp.sum(exp_p, axis=-1, keepdims=True)
    gate = group_p[:, None] * exp_p
    expert_id = group_idx[:, None] * EXPERTS_PER_GROUP + exp_idx
    combine = jnp.sum(jax.nn.one_hot(expert_id, N_EXPERTS, dtype=f32) * gate[..., None], axis=1)
    h = jax.nn.silu(jnp.einsum("td,edf->tef", t, expert_w_gate)) \
        * jnp.einsum("td,edf->tef", t, expert_w_up)
    h = h * combine[:, :, None].astype(h.dtype)
    y = jnp.einsum("tef,efd->td", h, expert_w_down)
    return y.reshape(bsz, seq, d)

def second_inputs(seed: int = 0) -> dict:
    key = jax.random.key(seed)
    ks = jax.random.split(key, 24)
    f32 = jnp.float32
    nrm = lambda k, shape, scale: jax.random.normal(k, shape, f32) * scale
    dt = jnp.exp(jax.random.uniform(ks[4], (DEPTH_2, DN_HEADS), f32,
                                    minval=float(np.log(1e-3)), maxval=float(np.log(1e-1))))
    return {
        "x": nrm(ks[0], (BATCH, SEQ, D_MODEL), 1.0),
        "w_in": nrm(ks[1], (DEPTH_2, D_MODEL, PROJ_DIM), D_MODEL ** -0.5),
        "conv_w": nrm(ks[2], (DEPTH_2, CONV_WIDTH, 3 * DN_DIM), CONV_WIDTH ** -0.5),
        "a_log": jnp.log(jax.random.uniform(ks[3], (DEPTH_2, DN_HEADS), f32, minval=1.0, maxval=16.0)),
        "dt_bias": dt + jnp.log(-jnp.expm1(-dt)),
        "dn_norm_g": 1.0 + nrm(ks[5], (DEPTH_2, DN_HEAD_DIM), 0.1),
        "w_dn_out": nrm(ks[6], (DEPTH_2, DN_DIM, D_MODEL), DN_DIM ** -0.5),
        "sgu_ln_g": 1.0 + nrm(ks[7], (DEPTH_2, SGU_DIM), 0.1),
        "sgu_ln_b": nrm(ks[8], (DEPTH_2, SGU_DIM), 0.02),
        "spatial_w": nrm(ks[9], (DEPTH_2, SGU_GROUPS, SGU_CHUNK, SGU_CHUNK), 0.05),
        "spatial_b": 1.0 + nrm(ks[10], (DEPTH_2, SGU_GROUPS, SGU_CHUNK), 0.1),
        "w_sgu_out": nrm(ks[11], (DEPTH_2, SGU_DIM, D_MODEL), SGU_DIM ** -0.5),
        "w_out": nrm(ks[12], (DEPTH_2, D_MODEL, D_MODEL), D_MODEL ** -0.5 * DEEPNORM_BETA),
        "ln1_g": 1.0 + nrm(ks[13], (DEPTH_2, D_MODEL), 0.1),
        "ln1_b": nrm(ks[14], (DEPTH_2, D_MODEL), 0.02),
        "router_group_w": nrm(ks[15], (DEPTH_2, D_MODEL, N_GROUPS), D_MODEL ** -0.5),
        "router_group_b": nrm(ks[16], (DEPTH_2, N_GROUPS), 0.01),
        "router_expert_w": nrm(ks[17], (DEPTH_2, D_MODEL, N_EXPERTS), D_MODEL ** -0.5),
        "router_expert_b": nrm(ks[18], (DEPTH_2, N_EXPERTS), 0.01),
        "expert_w_gate": nrm(ks[19], (DEPTH_2, N_EXPERTS, D_MODEL, EXPERT_FF), D_MODEL ** -0.5),
        "expert_w_up": nrm(ks[20], (DEPTH_2, N_EXPERTS, D_MODEL, EXPERT_FF), D_MODEL ** -0.5),
        "expert_w_down": nrm(ks[21], (DEPTH_2, N_EXPERTS, EXPERT_FF, D_MODEL), EXPERT_FF ** -0.5 * DEEPNORM_BETA),
        "ln2_g": 1.0 + nrm(ks[22], (DEPTH_2, D_MODEL), 0.1),
        "ln2_b": nrm(ks[23], (DEPTH_2, D_MODEL), 0.02),
    }

def second_block(x, w_in, conv_w, a_log, dt_bias, dn_norm_g, w_dn_out, sgu_ln_g, sgu_ln_b,
              spatial_w, spatial_b, w_sgu_out, w_out, ln1_g, ln1_b,
              router_group_w, router_group_b, router_expert_w, router_expert_b,
              expert_w_gate, expert_w_up, expert_w_down, ln2_g, ln2_b):
    h = x
    for l in range(DEPTH_2):
        mix = hybrid_mixer(h, w_in[l], conv_w[l], a_log[l], dt_bias[l], dn_norm_g[l], w_dn_out[l],
                           sgu_ln_g[l], sgu_ln_b[l], spatial_w[l], spatial_b[l], w_sgu_out[l], w_out[l])
        h = layer_norm_2(DEEPNORM_ALPHA * h + mix, ln1_g[l], ln1_b[l])
        ffn = hierarchical_moe(h, router_group_w[l], router_group_b[l], router_expert_w[l],
                               router_expert_b[l], expert_w_gate[l], expert_w_up[l], expert_w_down[l])
        h = layer_norm_2(DEEPNORM_ALPHA * h + ffn, ln2_g[l], ln2_b[l])
    return h


def setup_inputs(seed=0):
    out = dict(first_inputs(seed))
    for name, value in second_inputs(seed + 1).items():
        if name != "x":
            out[name + "_2"] = value
    return out


def reference(
    x, a_w_in, a_cmp_pos, a_cmp_w1, a_cmp_b1, a_cmp_w2, a_pool_w, a_pool_scale, a_w_out, c_w_in,
    c_gate_w2, c_gate_b, c_norm_g, c_w_out, ln1_g, ln1_b, ln2_g, ln2_b, mlp_w1, mlp_w2, w_in_2,
    conv_w_2, a_log_2, dt_bias_2, dn_norm_g_2, w_dn_out_2, sgu_ln_g_2, sgu_ln_b_2, spatial_w_2,
    spatial_b_2, w_sgu_out_2, w_out_2, ln1_g_2, ln1_b_2, router_group_w_2, router_group_b_2,
    router_expert_w_2, router_expert_b_2, expert_w_gate_2, expert_w_up_2, expert_w_down_2,
    ln2_g_2, ln2_b_2,
):
    x = first_block(
        x, a_w_in, a_cmp_pos, a_cmp_w1, a_cmp_b1, a_cmp_w2, a_pool_w, a_pool_scale, a_w_out,
        c_w_in, c_gate_w2, c_gate_b, c_norm_g, c_w_out, ln1_g, ln1_b, ln2_g, ln2_b, mlp_w1,
        mlp_w2,
    )
    return second_block(
        x, w_in_2, conv_w_2, a_log_2, dt_bias_2, dn_norm_g_2, w_dn_out_2, sgu_ln_g_2,
        sgu_ln_b_2, spatial_w_2, spatial_b_2, w_sgu_out_2, w_out_2, ln1_g_2, ln1_b_2,
        router_group_w_2, router_group_b_2, router_expert_w_2, router_expert_b_2,
        expert_w_gate_2, expert_w_up_2, expert_w_down_2, ln2_g_2, ln2_b_2,
    )


_drawn_inputs = setup_inputs


def setup_inputs(seed=0):
    import zlib

    import numpy as np

    out = dict(_drawn_inputs(seed))
    spreads = {}
    factors = {'a_cmp_pos': 8.0,
     'a_cmp_b1': 21.903,
     'c_gate_b': 5.487,
     'dn_norm_g_2': 2.846,
     'sgu_ln_g_2': 6.026,
     'sgu_ln_b_2': 37.303,
     'spatial_b_2': 2.9,
     'router_group_b_2': 6.204,
     'router_expert_b_2': 32.968,
     'ln2_b_2': 2.858}
    for name, (base, spread) in spreads.items():
        noise = np.random.default_rng([zlib.crc32(name.encode()), seed]).standard_normal(out[name].shape)
        drawn = base * np.exp(spread * noise) if base else spread * noise
        out[name] = __import__('jax').numpy.asarray(drawn.astype(out[name].dtype))
    for name, factor in factors.items():
        out[name] = (out[name] * factor).astype(out[name].dtype)
    return out
```

```python
from contextlib import ExitStack

import concourse.bass as bass
from concourse import mybir

ALU = mybir.AluOpType
ACT = mybir.ActivationFunctionType
AX = mybir.AxisListType
F32 = mybir.dt.float32
BF16 = mybir.dt.bfloat16

P = 128
T = 256
TT = T // P
D = 1024
KT = D // P
BANK = 512
SLOT = 4096
RING = 3
CH = 64
NCH = T // CH
ALPHA1 = 4.0 ** 0.25
ALPHA2 = 2.0 ** 0.25
LN_EPS = 1e-5
NORM_EPS = 1e-6
NEG = -1e30
NCMP = (T - 32) // 16 + 1
NFF = 8
NEXP = 16
SMALL = 16 * 32
LEVELS = 6


def build(nc, A, out):
    def bc(ap, shape):
        return ap.broadcast_to(shape)

    with ExitStack() as ctx:
        def sb(name, shape, dt=F32):
            return ctx.enter_context(nc.sbuf_tensor(name, shape, dt))

        sems = {}

        def S(name):
            if name not in sems:
                sems[name] = ctx.enter_context(nc.semaphore(name))
            return sems[name]

        PS = ctx.enter_context(nc.psum_tensor("PS", [P, 8, BANK], F32))
        ring = sb("ring", [P, RING, SLOT])
        xt = sb("xt", [P, TT, D])
        xT = sb("xT", [P, KT, T])
        res = sb("res", [P, TT, D])
        gb = sb("gb", [P, 2, D])
        ident = sb("ident", [P, P])
        identb = sb("identb", [P, P], BF16)
        maskb = sb("maskb", [P, P], BF16)
        ones = sb("ones", [P, P])
        tri = sb("tri", [P, P])
        tril = sb("tril", [P, P])
        blk = sb("blk", [P, P])
        lvl = sb("lvl", [P, LEVELS, P])
        lvl0 = sb("lvl0", [P, P])
        caus = sb("caus", [P, P])
        cmk = sb("cmk", [P, TT, 16])
        cma = sb("cma", [P, TT, 16])
        hmask = sb("hmask", [P, 4])
        rows = sb("rows", [P, P])
        rowc = sb("rowc", [P, P])
        vec = sb("vec", [P, P])
        cw = sb("cw", [P, P])
        w2c = sb("w2c", [CH, 2, 64])
        posc = cw[:, 96:P].rearrange("p (v k) -> p v k", v=2)
        poolw = sb("poolw", [P, 4, P])
        wsm = sb("wsm", [P, KT, 16])
        wsm2 = sb("wsm2", [P, KT, 16])
        wrt = sb("wrt", [P, KT, 20])
        gw2 = sb("gw2", [17, 512])
        brt = sb("brt", [P, 20])
        adt = sb("adt", [P, 2, 8])
        st = sb("st", [P, 96])
        AR = sb("AR", [P, 25700])
        u_w = sb("u_w", [P, 8, P])
        cst = sb("cst", [P, 4])

        def carve(off, *dims, p=P):
            n = 1
            for d in dims:
                n *= d
            v = AR[0:p, off:off + n]
            if len(dims) == 1:
                return v
            names = "abcd"[:len(dims)]
            kw = {names[i]: dims[i] for i in range(len(dims) - 1)}
            return v.rearrange(f"p ({' '.join(names)}) -> p {' '.join(names)}", **kw)

        VEC = {}
        for name, n in (("pool_scale", 4), ("g0", 8), ("b0", 8), ("g1", 8), ("b1", 8), ("g2", 8), ("b2", 8),
                        ("g3", 8), ("b3", 8), ("g4", 8), ("b4", 8), ("g5", 8), ("b5", 8), ("norm_g", 2),
                        ("dn_g", 1), ("sp_b", 8), ("cmp_b1", 2)):
            VEC[name] = sum(VEC[k][1] for k in VEC), n

        def col(name, i=0):
            return vec[:, VEC[name][0] + i:VEC[name][0] + i + 1]

        LN_VECS = [("ln1_g", 0), ("ln2_g", 0), ("ln1_g", 1), ("ln2_g", 1), ("ln1_g_2", 0), ("ln2_g_2", 0)]

        a_q = carve(0, 4, T)
        a_kk = carve(1024, 2, T)
        a_v = carve(1536, TT, 2, P)
        a_g = carve(2048, TT, 24)
        a_k2 = carve(2096, 2, 2, P)
        a_kb = carve(2608, 2, 16, 2, 15)
        a_g1 = carve(3568, 30, p=64)
        a_g1v = carve(3600, 2, 4, 32, p=64)
        a_kc = carve(3856, 15)
        a_vc = carve(3872, 4, 2, 64)
        a_sc = carve(4384, TT, 8, 16)
        a_pc = carve(4640, TT, 8, 32)
        a_pcT = carve(5152, 2, TT, P)
        a_S = carve(5664, 3, BANK)
        a_T = carve(7200, 3, BANK)
        a_o = carve(8736, 8, T)
        a_m = carve(10784, 64)
        a_ci = carve(10848, T)
        a_rc = carve(11104, 4, T)
        a_u = [carve(12128 + i * 1088, 4, 16 + T) for i in range(3)]
        a_r = carve(15392, 4, T)
        f_h = carve(0, 2, 4, T)
        c_q, c_k = carve(0, 4, T), carve(1024, 4, T)
        c_v = carve(2048, TT, D)
        c_r = carve(4096, 8, T)
        c_a = carve(6144, T, p=17)
        c_la, c_t1, c_t2 = carve(6400, TT, 512), carve(7424, TT, 512), carve(8448, TT, 512)
        c_eb, c_en = carve(9472, TT, 4, P), carve(10496, TT, 4, P)
        c_k2T, c_k2 = carve(11520, TT, 4, P), carve(12544, TT, 4, P)
        c_at = carve(13568, TT, 4, P)
        c_S = carve(14592, 3, 4, T)
        c_o, c_sq, c_rs = carve(17664, 8, T), carve(19712, 8, T), carve(21760, 4, T)
        s_q, s_k, s_v = carve(0, 8, T), carve(2048, 8, T), carve(4096, 8, T)
        s_o = s_q
        s_z, s_y = carve(6144, 8, T), carve(8192, 8, T)
        s_raw = carve(10240, 2, 2, 3 + T)
        s_acc = carve(11276, 2, 2, T)
        s_rn = s_raw.rearrange("p a b c -> p (a b c)")
        s_M = carve(12300, 8, P)
        DB = 13324
        s_D, s_DT, s_qd, s_B, s_Ti, s_R, s_Y, s_Kb, s_Kd, s_Vb, s_Bl = (carve(DB + i * 1024, TT, 4, P) for i in range(11))
        s_A, s_QK, s_U, s_WT = s_D, s_DT, s_Y, s_Bl
        s_S = carve(DB + 11 * 1024, 2, 4, P)
        u_u, u_v = carve(DB, TT, D), carve(DB + 2048, TT, D)
        u_gT = carve(DB + 4096, 8, T)
        u_wT = carve(DB + 7168, 8, P)
        s_sg = carve(DB + 8192, 8, T)
        s_vn = u_vn = sb("s_vn", [P, 4, P])
        s_ab = sb("s_ab", [P, TT, 16])
        s_sc = sb("s_sc", [P, 8, TT, 8])
        s_el = sb("s_el", [P, 4, NCH])
        e_cb = carve(0, NEXP, T)
        e_cT = carve(4096, T, p=NEXP)
        e_lg = carve(4352, TT, 20)
        e_sm = carve(4400, 16, TT, 16)
        e_h = carve(4912, 2, 2, T)
        e_sg = carve(5936, 2, 2, T)
        e_uc = carve(6960, 2, 2, T)

        chunks = []

        def cols(name, src, c0, n):
            chunks.append((name, [(slice(0, KT * n), P, src[:, c0:c0 + n].rearrange("(k p) n -> p k n", p=P), (KT, n))]))

        def rowsof(name, src, r0, n):
            chunks.append((name, [(slice(0, n // P * D), P, src[r0:r0 + n, :].rearrange("(k p) n -> p k n", p=P), (n // P, D))]))

        aw = A["a_w_in"][0]
        cols("aq", aw, 0, 512)
        cols("akv", aw, 512, 512)
        cols("awin", aw, 1024, 280)
        chunks.append(("acmp", [(slice(0, 2048), P, A["a_cmp_w1"][0].rearrange("v (k p) n -> p v k n", p=P), (2, 16, 64))]))
        cols("au", aw, 1304, 512)
        wo = A["a_w_out"][0]
        chunks.append(("aout0", [(slice(0, SLOT), (64 * g, 64), wo[256 * g:256 * g + 256, :].rearrange("(k p) n -> p k n", p=64), (4, D))
                                 for g in range(2)]))
        rowsof("aout1", wo, 512, 512)

        def mlp_stream(l):
            w1, w2 = A["mlp_w1"][l], A["mlp_w2"][l]
            for c in range(NFF + 1):
                if c < NFF:
                    cols(f"f{l}w1_{c}", w1, 512 * c, 512)
                if c >= 1:
                    rowsof(f"f{l}w2_{c - 1}", w2, 512 * (c - 1), 512)

        mlp_stream(0)
        cwi = A["c_w_in"][0]
        for i in range(6):
            cols(f"c{i}", cwi, 512 * i, 512)
        rowsof("cout0", A["c_w_out"][0], 0, 512)
        rowsof("cout1", A["c_w_out"][0], 512, 512)
        mlp_stream(1)
        wi = A["w_in_2"][0]
        UV = 3072 + 1024 + 16
        for i in range(4):
            cols(f"suv{i}", wi, UV + 512 * i, 512)
        for i in range(2):
            cols(f"sgs{i}", wi, UV + 3072 + 512 * i, 512)
        for i in range(2):
            cols(f"swg{i}", A["w_sgu_out_2"][0], 512 * i, 512)
        for i in range(6):
            cols(f"sqkv{i}", wi, 512 * i, 512)
        for i in range(2):
            cols(f"sz{i}", wi, 3072 + 512 * i, 512)
        for i in range(2):
            cols(f"sgd{i}", wi, UV + 2048 + 512 * i, 512)
        for i in range(2):
            cols(f"swd{i}", A["w_dn_out_2"][0], 512 * i, 512)
        for i in range(2):
            rowsof(f"sout{i}", A["w_out_2"][0], 512 * i, 512)
        wg, wu, wd = A["expert_w_gate_2"][0], A["expert_w_up_2"][0], A["expert_w_down_2"][0]
        for e in range(NEXP + 1):
            if e < NEXP:
                chunks.append((f"egu{e}", [(slice(2048 * j, 2048 * j + 2048), P, w[e].rearrange("(k p) n -> p k n", p=P), (KT, 256))
                                           for j, w in enumerate((wg, wu))]))
            if e >= 1:
                rowsof(f"ed{e - 1}", wd[e - 1], 0, 256)

        index = {name: n for n, (name, _) in enumerate(chunks)}
        landed, count = {}, [0] * RING
        for n, (name, parts) in enumerate(chunks):
            count[n % RING] += 16 * len(parts)
            landed[name] = n % RING, count[n % RING]
        release = {}

        def slot(name):
            return ring[:, index[name] % RING, :]

        def colview(name, n=512):
            return slot(name)[:, 0:KT * n].rearrange("p (k n) -> p k n", k=KT)

        def rowview(name, k=4):
            return slot(name)[:, 0:k * D].rearrange("p (k n) -> p k n", k=k)

        def arrived(eng, name):
            s, v = landed[name]
            eng.wait_ge(S(f"weights{s}"), v)

        use, used = {}, [0] * 8

        def claim(pe, name, bank):
            n = used[bank]
            used[bank] += 1
            use[name] = bank, n
            if n:
                pe.wait_ge(S(f"evac{bank}"), n)
            return PS[:, bank, :]

        def close(ins, name, chunk=None):
            bank, n = use[name]
            ins.then_inc(S(f"full{bank}"), 1)
            if chunk is not None:
                release[chunk] = f"full{bank}", n + 1

        def full(eng, name):
            bank, n = use[name]
            eng.wait_ge(S(f"full{bank}"), n + 1)
            return PS[:, bank, :]

        def evacuated(ins, name):
            ins.then_inc(S(f"evac{use[name][0]}"), 1)

        def read_out(eng, name):
            bank, n = use[name]
            eng.wait_ge(S(f"evac{bank}"), n + 1)

        turn = [0]

        def nxt(lo=0, hi=8):
            turn[0] += 1
            return lo + turn[0] % (hi - lo)

        block = ctx.enter_context(nc.Block())

        @block.tensor
        def _(pe):
            passed = [0]
            mm = nc.tensor.matmul

            def spent(ins, chunk):
                passed[0] += 1
                ins.then_inc(S("w_spent"), 1)
                release[chunk] = "w_spent", passed[0]

            def by_feature(chunk, n_tiles, act, pre, lo=0, hi=8, view=None, last=True):
                arrived(pe, chunk)
                w = colview(chunk) if view is None else view
                for j in range(0, n_tiles, 2):
                    ps = claim(pe, (pre, j // 2), nxt(lo, hi))
                    for m in range(j, min(j + 2, n_tiles)):
                        for k in range(KT):
                            ins = mm(ps[:, (m - j) * T:(m - j + 1) * T], w[:, k, m * P:(m + 1) * P], act[:, k, :],
                                     start=(k == 0), stop=(k == KT - 1))
                    close(ins, (pre, j // 2), chunk if last and j + 2 >= n_tiles else None)

            def by_token(chunk, pre, lo=0, hi=8, act=None):
                arrived(pe, chunk)
                w = colview(chunk)
                for t in range(TT):
                    ps = claim(pe, (pre, t), nxt(lo, hi))
                    for k in range(KT):
                        ins = mm(ps, xT[:, k, t * P:(t + 1) * P], w[:, k, :], start=(k == 0), stop=(k == KT - 1))
                    close(ins, (pre, t), chunk if t == TT - 1 else None)

            def by_rows(chunk, nk, act, pre, first, last):
                arrived(pe, chunk)
                w = rowview(chunk, nk)
                for t in range(TT):
                    for n in range(2):
                        if first:
                            claim(pe, (pre, t, n), 2 * t + n)
                        ps = PS[:, 2 * t + n, :]
                        for k in range(nk):
                            ins = mm(ps, act(k)[:, t * P:(t + 1) * P], w[:, k, n * BANK:(n + 1) * BANK],
                                     start=first and k == 0, stop=last and k == nk - 1, skip_group_check=True)
                        if last:
                            close(ins, (pre, t, n), chunk if (t, n) == (TT - 1, 1) else None)
                if not last:
                    spent(ins, chunk)

            def transposes(src, pre, lo=0, hi=8):
                for j in range(4):
                    ps = claim(pe, (pre, j), nxt(lo, hi))
                    for k in (2 * j, 2 * j + 1):
                        for t in range(TT):
                            o = (k - 2 * j) * T + t * P
                            ins = nc.tensor.transpose(ps[:, o:o + P], src[:, t, k * P:(k + 1) * P], ident[:])
                    close(ins, (pre, j))

            def norm_transposes(l):
                pe.wait_ge(S("normed"), TT * (l + 1))
                transposes(res, f"nT{l}", 4, 8)

            def xT_ready(l):
                for j in range(4):
                    read_out(pe, (f"nT{l}" if l >= 0 else "xT", j))

            pe.wait_ge(S("consts"), 1)
            pe.wait_ge(S("small"), SMALL)
            ps = claim(pe, "vec", 0)
            nc.tensor.transpose(ps[:, 0:P], rows[:], ident[:])
            ins = nc.tensor.transpose(ps[:, P:2 * P], rowc[:], ident[:])
            close(ins, "vec")
            pe.wait_ge(S("x_in"), 16)
            transposes(xt, "xT")

            xT_ready(-1)
            by_feature("aq", 4, xT, "aq")
            arrived(pe, "akv")
            w = colview("akv")
            ps = claim(pe, "acmp", nxt())
            for m in range(2):
                for k in range(KT):
                    ins = mm(ps[:, m * T:(m + 1) * T], w[:, k, m * P:(m + 1) * P], xT[:, k, :], start=(k == 0), stop=(k == KT - 1))
            close(ins, "acmp")
            ps = claim(pe, "aks", nxt())
            for k in range(KT):
                ins = mm(ps[:, 0:T], w[:, k, 256:384], xT[:, k, :], start=(k == 0), stop=(k == KT - 1))
            close(ins, "aks")
            ps = claim(pe, "avs", nxt())
            for t in range(TT):
                for k in range(KT):
                    ins = mm(ps[:, t * P:(t + 1) * P], xT[:, k, t * P:(t + 1) * P], w[:, k, 384:512], start=(k == 0), stop=(k == KT - 1))
            close(ins, "avs", "akv")
            arrived(pe, "awin")
            w = colview("awin", 280)
            ps = claim(pe, "akw", nxt())
            for k in range(KT):
                ins = mm(ps[:, 0:T], w[:, k, 0:P], xT[:, k, :], start=(k == 0), stop=(k == KT - 1))
            close(ins, "akw")
            ps = claim(pe, "avw", nxt())
            for t in range(TT):
                for k in range(KT):
                    ins = mm(ps[:, t * 256:t * 256 + 152], xT[:, k, t * P:(t + 1) * P], w[:, k, P:280], start=(k == 0), stop=(k == KT - 1))
            close(ins, "avw", "awin")
            arrived(pe, "acmp")
            w = slot("acmp")[:, 0:2048].rearrange("p (v k n) -> p v k n", v=2, k=16)
            pe.wait_ge(S("cmp_blocks"), 1)
            ps = claim(pe, "ac1", nxt())
            for v in range(2):
                for k in range(16):
                    ins = mm(ps[0:64, v * 32:v * 32 + 30], w[:, v, k, :], a_kb[:, v, k].rearrange("p g c -> p (g c)"), start=(k == 0), stop=(k == 15))
            close(ins, "ac1", "acmp")
            by_feature("au", 4, xT, "au")
            read_out(pe, "ac1")
            ps = claim(pe, "ac2", nxt())
            for g in range(2):
                mm(ps[g * 64:g * 64 + 64, 0:15], w2c[:, 0, :], a_g1[:, g * 15:g * 15 + 15], start=True, stop=True, skip_group_check=True)
            for g in range(2):
                ins = mm(ps[:, P + g * 64:P + g * 64 + 64], a_g1v[:, g].rearrange("p i c -> p (i c)"), w2c[:, 1, :], start=True, stop=True, skip_group_check=True)
            close(ins, "ac2")
            for j in range(2):
                read_out(pe, ("aq", j))
            read_out(pe, "ac2")
            for g in range(2):
                ps = claim(pe, ("asc", g), nxt(2, 8))
                for t in range(TT):
                    for i in range(4):
                        o = t * P + i * 32
                        ins = mm(ps[:, o:o + 15], a_q[64 * g:64 * g + 64, i, t * P:(t + 1) * P], a_kc[64 * g:64 * g + 64, :], start=True, stop=True)
                close(ins, ("asc", g))

            units = [(t, g, a, h) for t in range(TT) for g in range(2) for a in range(2) for h in range(1 + t)]

            def scores(u):
                t, g, a, h = u
                nh, nk = (4, P) if t == 0 else (2, T)
                read_out(pe, "aks" if a == 0 else "akw")
                ps = claim(pe, ("s", u), nxt(2, 8))
                for i in range(nh):
                    head = (h * nh + i)
                    mm(ps[:, i * nk:(i + 1) * nk], a_q[64 * g:64 * g + 64, head, t * P:(t + 1) * P], a_kk[64 * g:64 * g + 64, a, 0:nk],
                       start=True, stop=False, skip_group_check=True)
                    ins = mm(ps[:, i * nk + t * P:(i + 1) * nk], identb[:], maskb[:], start=False, stop=True, skip_group_check=True)
                close(ins, ("s", u))

            def prob_transposes(u, n):
                t, g, a, h = u
                nh, nk = (4, P) if t == 0 else (2, T)
                pe.wait_ge(S("probs"), n + 1)
                ps = claim(pe, ("t", u), nxt(2, 8))
                for i in range(nh):
                    for kb in range(1 + t):
                        o = (kb * nh + i) * P
                        ins = nc.tensor.transpose(ps[:, o:o + P], a_S[:, n % 3, i * nk + kb * P:i * nk + kb * P + P], ident[:])
                close(ins, ("t", u))

            def values(u, n):
                t, g, a, h = u
                nh = 4 if t == 0 else 2
                read_out(pe, ("t", u))
                for kb in range(1 + t):
                    o = h * nh * P
                    ins = mm(PS[64 * g:64 * g + 64, t, o:o + nh * P], a_v[:, kb, a, 64 * g:64 * g + 64],
                             a_T[:, n % 3, kb * nh * P:(kb + 1) * nh * P], start=False, stop=(kb == t), skip_group_check=True)
                if g == 1 and a == 1 and h == t:
                    close(ins, ("o", t))

            for n, u in enumerate(units[:2]):
                scores(u)
            pe.wait_ge(S("cprobs"), 1)
            ps = claim(pe, "apct", nxt(2, 8))
            for g in range(2):
                for t in range(TT):
                    ins = nc.tensor.transpose(ps[:, (g * TT + t) * P:(g * TT + t + 1) * P], a_pc[:, t, 4 * g:4 * g + 4].rearrange("p h c -> p (h c)"), ident[:])
            close(ins, "apct")
            read_out(pe, "avs")
            read_out(pe, "avw")
            read_out(pe, "apct")
            for t in range(TT):
                claim(pe, ("o", t), t)
                for g in range(2):
                    for i in range(4):
                        mm(PS[64 * g:64 * g + 64, t, i * P:(i + 1) * P], a_vc[:, i, g, :], a_pcT[:, g, t, :],
                           start=(i == 0), stop=False, skip_group_check=True)
            for n, u in enumerate(units):
                if n + 2 < len(units):
                    scores(units[n + 2])
                prob_transposes(u, n)
                if n:
                    values(units[n - 1], n - 1)
            values(units[-1], len(units) - 1)
            pe.wait_ge(S("pooled"), 1)
            for j in range(2):
                ps = claim(pe, ("ap", j), nxt(4, 8))
                for g in (2 * j, 2 * j + 1):
                    ins = mm(ps[:, (g - 2 * j) * T:(g - 2 * j + 1) * T], poolw[:, g, :], a_r[:, g, :], start=True, stop=True)
                close(ins, ("ap", j))
            for t in range(TT):
                read_out(pe, ("o", t))
            by_rows("aout0", 4, lambda k: a_o[:, k], "m0", True, False)
            for j in range(2):
                read_out(pe, ("ap", j))
            by_rows("aout1", 4, lambda k: a_o[:, 4 + k], "m0", False, True)

            def feed_forward(l, ln):
                norm_transposes(ln)
                xT_ready(ln)
                for c in range(NFF + 1):
                    if c < NFF:
                        by_feature(f"f{l}w1_{c}", 4, xT, f"h{l}_{c}", 4, 8)
                    if c:
                        pe.wait_ge(S("hidden"), 2 * (l * NFF + c))
                        by_rows(f"f{l}w2_{c - 1}", 4, lambda k: f_h[:, (c - 1) % 2, k], f"m{ln + 1}", c == 1, c == NFF)

            feed_forward(0, 0)

            norm_transposes(1)
            xT_ready(1)
            ps = claim(pe, "ga", nxt())
            for k in range(KT):
                ins = mm(ps[0:16, 0:T], wsm[:, k, :], xT[:, k, :], start=(k == 0), stop=(k == KT - 1))
            close(ins, "ga")
            by_feature("c0", 4, xT, "gq")
            read_out(pe, "ga")
            for t in range(TT):
                ps = claim(pe, ("gz", t), nxt())
                ins = mm(ps, c_a[:, t * P:(t + 1) * P], gw2[:], start=True, stop=True)
                close(ins, ("gz", t))
            by_feature("c1", 4, xT, "gk")
            for t in range(TT):
                read_out(pe, ("gz", t))
                ps = claim(pe, ("gb", t), nxt())
                for h in range(4):
                    ins = mm(ps[:, h * P:(h + 1) * P], c_la[:, t, h * P:(h + 1) * P], tri[:], start=True, stop=True)
                close(ins, ("gb", t))
            for i in range(2):
                by_token(f"c{2 + i}", f"gv{i}")
            for i in range(2):
                by_feature(f"c{4 + i}", 4, xT, f"gr{i}")
            pe.wait_ge(S("gla_scaled"), 1)
            for t in range(TT):
                ps = claim(pe, ("gatt", t), nxt())
                for h in range(4):
                    ins = mm(ps[:, h * P:(h + 1) * P], c_k[:, h, t * P:(t + 1) * P], c_q[:, h, t * P:(t + 1) * P], start=True, stop=True)
                close(ins, ("gatt", t))
            pe.wait_ge(S("gla_scaled"), 2)
            for t in range(TT):
                ps = claim(pe, ("gk2", t), nxt())
                for h in range(4):
                    ins = nc.tensor.transpose(ps[:, h * P:(h + 1) * P], c_k2T[:, t, h, :], ident[:])
                close(ins, ("gk2", t))
            for t in range(TT):
                read_out(pe, ("gk2", t))
                for i in range(2):
                    read_out(pe, (f"gv{i}", t))
            for n in range(NCH - 1):
                t, r = n // 2, 64 * (n % 2)
                for j in range(2):
                    ps = claim(pe, ("gu", n, j), nxt())
                    for h in (2 * j, 2 * j + 1):
                        ins = mm(ps[:, (h - 2 * j) * T:(h - 2 * j + 1) * T], c_k2[r:r + 64, t, h, :], c_v[r:r + 64, t, h * T:(h + 1) * T],
                                 start=True, stop=True)
                    close(ins, ("gu", n, j))
            for t in range(TT):
                read_out(pe, ("gatt", t))
            read_out(pe, ("gu", NCH - 2, 1))
            for h in range(4):
                ps = claim(pe, ("go", h), nxt())
                for e in range(2):
                    for t in range(TT):
                        mm(ps[:, e * T + t * P:e * T + (t + 1) * P], c_v[:, t, h * T + e * P:h * T + (e + 1) * P], c_at[:, t, h, :],
                           start=(t == 0), stop=False, skip_group_check=True)
                    for n in range(1, NCH):
                        ins = mm(ps[:, e * T + n * CH:e * T + (n + 1) * CH], c_S[:, n - 1, h, e * P:(e + 1) * P],
                                 c_q[:, h, n * CH:(n + 1) * CH], start=False, stop=(n == NCH - 1), skip_group_check=True)
                close(ins, ("go", h))
            for j in range(2):
                read_out(pe, ("go", 2 * j + 1))
                ps = claim(pe, ("gn", j), nxt())
                for h in (2 * j, 2 * j + 1):
                    for e in range(2):
                        ins = mm(ps[:, (h - 2 * j) * T:(h - 2 * j + 1) * T], ones[:], c_sq[:, 2 * h + e, :], start=(e == 0), stop=(e == 1))
                close(ins, ("gn", j))
            pe.wait_ge(S("gla_out"), 1)
            by_rows("cout0", 4, lambda k: c_o[:, k], "m2", True, False)
            by_rows("cout1", 4, lambda k: c_o[:, 4 + k], "m2", False, True)
            feed_forward(1, 2)

            norm_transposes(3)
            xT_ready(3)
            pe.wait_ge(S("sp_w_masked"), 1)
            for j in range(2):
                ps = claim(pe, ("uw", j), nxt(4, 8))
                for g in range(4):
                    ins = nc.tensor.transpose(ps[:, g * P:(g + 1) * P], u_w[:, 4 * j + g, :], ident[:])
                close(ins, ("uw", j))
            for i in range(4):
                by_token(f"suv{i}", f"uv{i}")
            for i in range(2):
                by_feature(f"sgs{i}", 4, xT, f"gs{i}")
            for j in range(2):
                read_out(pe, ("uw", j))
            pe.wait_ge(S("sgu_v"), TT)
            for t in range(TT):
                for j in range(2):
                    ps = claim(pe, ("sp", t, j), nxt())
                    for g in range(4):
                        ins = mm(ps[:, g * P:(g + 1) * P], u_wT[:, 4 * j + g, :], u_v[:, t, (4 * j + g) * P:(4 * j + g + 1) * P], start=True, stop=True)
                    close(ins, ("sp", t, j))
            for t in range(TT):
                for j in range(2):
                    read_out(pe, ("sp", t, j))
            transposes(u_u, "gT")
            for j in range(4):
                read_out(pe, ("gT", j))
            for i in range(2):
                by_feature(f"swg{i}", 4, u_gT, f"yg{i}")

            ps = claim(pe, "ab", nxt())
            for t in range(TT):
                for k in range(KT):
                    ins = mm(ps[:, t * 16:t * 16 + 16], xT[:, k, t * P:(t + 1) * P], wsm2[:, k, :], start=(k == 0), stop=(k == KT - 1))
            close(ins, "ab")
            for i in range(6):
                by_feature(f"sqkv{i}", 4, xT, f"qkv{i}")
            for i in range(2):
                by_feature(f"sz{i}", 4, xT, f"z{i}")
            for j in range(8):
                pe.wait_ge(S("qk_squares"), j + 1)
                ps = claim(pe, ("qn", j), nxt())
                sq = s_acc[:, j % 2]
                ins = mm(ps, ones[:], sq.rearrange("p a b -> p (a b)"), start=True, stop=True)
                close(ins, ("qn", j))
            pe.wait_ge(S("dn_gates"), 1)
            ps = claim(pe, "gc", nxt())
            for t in range(TT):
                mm(ps[:, t * 8:t * 8 + 8], tri[:], s_sc[:, 1, t, :], start=True, stop=True)
            for t in range(TT):
                ins = mm(ps[:, 16 + t * 8:24 + t * 8], blk[:], s_sc[:, 1, t, :], start=True, stop=True)
            close(ins, "gc")
            for hb in range(2):
                for t in range(TT):
                    pe.wait_ge(S("gate_rows"), hb * TT + t + 1)
                    ps = claim(pe, ("GB", hb, t), nxt())
                    ins = mm(ps, ones[:], s_M[:, 4 * t:4 * t + 4].rearrange("p h t -> p (h t)"), start=True, stop=True)
                    close(ins, ("GB", hb, t))
                pe.wait_ge(S("qk_normed"), 8)
                pe.wait_ge(S("qkv_done"), 12)
                for t in range(TT):
                    for what, rhs in (("kk", s_k), ("kq", s_q)):
                        ps = claim(pe, (what, hb, t), nxt())
                        for h in range(4):
                            ins = mm(ps[:, h * P:(h + 1) * P], s_k[:, 4 * hb + h, t * P:(t + 1) * P], rhs[:, 4 * hb + h, t * P:(t + 1) * P],
                                     start=True, stop=True)
                        close(ins, (what, hb, t))
                    for what, src in (("kt", s_k), ("vt", s_v)):
                        ps = claim(pe, (what, hb, t), nxt())
                        for h in range(4):
                            ins = nc.tensor.transpose(ps[:, h * P:(h + 1) * P], src[:, 4 * hb + h, t * P:(t + 1) * P], ident[:])
                        close(ins, (what, hb, t))
                for t in range(TT):
                    read_out(pe, ("kk", hb, t))
                    ps = claim(pe, ("at", hb, t), nxt())
                    for h in range(4):
                        ins = nc.tensor.transpose(ps[:, h * P:(h + 1) * P], s_A[:, t, h, :], ident[:])
                    close(ins, ("at", hb, t))
                for l in range(1, LEVELS):
                    for t in range(TT):
                        pe.wait_ge(S("level_mask"), (hb * (LEVELS - 1) + l - 1) * TT + t + 1)
                        if l == 1:
                            pe.wait_ge(S("inv_start"), hb * TT + t + 1)
                        else:
                            read_out(pe, ("Rl", hb, l - 1, t))
                        ps = claim(pe, ("Yl", hb, l, t), nxt())
                        for h in range(4):
                            ins = mm(ps[:, h * P:(h + 1) * P], s_Bl[:, t, h, :], s_Ti[:, t, h, :], start=True, stop=True)
                        close(ins, ("Yl", hb, l, t))
                    for t in range(TT):
                        read_out(pe, ("Yl", hb, l, t))
                        if l < LEVELS - 1:
                            ps = claim(pe, ("Tl", hb, l, t), nxt())
                            for h in range(4):
                                ins = mm(ps[:, h * P:(h + 1) * P], s_R[:, t, h, :], s_Y[:, t, h, :], start=True, stop=True)
                            close(ins, ("Tl", hb, l, t))
                        ps = claim(pe, ("Rl", hb, l, t), nxt())
                        for h in range(4):
                            ins = mm(ps[:, h * P:(h + 1) * P], s_Y[:, t, h, :], s_R[:, t, h, :], start=True, stop=True)
                        close(ins, ("Rl", hb, l, t))
                for t in range(TT):
                    read_out(pe, ("kt", hb, t))
                    read_out(pe, ("vt", hb, t))
                    read_out(pe, ("Rl", hb, LEVELS - 1, t))
                    ps = claim(pe, ("U", hb, t), nxt())
                    for h in range(4):
                        ins = mm(ps[:, h * P:(h + 1) * P], s_R[:, t, h, :], s_Vb[:, t, h, :], start=True, stop=True)
                    close(ins, ("U", hb, t))
                    ps = claim(pe, ("W", hb, t), nxt())
                    for h in range(4):
                        ins = mm(ps[:, h * P:(h + 1) * P], s_Kb[:, t, h, :], s_R[:, t, h, :], start=True, stop=True)
                    close(ins, ("W", hb, t))
                for t in range(TT):
                    read_out(pe, ("kq", hb, t))
                    read_out(pe, ("U", hb, t))
                    read_out(pe, ("W", hb, t))
                pe.wait_ge(S("q_decayed"), hb + 1)
                for n in range(NCH):
                    t, r = n // 2, CH * (n % 2)
                    cc = slice(r, r + CH)
                    if n:
                        read_out(pe, ("su", hb, n - 1))
                        ps = claim(pe, ("vn", hb, n), nxt())
                        for h in range(4):
                            ins = mm(ps[cc, h * P:(h + 1) * P], s_WT[:, t, h, cc], s_S[:, n % 2, h, :], start=True, stop=True)
                        close(ins, ("vn", hb, n))
                        read_out(pe, ("vn", hb, n))
                    else:
                        pe.wait_ge(S("v_first"), hb + 1)
                    if n < NCH - 1:
                        ps = claim(pe, ("su", hb, n), nxt())
                        for h in range(4):
                            ins = mm(ps[:, h * P:(h + 1) * P], s_Kd[cc, t, h, :], s_vn[cc, h, :], start=True, stop=True)
                        close(ins, ("su", hb, n))
                    ps = claim(pe, ("ot", hb, n), nxt())
                    for h in range(4):
                        if n:
                            mm(ps[:, h * CH:(h + 1) * CH], s_S[:, n % 2, h, :], s_qd[:, t, h, cc], start=True, stop=False)
                        ins = mm(ps[:, h * CH:(h + 1) * CH], s_vn[cc, h, :], s_QK[cc, t, h, cc], start=(n == 0), stop=True)
                    close(ins, ("ot", hb, n))
            for i in range(2):
                by_feature(f"sgd{i}", 4, xT, f"gd{i}")
            for j in range(4):
                pe.wait_ge(S("dn_squares"), j + 1)
                ps = claim(pe, ("dn", j), nxt())
                ins = mm(ps, ones[:], s_acc[:, j % 2].rearrange("p a b -> p (a b)"), start=True, stop=True)
                close(ins, ("dn", j))
            pe.wait_ge(S("dn_out"), 4)
            for i in range(2):
                by_feature(f"swd{i}", 4, s_o, f"yd{i}")
            for i in range(2):
                for j in range(2):
                    pe.wait_ge(S("y_mixed"), 2 * i + j + 1)
                by_rows(f"sout{i}", 4, lambda k: s_y[:, 4 * i + k], "m4", i == 0, i == 1)

            norm_transposes(4)
            xT_ready(4)
            ps = claim(pe, "rl", nxt(4, 8))
            for t in range(TT):
                for k in range(KT):
                    ins = mm(ps[:, t * 32:t * 32 + 20], xT[:, k, t * P:(t + 1) * P], wrt[:, k, :], start=(k == 0), stop=(k == KT - 1))
            close(ins, "rl")
            pe.wait_ge(S("combined"), 1)
            ps = claim(pe, "ct", nxt(4, 8))
            for t in range(TT):
                ins = nc.tensor.transpose(ps[0:NEXP, t * P:(t + 1) * P], e_sm[:, 15, t, :], ident[:])
            close(ins, "ct")
            read_out(pe, "ct")
            for j in range(NEXP // 2):
                ps = claim(pe, ("cb", j), nxt(4, 8))
                for e in (2 * j, 2 * j + 1):
                    ins = mm(ps[:, (e - 2 * j) * T:(e - 2 * j + 1) * T], ident[0:NEXP, e:e + 1].broadcast_to([NEXP, P]), e_cT[:], start=True, stop=True)
                close(ins, ("cb", j))
            for e in range(NEXP + 1):
                if e < NEXP:
                    arrived(pe, f"egu{e}")
                    for j, what in enumerate("gu"):
                        w = slot(f"egu{e}")[:, 2048 * j:2048 * j + 2048].rearrange("p (k n) -> p k n", k=KT)
                        by_feature(f"egu{e}", 2, xT, f"e{what}{e}", 4, 8, view=w, last=(j == 1))
                if e:
                    pe.wait_ge(S("expert_h"), e)
                    by_rows(f"ed{e - 1}", 2, lambda k: e_h[:, (e - 1) % 2, k], "m5", e == 1, e == NEXP)

        @block.vector
        def _(ve):
            v = nc.vector
            steps = [0]

            def after(ins):
                steps[0] += 1
                ins.then_inc(S("vec_step"), 1)
                ve.wait_ge(S("vec_step"), steps[0])

            def layer_norm(l, alpha):
                for t in range(TT):
                    if l:
                        ve.wait_ge(S("xt_ready"), TT * (l - 1) + t + 1)
                    for n in range(2):
                        ps = full(ve, (f"m{l}", t, n))
                        r = res[:, t, n * BANK:(n + 1) * BANK]
                        evacuated(v.scalar_tensor_tensor(r, xt[:, t, n * BANK:(n + 1) * BANK], alpha, ps, ALU.mult, ALU.add), (f"m{l}", t, n))
                        read_out(ve, (f"m{l}", t, n))
                        ins = v.bn_stats(st[:, 16 * t + 6 * n:16 * t + 6 * n + 6], r)
                    after(ins)
                    v.bn_aggr(st[:, 16 * t + 12:16 * t + 14], st[:, 16 * t:16 * t + 12]).then_inc(S("variance"), 1)
                for t in range(TT):
                    ve.wait_ge(S("rstd"), n_norm[0] * TT + t + 1)
                    ve.wait_ge(S("variance"), n_norm[0] * TT + t + 1)
                    v.tensor_scalar(res[:, t, :], res[:, t, :], st[:, 16 * t + 12:16 * t + 13], st[:, 16 * t + 14:16 * t + 15],
                                    ALU.subtract, ALU.mult).then_inc(S("normed"), 1)
                n_norm[0] += 1

            n_norm = [0]

            def features(l):
                for j in (1, 3):
                    ps = full(ve, (f"nT{l}", j))
                    for k in (2 * j, 2 * j + 1):
                        ins = v.tensor_scalar(xT[:, k, :], ps[:, (k - 2 * j) * T:(k - 2 * j + 1) * T], col(f"g{l}", k), col(f"b{l}", k),
                                              ALU.mult, ALU.add)
                    evacuated(ins, (f"nT{l}", j))

            v.memset(rows[:], 0.0).then_inc(S("rows_zero"), 1)
            v.memset(ones[:], 1.0)
            v.memset(cst[:, 0:1], LN_EPS)
            v.memset(cst[:, 1:2], NORM_EPS)
            v.memset(a_g1v, 0.0)
            v.memset(a_pc, 0.0)
            v.memset(a_u[0][:, :, 0:16], 0.0).then_inc(S("vec_consts"), 1)
            ve.wait_ge(S("win_counts"), 1)
            v.reciprocal(a_rc, a_rc).then_inc(S("win_recip"), 1)
            ps = full(ve, "vec")
            v.tensor_copy(vec[:], ps[:, 0:P])
            evacuated(v.tensor_copy(cw[:], ps[:, P:2 * P]), "vec")
            for j in (1, 3):
                ps = full(ve, ("xT", j))
                evacuated(v.tensor_copy(xT[:, 2 * j:2 * j + 2].rearrange("p a b -> p (a b)"), ps), ("xT", j))
            ps = full(ve, "acmp").rearrange("p (v n e) -> p v n e", v=2, e=2)
            for par in range(2):
                for g in range(2):
                    ins = v.tensor_copy(a_k2[64 * par:64 * par + 64, :, g, :], ps[64 * g:64 * g + 64, :, :, par])
            evacuated(ins, "acmp")
            read_out(ve, "acmp")
            read_out(ve, "vec")
            for kv in range(2):
                for h in range(2):
                    ins = v.tensor_tensor(a_kb[:, kv, 8 * h:8 * h + 8], a_k2[:, kv, :, 8 * h:8 * h + 120].rearrange("q g (c p) -> q p g c", p=8),
                                          posc[:, kv, 8 * h:8 * h + 8].unsqueeze(2).unsqueeze(3).broadcast_to([P, 8, 2, NCMP]), ALU.add)
            ins.then_inc(S("cmp_blocks"), 1)
            ps = full(ve, "ac2")
            v.tensor_copy(a_kc, ps[:, 0:NCMP])
            ve.wait_ge(S("consts"), 1)
            evacuated(v.tensor_tensor(a_vc.rearrange("p i g d -> p i (g d)"), ps[:, P:2 * P].unsqueeze(1).broadcast_to([P, 4, P]),
                                      hmask[:].unsqueeze(2).broadcast_to([P, 4, P]), ALU.mult), "ac2")
            sc = a_sc[:, :, :, 0:NCMP]
            cmx, csum = a_m[:, 0:16].rearrange("p (t h) -> p t h", t=TT), a_m[:, 16:32].rearrange("p (t h) -> p t h", t=TT)

            def over_c(ap):
                return ap.unsqueeze(3).broadcast_to([P, TT, 8, NCMP])

            for g in range(2):
                ps = full(ve, ("asc", g))[:, 0:256].rearrange("p (t h c) -> p t h c", t=TT, h=4)[:, :, :, 0:NCMP]
                evacuated(v.tensor_tensor(sc[:, :, 4 * g:4 * g + 4], ps, cma[:, :, 0:NCMP].unsqueeze(2).broadcast_to([P, TT, 4, NCMP]), ALU.add),
                          ("asc", g))
                read_out(ve, ("asc", g))
            after(v.tensor_reduce(cmx, sc, AX.X, ALU.max))
            v.tensor_tensor(sc, sc, over_c(cmx), ALU.subtract).then_inc(S("c_shifted"), 1)
            ve.wait_ge(S("c_exp"), 1)
            after(v.tensor_tensor(sc, sc, cmk[:, :, 0:NCMP].unsqueeze(2).broadcast_to([P, TT, 8, NCMP]), ALU.mult))
            after(v.tensor_reduce(csum, sc, AX.X, ALU.add))
            after(v.tensor_scalar(csum, csum, 1e-30, None, ALU.max))
            after(v.reciprocal(csum, csum))
            read_out(ve, "avw")
            gates = a_g.rearrange("p t (h b) -> p t h b", b=3)
            after(v.tensor_tensor(csum, csum, gates[:, :, :, 0], ALU.mult))
            v.tensor_tensor(a_pc[:, :, :, 0:NCMP], sc, over_c(csum), ALU.mult).then_inc(S("cprobs"), 1)

            units = [(t, g, a, h) for t in range(TT) for g in range(2) for a in range(2) for h in range(1 + t)]

            def maxima(n):
                t, g, a, h = units[n]
                nh = 4 if t == 0 else 2
                m = a_m[:, 32 + 8 * (n % 4):32 + 8 * (n % 4) + nh]
                ps = full(ve, ("s", units[n])).rearrange("p (h k) -> p h k", h=nh)
                if n >= 4:
                    read_out(ve, ("s", units[n - 4]))
                v.tensor_reduce(m, ps, AX.X, ALU.max, negate=True).then_inc(S("maxima"), 1)

            def weigh(n):
                t, g, a, h = units[n]
                nh, nk = (4, P) if t == 0 else (2, T)
                w = a_m[:, 32 + 8 * (n % 4) + 4:32 + 8 * (n % 4) + 4 + nh]
                h0 = 4 * g + h * nh
                read_out(ve, ("s", units[n]))
                after(v.reciprocal(w, w))
                after(v.tensor_tensor(w, w, gates[:, t, h0:h0 + nh, 1 + a], ALU.mult))
                s = a_S[:, n % 3, :].rearrange("p (h k) -> p h k", h=nh)
                v.tensor_tensor(s, s, w.unsqueeze(2).broadcast_to([P, nh, nk]), ALU.mult).then_inc(S("probs"), 1)

            for n in range(len(units) + 1):
                if n < len(units):
                    maxima(n)
                if n:
                    weigh(n - 1)
            layer_norm(0, ALPHA1)

            def feed_forward(l, ln):
                features(ln)
                for c in range(NFF):
                    for j in range(2):
                        read_out(ve, (f"h{l}_{c}", j))
                        h = f_h[:, c % 2, 2 * j:2 * j + 2]
                        v.tensor_tensor(h, h, h, ALU.mult).then_inc(S("hidden"), 1)
                layer_norm(ln + 1, ALPHA1)

            feed_forward(0, 0)

            features(1)
            after(v.memset(c_a, 1.0))
            ps = full(ve, "ga")
            evacuated(v.tensor_copy(c_a[0:16, :], ps[0:16, 0:T]), "ga")
            for t in range(TT):
                ps = full(ve, ("gz", t))
                ve.wait_ge(S("softplus"), t + 1)
                evacuated(v.scalar_tensor_tensor(c_la[:, t, :], ps, 0.0, c_t1[:, t, :], ALU.min, ALU.subtract), ("gz", t))
            for j in range(2):
                read_out(ve, ("gq", j))
                read_out(ve, ("gk", j))
            for t in range(TT):
                read_out(ve, ("gb", t))
                ts = slice(t * P, (t + 1) * P)
                v.tensor_tensor(c_k[:, :, ts], c_k[:, :, ts], c_en[:, t], ALU.mult)
                ins = v.tensor_tensor(c_q[:, :, ts], c_q[:, :, ts], c_eb[:, t], ALU.mult)
            ins.then_inc(S("gla_scaled"), 1)
            ve.wait_ge(S("gla_scaled"), 1)
            for t in range(TT):
                last = c_eb[:, t].rearrange("p h (c x) -> p h c x", x=CH)[:, :, :, CH - 1:CH].broadcast_to([P, 4, 2, CH])
                ins = v.tensor_tensor(c_k2T[:, t].rearrange("p h (c x) -> p h c x", x=CH),
                                      c_k[:, :, t * P:(t + 1) * P].rearrange("p h (c x) -> p h c x", x=CH), last, ALU.mult)
            ins.then_inc(S("gla_scaled"), 1)
            for t in range(TT):
                ps = full(ve, ("gatt", t)).rearrange("p (h c) -> p h c", h=4)
                evacuated(v.tensor_tensor(c_at[:, t], ps, tri[:].unsqueeze(1).broadcast_to([P, 4, P]), ALU.mult), ("gatt", t))
            for n in range(NCH - 1):
                for j in range(2):
                    ps = full(ve, ("gu", n, j))
                    if n == 0:
                        ins = v.tensor_copy(c_S[:, 0, 2 * j:2 * j + 2].rearrange("p a b -> p (a b)"), ps)
                    else:
                        read_out(ve, ("gu", n - 1, j))
                        for h in (2 * j, 2 * j + 1):
                            last = (n % 2) * CH + CH - 1
                            ins = v.scalar_tensor_tensor(c_S[:, n, h], c_S[:, n - 1, h], c_eb[:, n // 2, h, last:last + 1],
                                                         ps[:, (h - 2 * j) * T:(h - 2 * j + 1) * T], ALU.mult, ALU.add)
                    evacuated(ins, ("gu", n, j))
            for h in range(4):
                if h % 2 == 0:
                    ve.wait_ge(S("gla_rstd"), h // 2 + 1)
                for e in range(2):
                    ins = v.scalar_tensor_tensor(c_o[:, 2 * h + e], c_o[:, 2 * h + e], col("norm_g", e), c_rs[:, h], ALU.mult, ALU.mult)
            for i in range(2):
                for j in range(2):
                    read_out(ve, (f"gr{i}", j))
            after(ins)
            v.tensor_tensor(c_o, c_o, c_r, ALU.mult).then_inc(S("gla_out"), 1)
            layer_norm(2, ALPHA1)
            feed_forward(1, 2)

            features(3)
            for t in range(TT):
                for i in range(2):
                    read_out(ve, (f"uv{2 + i}", t))
                    ins = v.bn_stats(st[:, 16 * t + 6 * i:16 * t + 6 * i + 6], u_v[:, t, i * BANK:(i + 1) * BANK])
                after(ins)
                v.bn_aggr(st[:, 16 * t + 12:16 * t + 14], st[:, 16 * t:16 * t + 12]).then_inc(S("variance"), 1)
            for t in range(TT):
                ve.wait_ge(S("rstd"), n_norm[0] * TT + t + 1)
                ve.wait_ge(S("variance"), n_norm[0] * TT + t + 1)
                v.tensor_scalar(u_v[:, t, :], u_v[:, t, :], st[:, 16 * t + 12:16 * t + 13], st[:, 16 * t + 14:16 * t + 15],
                                ALU.subtract, ALU.mult).then_inc(S("sgu_normed"), 1)
            n_norm[0] += 1
            for t in range(TT):
                for j in range(2):
                    read_out(ve, (f"uv{j}", t))
                    ps = full(ve, ("sp", t, j))
                    for g in range(4):
                        u = u_u[:, t, (4 * j + g) * P:(4 * j + g + 1) * P]
                        ins = v.scalar_tensor_tensor(u, ps[:, g * P:(g + 1) * P], col("sp_b", 4 * j + g), u, ALU.add, ALU.mult)
                    evacuated(ins, ("sp", t, j))
            for i in range(2):
                for j in range(2):
                    ps = full(ve, (f"yg{i}", j))
                    read_out(ve, (f"gs{i}", j))
                    k = slice(4 * i + 2 * j, 4 * i + 2 * j + 2)
                    evacuated(v.tensor_tensor(s_y[:, k].rearrange("p a b -> p (a b)"), ps, s_sg[:, k].rearrange("p a b -> p (a b)"), ALU.mult),
                              (f"yg{i}", j))

            beta, g_, gcum, glast, f_kd, e_g, f_kb, y_ = (s_sc[:, i] for i in range(8))
            ps = full(ve, "ab")
            evacuated(v.tensor_copy(s_ab[:], ps[:, 0:32].rearrange("p (t c) -> p t c", t=TT)), "ab")
            read_out(ve, "ab")
            v.tensor_tensor(y_, s_ab[:, :, 0:8], adt[:, 1:2].broadcast_to([P, TT, 8]), ALU.add).then_inc(S("ab_ready"), 1)
            v.memset(s_raw[:, :, :, 0:3], 0.0).then_inc(S("raw_pad"), 1)
            ve.wait_ge(S("ab_act"), 1)
            ve.wait_ge(S("ab_ready"), 1)
            v.tensor_scalar(beta, beta, 1.0, None, ALU.add)
            after(v.scalar_tensor_tensor(y_, y_, 0.0, f_kb, ALU.max, ALU.add))
            v.reciprocal(beta, beta)
            v.scalar_tensor_tensor(g_, y_, -1.0, adt[:, 0:1].broadcast_to([P, TT, 8]), ALU.mult, ALU.mult).then_inc(S("dn_gates"), 1)
            for i in range(6):
                for j in range(2):
                    n = 2 * i + j
                    read_out(ve, (f"qkv{i}", j))
                    ve.wait_ge(S("raw_pad"), 1)
                    if n >= 2:
                        ve.wait_ge(S("qkv_done"), n - 1)
                    for tap in range(3, -1, -1):
                        for m in range(2):
                            o, x = s_acc[:, n % 2, m], s_raw[:, n % 2, m, tap:tap + T]
                            wt = cw[:, tap * 24 + 2 * n + m:tap * 24 + 2 * n + m + 1]
                            if tap == 3:
                                ins = v.tensor_scalar(o, x, wt, None, ALU.mult)
                            else:
                                ins = v.scalar_tensor_tensor(o, x, wt, o, ALU.mult, ALU.add)
                        if tap:
                            after(ins)
                    ins.then_inc(S("convolved"), 1)
            for n in range(8):
                ve.wait_ge(S("qk_rnorm"), n + 1)
                x = (s_q if n < 4 else s_k)[:, 2 * (n % 4):2 * (n % 4) + 2].rearrange("p a b -> p (a b)")
                v.scalar_tensor_tensor(x, x, float(P) ** -0.5 if n < 4 else 1.0, s_rn[:, (n % 2) * BANK:(n % 2) * BANK + BANK],
                                       ALU.mult, ALU.mult).then_inc(S("qk_normed"), 1)
            ps = full(ve, "gc")
            evacuated(v.tensor_copy(s_sc[:, 2:4].rearrange("p a t h -> p (a t h)"), ps[:, 0:32]), "gc")
            read_out(ve, "gc")
            v.tensor_tensor(f_kd, glast, gcum, ALU.subtract).then_inc(S("gate_diff"), 1)
            ve.wait_ge(S("gate_exp"), 1)
            ve.wait_ge(S("qk_normed"), 8)
            v.tensor_tensor(f_kb, e_g, beta, ALU.mult)
            for hb in range(2):
                hs = slice(4 * hb, 4 * hb + 4)

                def per_head(ap, t):
                    return ap[:, t, hs].unsqueeze(2).broadcast_to([P, 4, P])

                for t in range(TT):
                    if hb:
                        full(ve, ("GB", 0, t))
                    v.tensor_tensor(s_M[:, 4 * t:4 * t + 4], tri[:].unsqueeze(1).broadcast_to([P, 4, P]), per_head(g_, t), ALU.mult)\
                        .then_inc(S("gate_rows"), 1)
                for t in range(TT):
                    ps = full(ve, ("GB", hb, t))
                    for h in range(4):
                        o, gc = slice(h * P, (h + 1) * P), gcum[:, t, 4 * hb + h:4 * hb + h + 1]
                        v.tensor_scalar(s_DT[:, t, h], ps[:, o], gc, 0.0, ALU.subtract, ALU.min)
                        ins = v.tensor_scalar(s_D[:, t, h], ps[:, o], gc, 0.0, ALU.subtract, ALU.max)
                    ins.then_inc(S("decay_args"), 1)
                    ve.wait_ge(S("decay_rows"), hb * TT + t + 1)
                    after(v.tensor_copy(s_el[:, :, 2 * t:2 * t + 2], s_qd[:, t].rearrange("p h (c x) -> p h c x", x=CH)[:, :, :, CH - 1]))
                    ins = v.tensor_tensor(s_qd[:, t], s_qd[:, t], s_q[:, hs, t * P:(t + 1) * P], ALU.mult)
                    ins.then_inc(S("q_decayed"), 1)
                for t in range(TT):
                    ps = full(ve, ("kk", hb, t))
                    ve.wait_ge(S("decay_masked"), hb * TT + t + 1)
                    for h in range(4):
                        ins = v.scalar_tensor_tensor(s_A[:, t, h], ps[:, h * P:(h + 1) * P], beta[:, t, 4 * hb + h:4 * hb + h + 1], s_D[:, t, h],
                                                     ALU.mult, ALU.mult)
                    evacuated(ins, ("kk", hb, t))
                    ps = full(ve, ("kq", hb, t))
                    evacuated(v.tensor_tensor(s_QK[:, t].rearrange("p h t -> p (h t)"), ps, s_DT[:, t].rearrange("p h t -> p (h t)"), ALU.mult),
                              ("kq", hb, t))
                    ps = full(ve, ("kt", hb, t)).rearrange("p (h d) -> p h d", h=4)
                    v.tensor_tensor(s_Kb[:, t], ps, per_head(f_kb, t), ALU.mult)
                    evacuated(v.tensor_tensor(s_Kd[:, t], ps, per_head(f_kd, t), ALU.mult), ("kt", hb, t))
                    ps = full(ve, ("vt", hb, t)).rearrange("p (h d) -> p h d", h=4)
                    evacuated(v.tensor_tensor(s_Vb[:, t], ps, per_head(beta, t), ALU.mult), ("vt", hb, t))
                for t in range(TT):
                    read_out(ve, ("at", hb, t))
                    for o, x, m in ((s_Ti, s_A, lvl0[:]), (s_R, s_B, lvl[:, 0])):
                        ins = v.tensor_tensor(o[:, t], x[:, t], m.unsqueeze(1).broadcast_to([P, 4, P]), ALU.mult)
                    after(ins)
                    for o in (s_Ti, s_R):
                        ins = v.scalar_tensor_tensor(o[:, t], o[:, t], -1.0, ident[:].unsqueeze(1).broadcast_to([P, 4, P]), ALU.mult, ALU.add)
                    ins.then_inc(S("inv_start"), 1)
                    ve.wait_ge(S("inv_start"), hb * TT + t + 1)
                for l in range(1, LEVELS):
                    for t in range(TT):
                        for name, o in (("Tl", s_Ti), ("Rl", s_R)):
                            if name == "Tl" and l == LEVELS - 1:
                                continue
                            if l > 1:
                                read_out(ve, (name, hb, l - 1, t))
                            ps = full(ve, (name, hb, l, t))
                            if name == "Tl":
                                full(ve, ("Rl", hb, l, t))
                            x = o[:, t].rearrange("p h t -> p (h t)")
                            evacuated(v.tensor_tensor(x, x, ps, ALU.subtract), (name, hb, l, t))
                for n in range(NCH):
                    t, r = n // 2, CH * (n % 2)
                    cc = slice(r, r + CH)
                    u = s_U[cc, t].rearrange("p h t -> p (h t)")
                    read_out(ve, ("U", hb, t))
                    if n == 0:
                        v.tensor_copy(s_vn[cc].rearrange("p h t -> p (h t)"), u).then_inc(S("v_first"), 1)
                    else:
                        ps = full(ve, ("vn", hb, n))
                        evacuated(v.tensor_tensor(s_vn[cc].rearrange("p h t -> p (h t)"), u, ps[cc, :], ALU.subtract), ("vn", hb, n))
                    if n < NCH - 1:
                        ps = full(ve, ("su", hb, n))
                        if n == 0:
                            ins = v.tensor_copy(s_S[:, 1].rearrange("p h t -> p (h t)"), ps)
                        else:
                            read_out(ve, ("su", hb, n - 1))
                            for h in range(4):
                                ins = v.scalar_tensor_tensor(s_S[:, (n + 1) % 2, h], s_S[:, n % 2, h], s_el[:, h, n:n + 1], ps[:, h * P:(h + 1) * P],
                                                             ALU.mult, ALU.add)
                        evacuated(ins, ("su", hb, n))
            for i in range(2):
                for j in range(2):
                    read_out(ve, (f"z{i}", j))
            for n in range(4):
                ve.wait_ge(S("dn_rstd"), n + 1)
                x = s_o[:, 2 * n:2 * n + 2].rearrange("p a b -> p (a b)")
                after(v.scalar_tensor_tensor(x, x, col("dn_g"), s_rn[:, (n % 2) * BANK:(n % 2) * BANK + BANK], ALU.mult, ALU.mult))
                ins = v.tensor_tensor(x, x, s_z[:, 2 * n:2 * n + 2].rearrange("p a b -> p (a b)"), ALU.mult)
                ins.then_inc(S("dn_out"), 1)
            for i in range(2):
                for j in range(2):
                    k = slice(4 * i + 2 * j, 4 * i + 2 * j + 2)
                    sg, y = s_sg[:, k].rearrange("p a b -> p (a b)"), s_y[:, k].rearrange("p a b -> p (a b)")
                    ps = full(ve, (f"yd{i}", j))
                    read_out(ve, (f"gd{i}", j))
                    evacuated(v.tensor_tensor(sg, ps, sg, ALU.mult), (f"yd{i}", j))
                    read_out(ve, (f"yd{i}", j))
                    v.tensor_tensor(y, y, sg, ALU.add).then_inc(S("y_mixed"), 1)
            layer_norm(4, ALPHA2)

            features(4)
            lg, el = e_lg[:, :, 0:4], e_lg[:, :, 4:20].rearrange("p t (g j) -> p t g j", g=4)
            ps = full(ve, "rl").rearrange("p (t c) -> p t c", c=32)[:, 0:TT, 0:20]
            evacuated(v.tensor_tensor(e_lg, ps, brt[:].unsqueeze(1).broadcast_to([P, TT, 20]), ALU.add), "rl")
            read_out(ve, "rl")

            def sm(i, n=4):
                return e_sm[:, i, :, 0:n]

            def one(i):
                return e_sm[:, i, :, 0:1].broadcast_to([P, TT, 4])

            first4 = e_sm[:, 14, :, 0:4]
            for i in range(4):
                ins = v.memset(e_sm[:, 14, :, i:i + 1], 4.0 - i)
            after(ins)

            def arg_max(x, m, tmp, o):
                after(v.tensor_reduce(sm(m, 1), x, AX.X, ALU.max))
                after(v.tensor_tensor(sm(tmp), x, one(m), ALU.is_equal))
                after(v.tensor_tensor(sm(tmp), sm(tmp), first4, ALU.mult))
                after(v.tensor_reduce(sm(13, 1), sm(tmp), AX.X, ALU.max))
                after(v.tensor_tensor(sm(o), sm(tmp), one(13), ALU.is_equal))

            arg_max(lg, 0, 1, 2)
            v.tensor_tensor(sm(3), lg, one(0), ALU.subtract).then_inc(S("router_arg"), 1)
            grp = e_sm[:, 15].rearrange("p t (g j) -> p t g j", g=4)
            after(v.tensor_tensor(grp, el, sm(2).unsqueeze(3).broadcast_to([P, TT, 4, 4]), ALU.mult))
            after(v.tensor_reduce(sm(5), e_sm[:, 15].rearrange("p t (g j) -> p t j g", g=4), AX.X, ALU.add))
            after(v.tensor_reduce(sm(6, 1), sm(5), AX.X, ALU.max))
            v.tensor_tensor(sm(7), sm(5), one(6), ALU.subtract).then_inc(S("router_arg"), 1)
            ve.wait_ge(S("router_exp"), 2)
            v.tensor_reduce(sm(4, 1), sm(3), AX.X, ALU.add)
            after(v.tensor_reduce(sm(8, 1), sm(7), AX.X, ALU.add))
            v.reciprocal(sm(4, 1), sm(4, 1))
            after(v.reciprocal(sm(8, 1), sm(8, 1)))
            after(v.tensor_tensor(sm(7), sm(7), one(8), ALU.mult))
            arg_max(sm(7), 9, 1, 10)
            after(v.scalar_tensor_tensor(sm(5), sm(10), -2.0, sm(7), ALU.mult, ALU.add))
            arg_max(sm(5), 11, 1, 12)
            v.tensor_tensor(sm(9, 1), sm(9, 1), sm(11, 1), ALU.add)
            after(v.tensor_tensor(sm(10), sm(10), sm(12), ALU.add))
            v.reciprocal(sm(9, 1), sm(9, 1))
            after(v.tensor_tensor(sm(7), sm(7), sm(10), ALU.mult))
            after(v.tensor_tensor(sm(7), sm(7), one(9), ALU.mult))
            after(v.tensor_tensor(sm(7), sm(7), one(4), ALU.mult))
            v.tensor_tensor(grp, sm(2).unsqueeze(3).broadcast_to([P, TT, 4, 4]), sm(7).unsqueeze(2).broadcast_to([P, TT, 4, 4]), ALU.mult)\
                .then_inc(S("combined"), 1)
            ps = full(ve, "ct")
            evacuated(v.tensor_copy(e_cT, ps[0:NEXP, 0:T]), "ct")
            for e in range(NEXP):
                if e % 2 == 0:
                    read_out(ve, ("cb", e // 2))
                ps = full(ve, (f"eu{e}", 0)).rearrange("p (m t) -> p m t", m=2)
                evacuated(v.tensor_tensor(e_uc[:, e % 2], ps, e_cb[:, e:e + 1].broadcast_to([P, 2, T]), ALU.mult), (f"eu{e}", 0))
                read_out(ve, (f"eu{e}", 0))
                read_out(ve, (f"eg{e}", 0))
                v.tensor_tensor(e_h[:, e % 2], e_uc[:, e % 2], e_sg[:, e % 2], ALU.mult).then_inc(S("expert_h"), 1)
            layer_norm(5, ALPHA2)

        @block.scalar
        def _(act):
            a = nc.scalar.activation
            steps = [0]

            def after(ins):
                steps[0] += 1
                ins.then_inc(S("act_step"), 1)
                act.wait_ge(S("act_step"), steps[0])

            def copy(name, out, in_=None, scale=1.0, func=ACT.Copy):
                ps = full(act, name)
                evacuated(a(out, ps if in_ is None else in_(ps), func, scale=scale), name)

            def flat(ap):
                return ap.rearrange("p a b -> p (a b)")

            n_norm = [0]

            def deviations():
                for t in range(TT):
                    act.wait_ge(S("variance"), n_norm[0] * TT + t + 1)
                    r = st[:, 16 * t + 14:16 * t + 15]
                    after(a(r, st[:, 16 * t + 13:16 * t + 14], ACT.Ln, bias=cst[:, 0:1]))
                    a(r, r, ACT.Exp, scale=-0.5).then_inc(S("rstd"), 1)
                n_norm[0] += 1

            def features(l):
                for j in (0, 2):
                    ps = full(act, (f"nT{l}", j))
                    for k in (2 * j, 2 * j + 1):
                        ins = a(xT[:, k, :], ps[:, (k - 2 * j) * T:(k - 2 * j + 1) * T], ACT.Identity, scale=col(f"g{l}", k), bias=col(f"b{l}", k))
                    evacuated(ins, (f"nT{l}", j))

            act.wait_ge(S("rows_zero"), 1)
            n = 0

            def load(dst, src):
                loads[0] += 1
                act.dma_start(dst, src).then_inc(S("small"), 16)

            loads = [0]
            for i, (name, l) in enumerate(LN_VECS):
                for k, v_ in (("g", name), ("b", name.replace("_g", "_b"))):
                    r0 = VEC[f"{k}{i}"][0]
                    load(rows[r0:r0 + 8, :], A[v_][l].rearrange("(a p) -> a p", p=P))
            for name, src in (("pool_scale", A["a_pool_scale"][0]), ("norm_g", A["c_norm_g"][0]), ("dn_g", A["dn_norm_g_2"][0])):
                r0, n = VEC[name]
                load(rows[r0:r0 + n, :], src.rearrange("(a p) -> a p", p=P))
            load(rows[VEC["sp_b"][0]:VEC["sp_b"][0] + 8, :], A["spatial_b_2"][0])
            load(rows[VEC["cmp_b1"][0]:VEC["cmp_b1"][0] + 2, 0:64], A["a_cmp_b1"][0])
            load(rowc[0:96, :], A["conv_w_2"][0].rearrange("j (m p) -> (j m) p", p=P))
            load(rowc[96:P, :], A["a_cmp_pos"][0].rearrange("v (k e) d -> (v k) (e d)", e=2))
            load(w2c[:], A["a_cmp_w2"][0].rearrange("v j d -> j v d"))
            load(poolw[:], A["a_pool_w"][0].rearrange("g c d -> c g d"))
            load(wsm[:], A["c_w_in"][0][:, 3072:3088].rearrange("(k p) n -> p k n", p=P))
            load(wsm2[:], A["w_in_2"][0][:, 4096:4112].rearrange("(k p) n -> p k n", p=P))
            load(wrt[:, :, 0:4], A["router_group_w_2"][0].rearrange("(k p) n -> p k n", p=P))
            load(wrt[:, :, 4:20], A["router_expert_w_2"][0].rearrange("(k p) n -> p k n", p=P))
            load(gw2[0:16, :], A["c_gate_w2"][0])
            load(gw2[16:17, :], A["c_gate_b"])
            load(brt[:, 0:4], A["router_group_b_2"].broadcast_to([P, 4]))
            load(brt[:, 4:20], A["router_expert_b_2"].broadcast_to([P, 16]))
            load(adt[:, 0], A["a_log_2"].broadcast_to([P, 8]))
            load(adt[:, 1], A["dt_bias_2"].broadcast_to([P, 8]))
            load(u_w[:], A["spatial_w_2"][0].rearrange("g t s -> t g s"))
            assert 16 * loads[0] == SMALL, loads

            for j in (0, 2):
                copy(("xT", j), flat(xT[:, 2 * j:2 * j + 2]))
            for j in range(2):
                ps = full(act, ("aq", j)).rearrange("p (m t) -> p m t", m=2)
                for half in range(2):
                    ins = a(a_q[64 * j:64 * j + 64, half::2], ps[64 * half:64 * half + 64], ACT.Copy, scale=64.0 ** -0.5)
                evacuated(ins, ("aq", j))
            copy("aks", a_kk[:, 0], lambda ps: ps[:, 0:T])
            copy("avs", a_v[:, :, 0, :], lambda ps: ps[:, 0:T].rearrange("p (t n) -> p t n", t=TT))
            copy("akw", a_kk[:, 1], lambda ps: ps[:, 0:T])
            ps = full(act, "avw").rearrange("p (t n) -> p t n", t=TT)
            a(a_v[:, :, 1, :], ps[:, :, 0:P], ACT.Copy)
            evacuated(a(a_g, ps[:, :, P:P + 24], ACT.Sigmoid), "avw")
            ps = full(act, "ac1")
            act.wait_ge(S("vec_consts"), 1)
            read_out(act, "vec")
            a(a_g1, ps[0:64, 0:30], ACT.Gelu_apprx_tanh, bias=col("cmp_b1", 0)[0:64])
            for g in range(2):
                ins = a(a_g1v[:, g, :, 0:NCMP], ps[0:64, 32 + g * NCMP:32 + (g + 1) * NCMP].unsqueeze(1).broadcast_to([64, 4, NCMP]),
                        ACT.Gelu_apprx_tanh, bias=col("cmp_b1", 1)[0:64])
            evacuated(ins, "ac1")
            for j in range(2):
                copy(("au", j), a_u[0][:, 2 * j:2 * j + 2, 16:16 + T], lambda ps: ps.rearrange("p (a b) -> p a b", a=2))
            act.wait_ge(S("c_shifted"), 1)
            a(a_sc[:, :, :, 0:NCMP], a_sc[:, :, :, 0:NCMP], ACT.Exp).then_inc(S("c_exp"), 1)
            units = [(t, g, a_, h) for t in range(TT) for g in range(2) for a_ in range(2) for h in range(1 + t)]

            def exps(n):
                t, g, a_, h = units[n]
                nh, nk = (4, P) if t == 0 else (2, T)
                act.wait_ge(S("maxima"), n + 1)
                if n >= 3:
                    full(act, ("t", units[n - 3]))
                ps = full(act, ("s", units[n]))
                m = 32 + 8 * (n % 4)
                for i in range(nh):
                    ins = a(a_S[:, n % 3, i * nk:(i + 1) * nk], ps[:, i * nk:(i + 1) * nk], ACT.Exp, bias=a_m[:, m + i:m + i + 1],
                            accum_out=a_m[:, m + 4 + i:m + 5 + i])
                evacuated(ins, ("s", units[n]))

            for n in range(len(units) + 1):
                if n < len(units):
                    exps(n)
                if n == 1:
                    copy("apct", a_pcT.rearrange("p a b c -> p (a b c)"))
                if n:
                    copy(("t", units[n - 1]), a_T[:, (n - 1) % 3])
            for t in range(TT):
                copy(("o", t), a_o[:, 0:4, t * P:(t + 1) * P], lambda ps: ps.rearrange("p (i q) -> p i q", i=4))
            for j in range(2):
                ps = full(act, ("ap", j))
                for g in (2 * j, 2 * j + 1):
                    ins = a(a_o[:, 4 + g], ps[:, (g - 2 * j) * T:(g - 2 * j + 1) * T], ACT.Copy, scale=col("pool_scale", g))
                evacuated(ins, ("ap", j))
            deviations()

            def feed_forward(l, ln):
                features(ln)
                for c in range(NFF):
                    for j in range(2):
                        copy((f"h{l}_{c}", j), flat(f_h[:, c % 2, 2 * j:2 * j + 2]), func=ACT.Relu)
                deviations()

            feed_forward(0, 0)

            features(1)
            for j in range(2):
                copy(("gq", j), flat(c_q[:, 2 * j:2 * j + 2]), scale=float(P) ** -0.5)
            for t in range(TT):
                ps = full(act, ("gz", t))
                after(a(c_t1[:, t, :], ps, ACT.Abs))
                after(a(c_t1[:, t, :], c_t1[:, t, :], ACT.Exp, scale=-1.0))
                a(c_t1[:, t, :], c_t1[:, t, :], ACT.Ln, bias=1.0).then_inc(S("softplus"), 1)
            for j in range(2):
                copy(("gk", j), flat(c_k[:, 2 * j:2 * j + 2]))
            for t in range(TT):
                ps = full(act, ("gb", t))
                a(flat(c_eb[:, t]), ps, ACT.Exp, scale=1.0 / 16)
                evacuated(a(flat(c_en[:, t]), ps, ACT.Exp, scale=-1.0 / 16), ("gb", t))
            for i in range(2):
                for t in range(TT):
                    copy((f"gv{i}", t), c_v[:, t, i * BANK:(i + 1) * BANK])
            for i in range(2):
                for j in range(2):
                    copy((f"gr{i}", j), flat(c_r[:, 4 * i + 2 * j:4 * i + 2 * j + 2]), func=ACT.Silu)
            for t in range(TT):
                copy(("gk2", t), flat(c_k2[:, t]))
            for h in range(4):
                ps = full(act, ("go", h))
                a(flat(c_o[:, 2 * h:2 * h + 2]), ps, ACT.Copy)
                evacuated(a(flat(c_sq[:, 2 * h:2 * h + 2]), ps, ACT.Square), ("go", h))
            for j in range(2):
                r = flat(c_rs[:, 2 * j:2 * j + 2])
                ps = full(act, ("gn", j))
                evacuated(a(r, ps, ACT.Ln, scale=1.0 / T, bias=cst[:, 0:1]), ("gn", j))
                read_out(act, ("gn", j))
                a(r, r, ACT.Exp, scale=-0.5).then_inc(S("gla_rstd"), 1)
            deviations()
            feed_forward(1, 2)

            features(3)
            for j in range(2):
                copy(("uw", j), flat(u_wT[:, 4 * j:4 * j + 4]))
            for i in range(4):
                for t in range(TT):
                    copy((f"uv{i}", t), (u_u if i < 2 else u_v)[:, t, (i % 2) * BANK:(i % 2 + 1) * BANK], func=ACT.Gelu)
            deviations()
            for i in range(2):
                for j in range(2):
                    copy((f"gs{i}", j), flat(s_sg[:, 4 * i + 2 * j:4 * i + 2 * j + 2]), func=ACT.Sigmoid)
            for j in range(4):
                copy(("gT", j), flat(u_gT[:, 2 * j:2 * j + 2]))
            beta, g_, gcum, glast, f_kd, e_g, f_kb, y_ = (s_sc[:, i] for i in range(8))
            act.wait_ge(S("ab_ready"), 1)
            after(a(f_kb, y_, ACT.Abs))
            after(a(f_kb, f_kb, ACT.Exp, scale=-1.0))
            a(f_kb, f_kb, ACT.Ln, bias=1.0)
            a(adt[:, 0], adt[:, 0], ACT.Exp)
            a(beta, s_ab[:, :, 8:16], ACT.Exp, scale=-1.0).then_inc(S("ab_act"), 1)
            act.wait_ge(S("raw_pad"), 1)

            def silu(n):
                act.wait_ge(S("convolved"), n + 1)
                dst = (s_q, s_k, s_v)[n // 4]
                a(flat(dst[:, 2 * (n % 4):2 * (n % 4) + 2]), flat(s_acc[:, n % 2]), ACT.Silu).then_inc(S("qkv_done"), 1)

            for n in range(12):
                if n >= 2:
                    silu(n - 2)
                copy((f"qkv{n // 2}", n % 2), s_raw[:, n % 2, :, 3:3 + T], lambda ps: ps.rearrange("p (a b) -> p a b", a=2))
            silu(10)
            silu(11)
            for i in range(2):
                for j in range(2):
                    copy((f"z{i}", j), flat(s_z[:, 4 * i + 2 * j:4 * i + 2 * j + 2]), func=ACT.Silu)

            def rnorm(n, what, src, scale, sig):
                if n < what[1]:
                    if n >= 2:
                        full(act, (what[0], n - 2))
                    a(flat(s_acc[:, n % 2]), flat(src(n)), ACT.Square).then_inc(S(sig[0]), 1)
                if n:
                    m = n - 1
                    if m >= 2:
                        act.wait_ge(S(sig[2]), m - 1)
                    r = s_rn[:, (m % 2) * BANK:(m % 2) * BANK + BANK]
                    ps = full(act, (what[0], m))
                    evacuated(a(r, ps, ACT.Ln, scale=scale, bias=cst[:, 1:2]), (what[0], m))
                    read_out(act, (what[0], m))
                    a(r, r, ACT.Exp, scale=-0.5).then_inc(S(sig[1]), 1)

            act.wait_ge(S("qkv_done"), 12)
            for n in range(9):
                rnorm(n, ("qn", 8), lambda n: (s_q if n < 4 else s_k)[:, 2 * (n % 4):2 * (n % 4) + 2], 1.0, ("qk_squares", "qk_rnorm", "qk_normed"))
            act.wait_ge(S("gate_diff"), 1)
            a(e_g, gcum, ACT.Exp)
            a(f_kd, f_kd, ACT.Exp).then_inc(S("gate_exp"), 1)
            for hb in range(2):
                for t in range(TT):
                    ps = full(act, ("GB", hb, t))
                    act.wait_ge(S("decay_args"), hb * TT + t + 1)
                    evacuated(a(flat(s_qd[:, t]), ps, ACT.Exp), ("GB", hb, t))
                    a(flat(s_DT[:, t]), flat(s_DT[:, t]), ACT.Exp).then_inc(S("decay_rows"), 1)
                    a(flat(s_D[:, t]), flat(s_D[:, t]), ACT.Exp, scale=-1.0).then_inc(S("decay_exp"), 1)
                for t in range(TT):
                    copy(("at", hb, t), flat(s_B[:, t]))
                for l in range(1, LEVELS):
                    for t in range(TT):
                        copy(("Yl", hb, l, t), flat(s_Y[:, t]))
                for t in range(TT):
                    copy(("U", hb, t), flat(s_U[:, t]))
                    copy(("W", hb, t), flat(s_WT[:, t]))
                for n in range(NCH):
                    copy(("ot", hb, n), s_o[:, 4 * hb:4 * hb + 4, n * CH:(n + 1) * CH], lambda ps: ps[:, 0:T].rearrange("p (h t) -> p h t", h=4))
            for i in range(2):
                for j in range(2):
                    copy((f"gd{i}", j), flat(s_sg[:, 4 * i + 2 * j:4 * i + 2 * j + 2]), func=ACT.Sigmoid)
            read_out(act, ("ot", 1, NCH - 1))
            for n in range(5):
                rnorm(n, ("dn", 4), lambda n: s_o[:, 2 * n:2 * n + 2], 1.0 / P, ("dn_squares", "dn_rstd", "dn_out"))
            deviations()

            features(4)
            for i, k in enumerate((3, 7)):
                act.wait_ge(S("router_arg"), i + 1)
                a(e_sm[:, k, :, 0:4], e_sm[:, k, :, 0:4], ACT.Exp).then_inc(S("router_exp"), 1)
            for j in range(NEXP // 2):
                copy(("cb", j), flat(e_cb[:, 2 * j:2 * j + 2]))
            for e in range(NEXP):
                if e >= 2:
                    act.wait_ge(S("expert_h"), e - 1)
                copy((f"eg{e}", 0), flat(e_sg[:, e % 2]), func=ACT.Silu)
            deviations()

        @block.gpsimd
        def _(pool):
            gp = nc.gpsimd
            steps = [0]

            def after(ins):
                steps[0] += 1
                ins.then_inc(S("pool_step"), 1)
                pool.wait_ge(S("pool_step"), steps[0])

            AFF = [(A["ln1_g"][0], A["ln1_b"][0]), (A["ln2_g"][0], A["ln2_b"][0]), (A["ln1_g"][1], A["ln1_b"][1]),
                   (A["ln2_g"][1], A["ln2_b"][1]), (A["sgu_ln_g_2"][0], A["sgu_ln_b_2"][0]),
                   (A["ln1_g_2"][0], A["ln1_b_2"][0]), (A["ln2_g_2"][0], A["ln2_b_2"][0])]

            def load_affine(n):
                for i in range(2):
                    gp.dma_start(gb[:, i, :], AFF[n][i].unsqueeze(0).broadcast_to([P, D])).then_inc(S("affine"), 16)

            def keep(ap, pattern, base, mult, fill=0.0):
                after(gp.affine_select(out=ap, in_=ap, compare_op=ALU.is_ge, fill=fill, base=base, pattern=pattern, channel_multiplier=mult))

            load_affine(0)

            def grid(ap, b):
                return ap.rearrange("p (k b) -> p k b", b=b)

            for ap in (ident[:], tri[:], tril[:], blk[:], lvl0[:], cmk[:], hmask[:], lvl[:]):
                ins = gp.memset(ap, 1.0)
            gp.memset(caus[:], 0.0)
            after(gp.iota(a_ci.bitcast(mybir.dt.int32), pattern=[[1, T]], base=1, channel_multiplier=0))
            keep(ident[:], [[-1, P]], 0, 1)
            keep(ident[:], [[1, P]], 0, -1)
            keep(caus[:], [[-1, P]], 0, 1, NEG)
            gp.tensor_copy(identb[:], ident[:])
            gp.tensor_copy(maskb[:], caus[:])
            for ap in (tri[:], tril[:], blk[:]):
                keep(grid(ap, CH), [[-CH, P // CH], [0, CH]], 0, 1)
                keep(grid(ap, CH), [[CH, P // CH], [0, CH]], CH - 1, -1)
            keep(tri[:], [[1, P]], 0, -1)
            keep(tril[:], [[-1, P]], -1, 1)
            for l in range(LEVELS):
                b = 1 << l
                ap = grid(lvl[:, l], 2 * b)
                keep(ap, [[-2 * b, P // 2 // b], [0, 2 * b]], 0, 1)
                keep(ap, [[2 * b, P // 2 // b], [0, 2 * b]], b - 1, -1)
                keep(ap, [[0, P // 2 // b], [1, 2 * b]], -b, 0)
            keep(grid(lvl0[:], 2), [[-2, P // 2], [0, 2]], -1, 1)
            keep(grid(lvl0[:], 2), [[2, P // 2], [0, 2]], 1, -1)
            keep(grid(lvl0[:], 2), [[0, P // 2], [-1, 2]], 0, 0)
            keep(cmk[:], [[P, TT], [-16, 16]], -31, 1)
            keep(hmask[:], [[-32, 4]], 0, 1)
            keep(hmask[:], [[32, 4]], 31, -1)
            gp.tensor_scalar(cma[:], cmk[:], -1.0, -NEG, ALU.add, ALU.mult).then_inc(S("consts"), 1)
            after(gp.tensor_copy(a_rc[:, 0], a_ci.bitcast(mybir.dt.int32)))
            for g in range(3, -1, -1):
                ins = gp.tensor_scalar(a_rc[:, g], a_rc[:, 0], float(2 << g), None, ALU.min)
            ins.then_inc(S("win_counts"), 1)
            pool.wait_ge(S("win_recip"), 1)
            ua, ub, uc = a_u
            pool.wait_ge(S("vec_consts"), 1)
            for j in range(2):
                read_out(pool, ("au", j))
            E = 16 + T
            after(gp.tensor_tensor(ub[:, :, 1:E], ua[:, :, 1:E], ua[:, :, 0:E - 1], ALU.add))
            after(gp.tensor_tensor(uc[:, 1:4, 3:E], ub[:, 1:4, 3:E], ub[:, 1:4, 1:E - 2], ALU.add))
            after(gp.tensor_tensor(ub[:, 2:4, 7:E], uc[:, 2:4, 7:E], uc[:, 2:4, 3:E - 4], ALU.add))
            after(gp.tensor_tensor(uc[:, 3:4, 15:E], ub[:, 3:4, 15:E], ub[:, 3:4, 7:E - 8], ALU.add))
            for g, src in enumerate((ub, uc, ub, uc)):
                ins = gp.tensor_tensor(a_r[:, g], src[:, g, 16:E], a_rc[:, g], ALU.mult)
            after(ins)
            gp.tensor_tensor(a_r, a_r, ua[:, :, 16:E], ALU.subtract).then_inc(S("pooled"), 1)
            pool.wait_ge(S("small"), SMALL)
            gp.affine_select(out=u_w[:], in_=u_w[:], compare_op=ALU.is_ge, fill=0.0, base=0, pattern=[[0, 8], [-1, P]],
                             channel_multiplier=1).then_inc(S("sp_w_masked"), 1)

            def affine(n, l):
                for t in range(TT):
                    pool.wait_ge(S("affine"), 32 * (n + 1))
                    pool.wait_ge(S("normed"), l * TT + t + 1)
                    after(gp.tensor_tensor(xt[:, t, :], res[:, t, :], gb[:, 0, :], ALU.mult))
                    gp.tensor_tensor(xt[:, t, :], xt[:, t, :], gb[:, 1, :], ALU.add).then_inc(S("xt_ready"), 1)
                if n + 1 < len(AFF):
                    pool.wait_ge(S("xt_ready"), (l + 1) * TT)
                    load_affine(n + 1)

            for l in range(4):
                affine(l, l)
            for t in range(TT):
                pool.wait_ge(S("affine"), 32 * 5)
                pool.wait_ge(S("sgu_normed"), t + 1)
                after(gp.tensor_tensor(u_v[:, t, :], u_v[:, t, :], gb[:, 0, :], ALU.mult))
                gp.tensor_tensor(u_v[:, t, :], u_v[:, t, :], gb[:, 1, :], ALU.add).then_inc(S("sgu_v"), 1)
            pool.wait_ge(S("sgu_v"), TT)
            load_affine(5)

            def bmask(ap):
                return ap.unsqueeze(1).broadcast_to([P, 4, P])

            for hb in range(2):
                for t in range(TT):
                    pool.wait_ge(S("decay_exp"), hb * TT + t + 1)
                    gp.tensor_tensor(s_DT[:, t], s_DT[:, t], bmask(tri[:]), ALU.mult)
                    gp.tensor_tensor(s_D[:, t], s_D[:, t], bmask(tril[:]), ALU.mult).then_inc(S("decay_masked"), 1)
                for l in range(1, LEVELS):
                    for t in range(TT):
                        read_out(pool, ("at", hb, t))
                        if l > 1:
                            full(pool, ("Yl", hb, l - 1, t))
                        gp.tensor_tensor(s_Bl[:, t], s_B[:, t], bmask(lvl[:, l]), ALU.mult).then_inc(S("level_mask"), 1)
            affine(5, 4)
            affine(6, 5)

        @block.sync
        def _(sp):
            sp.dma_start(xt[:], A["x"][0].rearrange("(t p) d -> p t d", p=P)).then_inc(S("x_in"), 16)
            for n, (name, parts) in enumerate(chunks):
                if n >= RING:
                    sem, value = release[chunks[n - RING][0]]
                    sp.wait_ge(S(sem), value)
                for where, part, src, (k, c) in [(w, p_, s_, d_) if len(d_) == 2 else (w, p_, s_, (d_[0] * d_[1], d_[2])) for w, p_, s_, d_ in parts]:
                    p0, pn = part if isinstance(part, tuple) else (0, part)
                    dst = ring[p0:p0 + pn, n % RING, where]
                    if len(src.shape) == 4:
                        dst = dst.rearrange("p (v k n) -> p v k n", v=2, n=c)
                    else:
                        dst = dst.rearrange("p (k n) -> p k n", n=c)
                    sp.dma_start(dst, src).then_inc(S(f"weights{n % RING}"), 16)
            for t in range(TT):
                sp.wait_ge(S("xt_ready"), 5 * TT + t + 1)
                sp.dma_start(out[0, t * P:(t + 1) * P, :], xt[:, t, :]).then_inc(S("stored"), 16)
            sp.wait_ge(S("stored"), 16 * TT)


NAMES = ["x", "a_w_in", "a_cmp_pos", "a_cmp_w1", "a_cmp_b1", "a_cmp_w2", "a_pool_w", "a_pool_scale", "a_w_out", "c_w_in",
         "c_gate_w2", "c_gate_b", "c_norm_g", "c_w_out", "ln1_g", "ln1_b", "ln2_g", "ln2_b", "mlp_w1", "mlp_w2", "w_in_2",
         "conv_w_2", "a_log_2", "dt_bias_2", "dn_norm_g_2", "w_dn_out_2", "sgu_ln_g_2", "sgu_ln_b_2", "spatial_w_2",
         "spatial_b_2", "w_sgu_out_2", "w_out_2", "ln1_g_2", "ln1_b_2", "router_group_w_2", "router_group_b_2",
         "router_expert_w_2", "router_expert_b_2", "expert_w_gate_2", "expert_w_up_2", "expert_w_down_2", "ln2_g_2", "ln2_b_2"]


def kernel(**inputs):
    import numpy as np
    import concourse.bacc as bacc
    from concourse.bass_utils import run_bass_kernel_spmd

    nc = bacc.Bacc("TRN2", target_bir_lowering=False, num_devices=1)
    arrays, aps = {}, {}
    for name in NAMES:
        a = np.ascontiguousarray(inputs[name])
        arrays[f"in_{name}"] = a
        aps[name] = nc.dram_tensor(f"in_{name}", a.shape, mybir.dt.from_np(a.dtype), kind="ExternalInput").ap()
    out = nc.dram_tensor("out_x", (1, T, D), F32, kind="ExternalOutput").ap()
    build(nc, aps, out)
    r = run_bass_kernel_spmd(nc, [arrays], core_ids=[0])
    return r.results[0]["out_x"]
```

```python
from contextlib import ExitStack

import concourse.bass as bass
from concourse import mybir

ALU = mybir.AluOpType
ACT = mybir.ActivationFunctionType
AX = mybir.AxisListType
F32 = mybir.dt.float32
BF16 = mybir.dt.bfloat16
F32R = mybir.dt.float32r

P = 128
T = 256
TT = T // P
D = 1024
KT = D // P
BANK = 512
PIECE = 2048
W = 256
RING = 3
PARTS = 3
CH = 64
NCH = T // CH
ALPHA1 = 4.0 ** 0.25
ALPHA2 = 2.0 ** 0.25
LN_EPS = 1e-5
NORM_EPS = 1e-6
NEG = -1e30
NCMP = (T - 32) // 16 + 1
NFF = 16
NEXP = 16
VECTORS = 16 * 15
SMALL = 16 * 11
SPLIT_ORDER = (1, 0, 3, 2)
LEVELS = 6


def build(nc, A, out):
    def bc(ap, shape):
        return ap.broadcast_to(shape)

    with ExitStack() as ctx:
        def sb(name, shape, dt=F32):
            return ctx.enter_context(nc.sbuf_tensor(name, shape, dt))

        sems = {}

        def S(name):
            if name not in sems:
                sems[name] = ctx.enter_context(nc.semaphore(name))
            return sems[name]

        PS = ctx.enter_context(nc.psum_tensor("PS", [P, 8, BANK], F32))
        ring = sb("ring", [P, RING, PIECE])
        w_hi = sb("w_hi", [P, PARTS, PIECE], F32R)
        w_lo = sb("w_lo", [P, PARTS, PIECE], F32R)
        xt = sb("xt", [P, TT, D])
        x_hi = sb("x_hi", [P, KT, T], F32R)
        x_lo = sb("x_lo", [P, KT, T], F32R)
        o_hi = sb("o_hi", [P, KT, T], F32R)
        o_lo = sb("o_lo", [P, KT, T], F32R)
        res = sb("res", [P, TT, D])
        gb = sb("gb", [P, 2, D])
        ident = sb("ident", [P, P])
        identb = sb("identb", [P, P], BF16)
        maskb = sb("maskb", [P, P], BF16)
        ones = sb("ones", [P, P])
        tri = sb("tri", [P, P])
        tril = sb("tril", [P, P])
        blk = sb("blk", [P, P])
        lvl = sb("lvl", [P, LEVELS, P], BF16)
        lvl0 = sb("lvl0", [P, P])
        cmk = sb("cmk", [P, TT, 16])
        cma = sb("cma", [P, TT, 16])
        hmask = sb("hmask", [P, 4])
        vec = sb("vec", [P, P])
        cw = sb("cw", [P, P])
        w2c = sb("w2c", [CH, 2, 64])
        posc = cw[:, 96:P].rearrange("p (v k) -> p v k", v=2)
        wsm = sb("wsm", [P, KT, 16])
        wsm2 = sb("wsm2", [P, KT, 16])
        wga = sb("wga", [P, KT, 24])
        wrt = sb("wrt", [P, KT, 20])
        brt = sb("brt", [P, 20])
        adt = sb("adt", [P, 2, 8])
        st = sb("st", [P, 96])
        AR = sb("AR", [P, 15500])
        cst = sb("cst", [P, 4])

        def carve(off, *dims, p=P):
            n = 1
            for d in dims:
                n *= d
            v = AR[0:p, off:off + n]
            if len(dims) == 1:
                return v
            names = "abcd"[:len(dims)]
            kw = {names[i]: dims[i] for i in range(len(dims) - 1)}
            return v.rearrange(f"p ({' '.join(names)}) -> p {' '.join(names)}", **kw)

        VEC = {}
        for name, n in (("pool_scale", 4), ("g0", 8), ("g2", 8), ("b0", 8), ("b2", 8), ("g1", 8), ("g3", 8), ("b1", 8),
                        ("b3", 8), ("g4", 8), ("b4", 8), ("g5", 8), ("b5", 8), ("norm_g", 2),
                        ("dn_g", 1), ("sp_b", 8), ("cmp_b1", 2)):
            VEC[name] = sum(VEC[k][1] for k in VEC), n

        def col(name, i=0):
            return vec[:, VEC[name][0] + i:VEC[name][0] + i + 1]

        a_q = carve(0, 4, T)
        a_kk = carve(1024, 2, T)
        a_v = carve(1536, TT, 2, P)
        a_g = carve(2048, TT, 24)
        a_k2 = carve(2096, 2, 2, P)
        a_kb = carve(2608, 2, 16, 2, 15)
        a_g1 = carve(3568, 30, p=64)
        a_g1v = carve(3600, 2, 4, 32, p=64)
        a_kc = carve(3856, 15)
        a_vc = carve(3872, 4, 2, 64)
        a_sc = carve(4384, TT, 8, 16)
        a_pc = carve(4640, TT, 8, 32)
        a_pcT = carve(5152, 2, TT, P)
        a_S = carve(5664, 3, BANK)
        a_T = carve(7200, 3, BANK)
        a_m = carve(8736, 64)
        a_ci = carve(8800, T)
        a_rc = carve(9056, 4, T)
        a_u = [carve(10080 + i * 1088, 4, 16 + T) for i in range(3)]
        a_r = a_rc
        poolw = carve(13344, 4, P)
        rows = carve(13856, P)
        rowc = carve(13984, P)
        caus = carve(14112, P)
        a_ps = carve(14240, 2, BANK)
        n_v = carve(13400, 4, BANK)
        f_h = carve(0, 4, BANK)
        c_q, c_k, c_en = carve(0, 4, T), carve(1024, 4, T), carve(2048, TT, 4, P)
        c_o = carve(1024, 8, T)
        c_v = carve(3072, TT, D)
        c_r = res[:].rearrange("p t (k n) -> p (t k) n", n=T)
        c_la, c_t1 = carve(5120, TT, 512), carve(6144, TT, 512)
        c_sq = carve(5120, 8, T)
        c_eb = carve(7168, TT, 4, P)
        c_k2T, c_k2 = carve(8192, TT, 4, P), carve(9216, TT, 4, P)
        c_rs = carve(8192, 4, T)
        c_at = carve(10240, TT, 4, P)
        c_S = carve(11264, 3, 4, T)
        c_a = carve(14336, T, p=17)
        gw2 = carve(14592, 512, p=17)
        s_q, s_k, s_v = carve(0, 4, T), carve(1024, 4, T), carve(2048, 4, T)
        s_o = s_q
        s_z = res[:].rearrange("p t (k n) -> p (t k) n", n=T)
        DB = 3072
        s_D, s_DT, s_qd, s_B, s_Ti, s_R, s_Y, s_Kb, s_Kd, s_Vb, s_Bl = (carve(DB + i * 1024, TT, 4, P) for i in range(11))
        s_A, s_QK, s_U, s_WT = s_D, s_DT, s_Y, s_Bl
        s_S = carve(DB + 11 * 1024, 2, 4, P)
        s_raw = carve(DB, 2, 2, 3 + T)
        s_acc = carve(DB + 1040, 2, 2, T)
        s_sq = carve(DB + 2064, 2, 2, T)
        s_rn = carve(DB + 3088, 4 * BANK)
        s_M = carve(DB + 6 * 1024, 8, P)
        s_on = carve(DB, 4, T)
        s_sg, s_y = carve(0, 8, T), carve(2048, 8, T)
        u_u, u_v = carve(4096, TT, D), carve(6144, TT, D)
        u_wT, u_w = carve(8192, 8, P), carve(9216, 8, P)
        s_vn = sb("s_vn", [P, 4, P])
        s_ab = sb("s_ab", [P, TT, 16])
        s_sc = sb("s_sc", [P, 8, TT, 8])
        s_el = sb("s_el", [P, 4, NCH])
        e_cb = carve(0, NEXP, T)
        e_cT = carve(4096, T, p=NEXP)
        e_lg = carve(4352, TT, 20)
        e_sm = carve(4400, 16, TT, 16)
        e_h = carve(4912, 2, 2, T)
        e_sg = carve(5936, 2, 2, T)
        e_uc = carve(6960, 2, 2, T)

        chunks = []

        def cols(pre, src, c0, n, first=0):
            for i in range(n):
                c = c0 + W * i
                chunks.append(((pre, first + i), [((0, P), src[:, c:c + W].rearrange("(k p) n -> p k n", p=P), (KT, W))]))

        def rowsof(pre, src, r0, n, first=0):
            for i in range(n):
                r = r0 + W * i
                chunks.append(((pre, first + i), [((0, P), src[r:r + W, :].rearrange("(k p) n -> p k n", p=P), (2, D))]))

        aw = A["a_w_in"][0]
        cols("aq", aw, 0, 2)
        cols("acmp", aw, 512, 1)
        cols("akv", aw, 768, 2)
        chunks.append(("cmp_w1", [((0, P), A["a_cmp_w1"][0].rearrange("v (k p) n -> p v k n", p=P), (2 * 16, 64))]))
        cols("au", aw, 1304, 2)
        wo = A["a_w_out"][0]
        for i in range(2):
            chunks.append((("aout", i), [((64 * g, 64), wo[256 * g + 128 * i:256 * g + 128 * i + 128, :].rearrange("(k p) n -> p k n", p=64), (2, D))
                                         for g in range(2)]))
        rowsof("aout", wo, 512, 2, 2)

        def mlp_stream(l):
            w1, w2 = A["mlp_w1"][l], A["mlp_w2"][l]
            for c in range(NFF + 1):
                if c < NFF:
                    cols(f"f{l}w1", w1, W * c, 1, c)
                if c >= 1:
                    rowsof(f"f{l}w2", w2, W * (c - 1), 1, c - 1)

        mlp_stream(0)
        cwi = A["c_w_in"][0]
        cols("gq", cwi, 0, 2)
        cols("gk", cwi, 512, 2)
        cols("gv", cwi, 1024, 4)
        cols("gr", cwi, 2048, 4)
        rowsof("gout", A["c_w_out"][0], 0, 4)
        mlp_stream(1)
        wi = A["w_in_2"][0]
        UV = 3072 + 1024 + 16
        for hb in range(2):
            for i in range(3):
                cols(("q", "k", "v")[i], wi, D * i + 512 * hb, 2, 2 * hb)
            if hb == 0:
                cols("z", wi, 3072, 4)
        cols("gd", wi, UV + 2048, 4)
        cols("yd", A["w_dn_out_2"][0], 0, 4)
        cols("uv", wi, UV + 1024, 4, 4)
        cols("uv", wi, UV, 4)
        cols("gs", wi, UV + 3072, 4)
        cols("yg", A["w_sgu_out_2"][0], 0, 4)
        rowsof("sout", A["w_out_2"][0], 0, 4)
        wg, wu, wd = A["expert_w_gate_2"][0], A["expert_w_up_2"][0], A["expert_w_down_2"][0]
        for e in range(NEXP + 1):
            if e < NEXP:
                cols("eg", wg[e], 0, 1, e)
                cols("eu", wu[e], 0, 1, e)
            if e >= 1:
                rowsof("ed", wd[e - 1], 0, 1, e - 1)

        index = {name: n for n, (name, _) in enumerate(chunks)}
        split = [name for name, _ in chunks if name != "cmp_w1"]
        part = {name: m for m, name in enumerate(split)}
        landed, count = {}, [0] * RING
        for n, (name, parts) in enumerate(chunks):
            count[n % RING] += 16 * len(parts)
            landed[name] = n % RING, count[n % RING]
        release = {}

        def colview(t, n):
            return t[:, n, :].rearrange("p (k n) -> p k n", k=KT)

        def rowview(t, n):
            return t[:, n, :].rearrange("p (k n) -> p k n", k=2)

        def arrived(eng, name):
            s, v = landed[name]
            eng.wait_ge(S(f"weights{s}"), v)

        use, used = {}, [0] * 8
        cmp_used = []
        reached = [0]
        pieces_for = {}

        def claim(pe, name, bank):
            n = used[bank]
            used[bank] += 1
            use[name] = bank, n
            if n:
                pe.wait_ge(S(f"evac{bank}"), n)
            return PS[:, bank, :]

        def close(ins, name, chunk=None):
            bank, n = use[name]
            ins.then_inc(S(f"full{bank}"), 1)
            pieces_for[name] = reached[0]
            if chunk is not None:
                release[chunk] = f"full{bank}", n + 1

        def full(eng, name):
            bank, n = use[name]
            eng.wait_ge(S(f"full{bank}"), n + 1)
            return PS[:, bank, :]

        def evacuated(ins, name):
            ins.then_inc(S(f"evac{use[name][0]}"), 1)

        def read_out(eng, name):
            bank, n = use[name]
            eng.wait_ge(S(f"evac{bank}"), n + 1)

        turn = [0]

        def nxt(lo=0, hi=8):
            turn[0] += 1
            return lo + turn[0] % (hi - lo)

        block = ctx.enter_context(nc.Block())

        @block.tensor
        def _(pe):
            passed = [0]
            mm = nc.tensor.matmul

            def spent(ins, chunk):
                passed[0] += 1
                ins.then_inc(S("w_spent"), 1)
                release[chunk] = "w_spent", passed[0]

            def take(chunk):
                m = part[chunk]
                reached[0] = m + 1
                pe.wait_ge(S("pieces_split"), m + 1)
                return m % PARTS

            def products(out, a_hi, a_lo, b_hi, b_lo, first, last):
                mm(out, a_hi, b_hi, start=first, stop=False, skip_group_check=True)
                mm(out, a_hi, b_lo, start=False, stop=False, skip_group_check=True)
                return mm(out, a_lo, b_hi, start=False, stop=last, skip_group_check=True)

            def by_feature(chunk, a_hi=x_hi, a_lo=x_lo, lo=0, hi=8, ready=None, layer=None):
                n = take(chunk)
                wh, wl = colview(w_hi, n), colview(w_lo, n)
                ps = claim(pe, chunk, nxt(lo, hi))
                order = list(range(KT)) if layer is None else [2 * j + i for j in SPLIT_ORDER for i in range(2)]
                for m in range(2):
                    for i, k in enumerate(order):
                        if m == 0 and i % 2 == 0 and ready is not None:
                            read_out(pe, ready[k // 2])
                        if m == 0 and i % 2 == 0 and layer is not None:
                            pe.wait_ge(S("x_split"), 4 * (layer + 1) + i // 2 + 1)
                        c = slice(m * P, (m + 1) * P)
                        ins = products(ps[:, m * T:(m + 1) * T], wh[:, k, c], wl[:, k, c], a_hi[:, k, :], a_lo[:, k, :], i == 0, i == KT - 1)
                close(ins, chunk, chunk)

            def by_token(chunk, lo=0, hi=8):
                n = take(chunk)
                wh, wl = colview(w_hi, n), colview(w_lo, n)
                ps = claim(pe, chunk, nxt(lo, hi))
                for t in range(TT):
                    for k in range(KT):
                        c = slice(t * P, (t + 1) * P)
                        ins = products(ps[:, t * W:(t + 1) * W], x_hi[:, k, c], x_lo[:, k, c], wh[:, k, :], wl[:, k, :], k == 0, k == KT - 1)
                close(ins, chunk, chunk)

            def by_rows(chunk, k0, pre, first, last):
                n = take(chunk)
                wh, wl = rowview(w_hi, n), rowview(w_lo, n)
                for t in range(TT):
                    for half in range(2):
                        if first:
                            claim(pe, (pre, t, half), 2 * t + half)
                        for k in range(2):
                            c, b = slice(t * P, (t + 1) * P), slice(half * BANK, (half + 1) * BANK)
                            ins = products(PS[:, 2 * t + half, :], o_hi[:, k0 + k, c], o_lo[:, k0 + k, c], wh[:, k, b], wl[:, k, b],
                                           first and k == 0, last and k == 1)
                        if last:
                            close(ins, (pre, t, half), chunk if (t, half) == (TT - 1, 1) else None)
                if not last:
                    spent(ins, chunk)

            def with_x(ps, w, t=None):
                for i, x in enumerate((x_hi, x_lo)):
                    for k in range(KT):
                        if t is None:
                            ins = mm(ps, w[:, k, :], x[:, k, :].bitcast(F32), start=i + k == 0, stop=i * k == KT - 1)
                        else:
                            ins = mm(ps, x[:, k, t * P:(t + 1) * P].bitcast(F32), w[:, k, :], start=i + k == 0, stop=i * k == KT - 1)
                return ins

            def transposes(src, pre, lo=0, hi=8):
                for j in range(4):
                    ps = claim(pe, (pre, j), nxt(lo, hi))
                    for k in (2 * j, 2 * j + 1):
                        for t in range(TT):
                            o = (k - 2 * j) * T + t * P
                            ins = nc.tensor.transpose(ps[:, o:o + P], src[:, t, k * P:(k + 1) * P], ident[:])
                    close(ins, (pre, j))

            def norm_transposes(l):
                for j in range(4):
                    claim(pe, (f"nT{l}", j), nxt(4, 8))
                for t in range(TT):
                    for j in range(4):
                        pe.wait_ge(S("normed"), 2 * (TT * l + t) + j // 2 + 1)
                        ps = PS[:, use[f"nT{l}", j][0], :]
                        for i in range(2):
                            k, o = 2 * j + i, i * T + t * P
                            ins = nc.tensor.transpose(ps[:, o:o + P], res[:, t, k * P:(k + 1) * P], ident[:])
                        if t == TT - 1:
                            close(ins, (f"nT{l}", j))

            def x_ready(l):
                pe.wait_ge(S("x_split"), 4 * (l + 2))

            pe.wait_ge(S("identity"), 1)
            pe.wait_ge(S("x_in"), 16)
            transposes(xt, "xT")

            by_feature(("aq", 0), ready=[("xT", j) for j in range(4)])
            x_ready(-1)
            by_feature(("aq", 1))
            by_feature(("acmp", 0))
            pe.wait_ge(S("consts"), 1)
            pe.wait_ge(S("vectors"), VECTORS)
            ps = claim(pe, "vec", nxt())
            nc.tensor.transpose(ps[:, 0:P], rows, ident[:])
            ins = nc.tensor.transpose(ps[:, P:2 * P], rowc, ident[:])
            close(ins, "vec")
            for i in range(2):
                n = take(("akv", i))
                wh, wl = colview(w_hi, n), colview(w_lo, n)
                ps = claim(pe, ("ak", i), nxt())
                for k in range(KT):
                    ins = products(ps[:, 0:T], wh[:, k, 0:P], wl[:, k, 0:P], x_hi[:, k, :], x_lo[:, k, :], k == 0, k == KT - 1)
                close(ins, ("ak", i))
                ps = claim(pe, ("av", i), nxt())
                for t in range(TT):
                    for k in range(KT):
                        c = slice(t * P, (t + 1) * P)
                        ins = products(ps[:, t * P:(t + 1) * P], x_hi[:, k, c], x_lo[:, k, c], wh[:, k, P:W], wl[:, k, P:W], k == 0, k == KT - 1)
                close(ins, ("av", i), ("akv", i))
            pe.wait_ge(S("small"), SMALL)
            ps = claim(pe, "ag", nxt())
            for t in range(TT):
                ins = with_x(ps[:, t * 24:t * 24 + 24], wga, t)
            close(ins, "ag")
            arrived(pe, "cmp_w1")
            w = ring[:, index["cmp_w1"] % RING, :].rearrange("p (v k n) -> p v k n", v=2, k=16)
            pe.wait_ge(S("cmp_blocks"), 1)
            ps = claim(pe, "ac1", nxt())
            for v in range(2):
                for k in range(16):
                    ins = mm(ps[0:64, v * 32:v * 32 + 30], w[:, v, k, :], a_kb[:, v, k].rearrange("p g c -> p (g c)"), start=(k == 0), stop=(k == 15))
            close(ins, "ac1")
            cmp_used.extend(use["ac1"])
            for i in range(2):
                by_feature(("au", i))
            read_out(pe, "ac1")
            ps = claim(pe, "ac2", nxt())
            for g in range(2):
                mm(ps[g * 64:g * 64 + 64, 0:15], w2c[:, 0, :], a_g1[:, g * 15:g * 15 + 15], start=True, stop=True, skip_group_check=True)
            for g in range(2):
                ins = mm(ps[:, P + g * 64:P + g * 64 + 64], a_g1v[:, g].rearrange("p i c -> p (i c)"), w2c[:, 1, :], start=True, stop=True, skip_group_check=True)
            close(ins, "ac2")
            for j in range(2):
                read_out(pe, ("aq", j))
            read_out(pe, "ac2")
            for g in range(2):
                ps = claim(pe, ("asc", g), nxt(2, 8))
                for t in range(TT):
                    for i in range(4):
                        o = t * P + i * 32
                        ins = mm(ps[:, o:o + 15], a_q[64 * g:64 * g + 64, i, t * P:(t + 1) * P], a_kc[64 * g:64 * g + 64, :], start=True, stop=True)
                close(ins, ("asc", g))

            units = [(t, g, a, h) for t in range(TT) for g in range(2) for a in range(2) for h in range(1 + t)]

            def scores(u):
                t, g, a, h = u
                nh, nk = (4, P) if t == 0 else (2, T)
                read_out(pe, ("ak", a))
                ps = claim(pe, ("s", u), nxt(2, 8))
                for i in range(nh):
                    head = (h * nh + i)
                    mm(ps[:, i * nk:(i + 1) * nk], a_q[64 * g:64 * g + 64, head, t * P:(t + 1) * P], a_kk[64 * g:64 * g + 64, a, 0:nk],
                       start=True, stop=False, skip_group_check=True)
                    ins = mm(ps[:, i * nk + t * P:(i + 1) * nk], identb[:], maskb[:], start=False, stop=True, skip_group_check=True)
                close(ins, ("s", u))

            def prob_transposes(u, n):
                t, g, a, h = u
                nh, nk = (4, P) if t == 0 else (2, T)
                pe.wait_ge(S("probs"), n + 1)
                ps = claim(pe, ("t", u), nxt(2, 8))
                for i in range(nh):
                    for kb in range(1 + t):
                        o = (kb * nh + i) * P
                        ins = nc.tensor.transpose(ps[:, o:o + P], a_S[:, n % 3, i * nk + kb * P:i * nk + kb * P + P], ident[:])
                close(ins, ("t", u))

            def values(u, n):
                t, g, a, h = u
                nh = 4 if t == 0 else 2
                read_out(pe, ("t", u))
                for kb in range(1 + t):
                    o = h * nh * P
                    ins = mm(PS[64 * g:64 * g + 64, t, o:o + nh * P], a_v[:, kb, a, 64 * g:64 * g + 64],
                             a_T[:, n % 3, kb * nh * P:(kb + 1) * nh * P], start=False, stop=(kb == t), skip_group_check=True)
                if g == 1 and a == 1 and h == t:
                    close(ins, ("o", t))

            for n, u in enumerate(units[:2]):
                scores(u)
            pe.wait_ge(S("cprobs"), 1)
            ps = claim(pe, "apct", nxt(2, 8))
            for g in range(2):
                for t in range(TT):
                    ins = nc.tensor.transpose(ps[:, (g * TT + t) * P:(g * TT + t + 1) * P], a_pc[:, t, 4 * g:4 * g + 4].rearrange("p h c -> p (h c)"), ident[:])
            close(ins, "apct")
            for i in range(2):
                read_out(pe, ("av", i))
            read_out(pe, "apct")
            for t in range(TT):
                claim(pe, ("o", t), t)
                for g in range(2):
                    for i in range(4):
                        mm(PS[64 * g:64 * g + 64, t, i * P:(i + 1) * P], a_vc[:, i, g, :], a_pcT[:, g, t, :],
                           start=(i == 0), stop=False, skip_group_check=True)
            for n, u in enumerate(units):
                if n + 2 < len(units):
                    scores(units[n + 2])
                prob_transposes(u, n)
                if n:
                    values(units[n - 1], n - 1)
            values(units[-1], len(units) - 1)
            pe.wait_ge(S("pooled"), 1)
            for j in range(2):
                ps = claim(pe, ("ap", j), nxt(4, 8))
                for g in (2 * j, 2 * j + 1):
                    ins = mm(ps[:, (g - 2 * j) * T:(g - 2 * j + 1) * T], poolw[:, g, :], a_r[:, g, :], start=True, stop=True)
                close(ins, ("ap", j))
            pe.wait_ge(S("o_split"), TT)
            for i in range(2):
                by_rows(("aout", i), 2 * i, "m0", i == 0, False)
            pe.wait_ge(S("o_split"), TT + 2)
            for i in range(2, 4):
                by_rows(("aout", i), 2 * i, "m0", False, i == 3)

            def feed_forward(l, ln):
                norm_transposes(ln)
                for c in range(NFF + 1):
                    if c < NFF:
                        by_feature((f"f{l}w1", c), lo=4, hi=8, layer=ln if c == 0 else None)
                    if c:
                        pe.wait_ge(S("hidden"), l * NFF + c)
                        by_rows((f"f{l}w2", c - 1), 2 * ((c - 1) % 4), f"m{ln + 1}", c == 1, c == NFF)

            feed_forward(0, 0)

            norm_transposes(1)
            by_feature(("gq", 0), layer=1)
            ps = claim(pe, "ga", nxt())
            ins = with_x(ps[0:16, 0:T], wsm)
            close(ins, "ga")
            by_feature(("gq", 1))
            read_out(pe, "ga")
            pe.wait_ge(S("gate_w"), 32)
            for t in range(TT):
                ps = claim(pe, ("gz", t), nxt())
                ins = mm(ps, c_a[:, t * P:(t + 1) * P], gw2, start=True, stop=True)
                close(ins, ("gz", t))
            for i in range(2):
                by_feature(("gk", i))
            for t in range(TT):
                read_out(pe, ("gz", t))
                ps = claim(pe, ("gb", t), nxt())
                for h in range(4):
                    ins = mm(ps[:, h * P:(h + 1) * P], c_la[:, t, h * P:(h + 1) * P], tri[:], start=True, stop=True)
                close(ins, ("gb", t))
            for i in range(4):
                by_token(("gv", i))
            for i in range(4):
                by_feature(("gr", i))
            pe.wait_ge(S("gla_scaled"), 1)
            for t in range(TT):
                ps = claim(pe, ("gatt", t), nxt())
                for h in range(4):
                    ins = mm(ps[:, h * P:(h + 1) * P], c_k[:, h, t * P:(t + 1) * P], c_q[:, h, t * P:(t + 1) * P], start=True, stop=True)
                close(ins, ("gatt", t))
            pe.wait_ge(S("gla_scaled"), 2)
            for t in range(TT):
                ps = claim(pe, ("gk2", t), nxt())
                for h in range(4):
                    ins = nc.tensor.transpose(ps[:, h * P:(h + 1) * P], c_k2T[:, t, h, :], ident[:])
                close(ins, ("gk2", t))
            for t in range(TT):
                read_out(pe, ("gk2", t))
            for i in range(4):
                read_out(pe, ("gv", i))
            for n in range(NCH - 1):
                t, r = n // 2, 64 * (n % 2)
                for j in range(2):
                    ps = claim(pe, ("gu", n, j), nxt())
                    for h in (2 * j, 2 * j + 1):
                        ins = mm(ps[:, (h - 2 * j) * T:(h - 2 * j + 1) * T], c_k2[r:r + 64, t, h, :], c_v[r:r + 64, t, h * T:(h + 1) * T],
                                 start=True, stop=True)
                    close(ins, ("gu", n, j))
            for t in range(TT):
                read_out(pe, ("gatt", t))
            read_out(pe, ("gu", NCH - 2, 1))
            for h in range(4):
                ps = claim(pe, ("go", h), nxt())
                for e in range(2):
                    for t in range(TT):
                        mm(ps[:, e * T + t * P:e * T + (t + 1) * P], c_v[:, t, h * T + e * P:h * T + (e + 1) * P], c_at[:, t, h, :],
                           start=(t == 0), stop=False, skip_group_check=True)
                    for n in range(1, NCH):
                        ins = mm(ps[:, e * T + n * CH:e * T + (n + 1) * CH], c_S[:, n - 1, h, e * P:(e + 1) * P],
                                 c_q[:, h, n * CH:(n + 1) * CH], start=False, stop=(n == NCH - 1), skip_group_check=True)
                close(ins, ("go", h))
            for j in range(2):
                read_out(pe, ("go", 2 * j + 1))
                ps = claim(pe, ("gn", j), nxt())
                for h in (2 * j, 2 * j + 1):
                    for e in range(2):
                        ins = mm(ps[:, (h - 2 * j) * T:(h - 2 * j + 1) * T], ones[:], c_sq[:, 2 * h + e, :], start=(e == 0), stop=(e == 1))
                close(ins, ("gn", j))
            for i in range(4):
                pe.wait_ge(S("o_split"), TT + 2 + i + 1)
                by_rows(("gout", i), 2 * i, "m2", i == 0, i == 3)
            feed_forward(1, 2)

            norm_transposes(3)
            by_feature(("q", 0), layer=3)
            ps = claim(pe, "ab", nxt())
            for t in range(TT):
                ins = with_x(ps[:, t * 16:t * 16 + 16], wsm2, t)
            close(ins, "ab")
            by_feature(("q", 1))
            pe.wait_ge(S("dn_gates"), 1)
            ps = claim(pe, "gc", nxt())
            for t in range(TT):
                mm(ps[:, t * 8:t * 8 + 8], tri[:], s_sc[:, 1, t, :], start=True, stop=True)
            for t in range(TT):
                ins = mm(ps[:, 16 + t * 8:24 + t * 8], blk[:], s_sc[:, 1, t, :], start=True, stop=True)
            close(ins, "gc")
            for hb in range(2):
                for name in "qkv" if hb else "kv":
                    for i in range(2):
                        by_feature((name, 2 * hb + i))
                for t in range(TT):
                    pe.wait_ge(S("gate_rows"), hb * TT + t + 1)
                    ps = claim(pe, ("GB", hb, t), nxt())
                    ins = mm(ps, ones[:], s_M[:, 4 * t:4 * t + 4].rearrange("p h t -> p (h t)"), start=True, stop=True)
                    close(ins, ("GB", hb, t))
                for j in range(4):
                    pe.wait_ge(S("qk_squares"), 4 * hb + j + 1)
                    ps = claim(pe, ("qn", hb, j), nxt())
                    ins = mm(ps, ones[:], s_sq[:, j % 2].rearrange("p a b -> p (a b)"), start=True, stop=True)
                    close(ins, ("qn", hb, j))
                if hb == 0:
                    by_feature(("z", 0))
                pe.wait_ge(S("qk_normed"), 4 * hb + 4)
                pe.wait_ge(S("qkv_done"), 6 * hb + 6)
                for t in range(TT):
                    for what, rhs in (("kk", s_k), ("kq", s_q)):
                        ps = claim(pe, (what, hb, t), nxt())
                        for h in range(4):
                            ins = mm(ps[:, h * P:(h + 1) * P], s_k[:, h, t * P:(t + 1) * P], rhs[:, h, t * P:(t + 1) * P],
                                     start=True, stop=True)
                        close(ins, (what, hb, t))
                    for what, src in (("kt", s_k), ("vt", s_v)):
                        ps = claim(pe, (what, hb, t), nxt())
                        for h in range(4):
                            ins = nc.tensor.transpose(ps[:, h * P:(h + 1) * P], src[:, h, t * P:(t + 1) * P], ident[:])
                        close(ins, (what, hb, t))
                for t in range(TT):
                    read_out(pe, ("kk", hb, t))
                    ps = claim(pe, ("at", hb, t), nxt())
                    for h in range(4):
                        ins = nc.tensor.transpose(ps[:, h * P:(h + 1) * P], s_A[:, t, h, :], ident[:])
                    close(ins, ("at", hb, t))
                for l in range(1, LEVELS):
                    for t in range(TT):
                        pe.wait_ge(S("level_mask"), (hb * (LEVELS - 1) + l - 1) * TT + t + 1)
                        if l == 1:
                            pe.wait_ge(S("inv_start"), hb * TT + t + 1)
                        else:
                            read_out(pe, ("Rl", hb, l - 1, t))
                        ps = claim(pe, ("Yl", hb, l, t), nxt())
                        for h in range(4):
                            ins = mm(ps[:, h * P:(h + 1) * P], s_Bl[:, t, h, :], s_Ti[:, t, h, :], start=True, stop=True)
                        close(ins, ("Yl", hb, l, t))
                    if l in (1, 3, 5) and hb == 0:
                        by_feature(("z", (l + 1) // 2))
                    for t in range(TT):
                        read_out(pe, ("Yl", hb, l, t))
                        if l < LEVELS - 1:
                            ps = claim(pe, ("Tl", hb, l, t), nxt())
                            for h in range(4):
                                ins = mm(ps[:, h * P:(h + 1) * P], s_R[:, t, h, :], s_Y[:, t, h, :], start=True, stop=True)
                            close(ins, ("Tl", hb, l, t))
                        ps = claim(pe, ("Rl", hb, l, t), nxt())
                        for h in range(4):
                            ins = mm(ps[:, h * P:(h + 1) * P], s_Y[:, t, h, :], s_R[:, t, h, :], start=True, stop=True)
                        close(ins, ("Rl", hb, l, t))
                for t in range(TT):
                    read_out(pe, ("kt", hb, t))
                    read_out(pe, ("vt", hb, t))
                    read_out(pe, ("Rl", hb, LEVELS - 1, t))
                    ps = claim(pe, ("U", hb, t), nxt())
                    for h in range(4):
                        ins = mm(ps[:, h * P:(h + 1) * P], s_R[:, t, h, :], s_Vb[:, t, h, :], start=True, stop=True)
                    close(ins, ("U", hb, t))
                    ps = claim(pe, ("W", hb, t), nxt())
                    for h in range(4):
                        ins = mm(ps[:, h * P:(h + 1) * P], s_Kb[:, t, h, :], s_R[:, t, h, :], start=True, stop=True)
                    close(ins, ("W", hb, t))
                for t in range(TT):
                    read_out(pe, ("kq", hb, t))
                    read_out(pe, ("U", hb, t))
                    read_out(pe, ("W", hb, t))
                pe.wait_ge(S("q_decayed"), hb + 1)
                for n in range(NCH):
                    t, r = n // 2, CH * (n % 2)
                    cc = slice(r, r + CH)
                    if n:
                        read_out(pe, ("su", hb, n - 1))
                        ps = claim(pe, ("vn", hb, n), nxt())
                        for h in range(4):
                            ins = mm(ps[cc, h * P:(h + 1) * P], s_WT[:, t, h, cc], s_S[:, n % 2, h, :], start=True, stop=True)
                        close(ins, ("vn", hb, n))
                        read_out(pe, ("vn", hb, n))
                    else:
                        pe.wait_ge(S("v_first"), hb + 1)
                    if n < NCH - 1:
                        ps = claim(pe, ("su", hb, n), nxt())
                        for h in range(4):
                            ins = mm(ps[:, h * P:(h + 1) * P], s_Kd[cc, t, h, :], s_vn[cc, h, :], start=True, stop=True)
                        close(ins, ("su", hb, n))
                    ps = claim(pe, ("ot", hb, n), nxt())
                    for h in range(4):
                        if n:
                            mm(ps[:, h * CH:(h + 1) * CH], s_S[:, n % 2, h, :], s_qd[:, t, h, cc], start=True, stop=False)
                        ins = mm(ps[:, h * CH:(h + 1) * CH], s_vn[cc, h, :], s_QK[cc, t, h, cc], start=(n == 0), stop=True)
                    close(ins, ("ot", hb, n))
                for j in range(2):
                    pe.wait_ge(S("dn_squares"), 2 * hb + j + 1)
                    ps = claim(pe, ("dn", hb, j), nxt())
                    ins = mm(ps, ones[:], s_sq[:, j % 2].rearrange("p a b -> p (a b)"), start=True, stop=True)
                    close(ins, ("dn", hb, j))
            for i in range(4):
                by_feature(("gd", i))
            pe.wait_ge(S("o_split"), TT + 2 + 4 + 4)
            for i in range(4):
                by_feature(("yd", i), o_hi, o_lo)
            for i in (4, 5, 6, 7, 0, 1, 2, 3):
                by_token(("uv", i))
            pe.wait_ge(S("sp_w_masked"), 1)
            for j in range(2):
                ps = claim(pe, ("uw", j), nxt())
                for g in range(4):
                    ins = nc.tensor.transpose(ps[:, g * P:(g + 1) * P], u_w[:, 4 * j + g, :], ident[:])
                close(ins, ("uw", j))
            for i in range(4):
                by_feature(("gs", i))
            for j in range(2):
                read_out(pe, ("uw", j))
            for t in range(TT):
                pe.wait_ge(S("sgu_v"), t + 1)
                for j in range(2):
                    ps = claim(pe, ("sp", t, j), nxt())
                    for g in range(4):
                        ins = mm(ps[:, g * P:(g + 1) * P], u_wT[:, 4 * j + g, :], u_v[:, t, (4 * j + g) * P:(4 * j + g + 1) * P], start=True, stop=True)
                    close(ins, ("sp", t, j))
            for t in range(TT):
                for j in range(2):
                    read_out(pe, ("sp", t, j))
            transposes(u_u, "gT")
            pe.wait_ge(S("o_split"), TT + 2 + 4 + 4 + 4)
            for i in range(4):
                by_feature(("yg", i), o_hi, o_lo)
            for i in range(4):
                pe.wait_ge(S("o_split"), TT + 2 + 4 + 4 + 4 + i + 1)
                by_rows(("sout", i), 2 * i, "m4", i == 0, i == 3)

            norm_transposes(4)
            by_feature(("eg", 0), lo=0, hi=4, layer=4)
            ps = claim(pe, "rl", nxt(4, 8))
            for t in range(TT):
                ins = with_x(ps[:, t * 32:t * 32 + 20], wrt, t)
            close(ins, "rl")
            by_feature(("eu", 0), lo=0, hi=4)
            by_feature(("eg", 1), lo=0, hi=4)
            pe.wait_ge(S("combined"), 1)
            ps = claim(pe, "ct", nxt(4, 8))
            for t in range(TT):
                ins = nc.tensor.transpose(ps[0:NEXP, t * P:(t + 1) * P], e_sm[:, 15, t, :], ident[:])
            close(ins, "ct")
            read_out(pe, "ct")
            for j in range(NEXP // 2):
                ps = claim(pe, ("cb", j), nxt(4, 8))
                for e in (2 * j, 2 * j + 1):
                    ins = mm(ps[:, (e - 2 * j) * T:(e - 2 * j + 1) * T], ident[0:NEXP, e:e + 1].broadcast_to([NEXP, P]), e_cT[:], start=True, stop=True)
                close(ins, ("cb", j))
            for e in range(NEXP + 1):
                if 1 < e < NEXP:
                    by_feature(("eg", e), lo=4, hi=8)
                if 0 < e < NEXP:
                    by_feature(("eu", e), lo=4, hi=8)
                if e:
                    pe.wait_ge(S("expert_h"), e)
                    by_rows(("ed", e - 1), 2 * ((e - 1) % 4), "m5", e == 1, e == NEXP)

        @block.vector
        def _(ve):
            v = nc.vector
            steps = [0]

            def after(ins):
                steps[0] += 1
                ins.then_inc(S("vec_step"), 1)
                ve.wait_ge(S("vec_step"), steps[0])

            pieces = [0]

            def split_ahead(n):
                while pieces[0] < min(n + PARTS - 1, len(split)):
                    m = pieces[0]
                    pieces[0] += 1
                    ve.wait_ge(S("hi_split"), m + 1)
                    v.tensor_tensor(w_lo[:, m % PARTS], ring[:, index[split[m]] % RING], w_hi[:, m % PARTS].bitcast(F32), ALU.subtract)\
                        .then_inc(S("pieces_split"), 1)

            def bank(name):
                split_ahead(pieces_for[name])
                return full(ve, name)

            def read(name):
                split_ahead(pieces_for[name])
                read_out(ve, name)

            def flat(ap):
                return ap.rearrange("p a b -> p (a b)")

            def split_operand(src, k):
                h, lo = flat(o_hi[:, k:k + 2]), flat(o_lo[:, k:k + 2])
                after(v.tensor_copy(h, src))
                v.tensor_tensor(lo, src, h.bitcast(F32), ALU.subtract).then_inc(S("o_split"), 1)

            def layer_norm(l, alpha):
                for t in range(TT):
                    if l:
                        ve.wait_ge(S("xt_ready"), TT * (l - 1) + t + 1)
                    for n in range(2):
                        ps = bank((f"m{l}", t, n))
                        r = res[:, t, n * BANK:(n + 1) * BANK]
                        evacuated(v.scalar_tensor_tensor(r, xt[:, t, n * BANK:(n + 1) * BANK], alpha, ps, ALU.mult, ALU.add), (f"m{l}", t, n))
                        read((f"m{l}", t, n))
                        ins = v.bn_stats(st[:, 16 * t + 6 * n:16 * t + 6 * n + 6], r)
                    after(ins)
                    v.bn_aggr(st[:, 16 * t + 12:16 * t + 14], st[:, 16 * t:16 * t + 12]).then_inc(S("variance"), 1)
                    ve.wait_ge(S("deviation"), n_norm[0] * TT + t + 1)
                    after(v.reciprocal(st[:, 16 * t + 15:16 * t + 16], st[:, 16 * t + 14:16 * t + 15]))
                    for n in range(2):
                        r = res[:, t, n * BANK:(n + 1) * BANK]
                        v.tensor_scalar(r, r, st[:, 16 * t + 12:16 * t + 13], st[:, 16 * t + 15:16 * t + 16], ALU.subtract, ALU.mult).then_inc(S("normed"), 1)
                n_norm[0] += 1

            n_norm = [0]

            def features(l):
                for j in SPLIT_ORDER:
                    hi, lo = flat(x_hi[:, 2 * j:2 * j + 2]), flat(x_lo[:, 2 * j:2 * j + 2])
                    if j % 2:
                        ps = bank((f"nT{l}", j))
                        for k in (2 * j, 2 * j + 1):
                            o = slice((k - 2 * j) * T, (k - 2 * j + 1) * T)
                            ins = v.tensor_scalar(n_v[:, j, o], ps[:, o], col(f"g{l}", k), col(f"b{l}", k), ALU.mult, ALU.add)
                        evacuated(ins, (f"nT{l}", j))
                        read((f"nT{l}", j))
                        after(v.tensor_copy(hi, n_v[:, j]))
                    else:
                        ve.wait_ge(S("x_hi"), 2 * l + j // 2 + 1)
                    v.tensor_tensor(lo, n_v[:, j], hi.bitcast(F32), ALU.subtract).then_inc(S("x_split"), 1)

            v.memset(rows, 0.0).then_inc(S("rows_zero"), 1)
            v.memset(ones[:], 1.0)
            v.memset(cst[:, 0:1], LN_EPS)
            v.memset(cst[:, 1:2], NORM_EPS)
            v.memset(a_g1v, 0.0)
            v.memset(a_pc, 0.0)
            v.memset(a_u[0][:, :, 0:16], 0.0).then_inc(S("vec_consts"), 1)
            for j in range(4):
                ve.wait_ge(S("x0_hi"), j + 1)
                ps = bank(("xT", j))
                evacuated(v.tensor_tensor(flat(x_lo[:, 2 * j:2 * j + 2]), ps, flat(x_hi[:, 2 * j:2 * j + 2]).bitcast(F32), ALU.subtract), ("xT", j))
                read(("xT", j))
            v.memset(cst[:, 2:3], 0.0).then_inc(S("x_split"), 4)
            ve.wait_ge(S("win_counts"), 1)
            v.reciprocal(a_rc, a_rc).then_inc(S("win_recip"), 1)
            ps = bank("vec")
            v.tensor_copy(vec[:], ps[:, 0:P])
            evacuated(v.tensor_copy(cw[:], ps[:, P:2 * P]), "vec")
            ps = bank(("acmp", 0)).rearrange("p (v n e) -> p v n e", v=2, e=2)
            for par in range(2):
                for g in range(2):
                    ins = v.tensor_copy(a_k2[64 * par:64 * par + 64, :, g, :], ps[64 * g:64 * g + 64, :, :, par])
            evacuated(ins, ("acmp", 0))
            read(("acmp", 0))
            read("vec")
            for kv in range(2):
                for h in range(2):
                    ins = v.tensor_tensor(a_kb[:, kv, 8 * h:8 * h + 8], a_k2[:, kv, :, 8 * h:8 * h + 120].rearrange("q g (c p) -> q p g c", p=8),
                                          posc[:, kv, 8 * h:8 * h + 8].unsqueeze(2).unsqueeze(3).broadcast_to([P, 8, 2, NCMP]), ALU.add)
            ins.then_inc(S("cmp_blocks"), 1)
            ps = bank("ac2")
            v.tensor_copy(a_kc, ps[:, 0:NCMP])
            ve.wait_ge(S("consts"), 1)
            evacuated(v.tensor_tensor(a_vc.rearrange("p i g d -> p i (g d)"), ps[:, P:2 * P].unsqueeze(1).broadcast_to([P, 4, P]),
                                      hmask[:].unsqueeze(2).broadcast_to([P, 4, P]), ALU.mult), "ac2")
            sc = a_sc[:, :, :, 0:NCMP]
            cmx, csum = a_m[:, 0:16].rearrange("p (t h) -> p t h", t=TT), a_m[:, 16:32].rearrange("p (t h) -> p t h", t=TT)

            def over_c(ap):
                return ap.unsqueeze(3).broadcast_to([P, TT, 8, NCMP])

            for g in range(2):
                ps = bank(("asc", g))[:, 0:256].rearrange("p (t h c) -> p t h c", t=TT, h=4)[:, :, :, 0:NCMP]
                evacuated(v.tensor_tensor(sc[:, :, 4 * g:4 * g + 4], ps, cma[:, :, 0:NCMP].unsqueeze(2).broadcast_to([P, TT, 4, NCMP]), ALU.add),
                          ("asc", g))
                read(("asc", g))
            after(v.tensor_reduce(cmx, sc, AX.X, ALU.max))
            v.tensor_tensor(sc, sc, over_c(cmx), ALU.subtract).then_inc(S("c_shifted"), 1)
            ve.wait_ge(S("c_exp"), 1)
            after(v.tensor_tensor(sc, sc, cmk[:, :, 0:NCMP].unsqueeze(2).broadcast_to([P, TT, 8, NCMP]), ALU.mult))
            after(v.tensor_reduce(csum, sc, AX.X, ALU.add))
            after(v.tensor_scalar(csum, csum, 1e-30, None, ALU.max))
            after(v.reciprocal(csum, csum))
            read("ag")
            gates = a_g.rearrange("p t (h b) -> p t h b", b=3)
            after(v.tensor_tensor(csum, csum, gates[:, :, :, 0], ALU.mult))
            v.tensor_tensor(a_pc[:, :, :, 0:NCMP], sc, over_c(csum), ALU.mult).then_inc(S("cprobs"), 1)

            units = [(t, g, a, h) for t in range(TT) for g in range(2) for a in range(2) for h in range(1 + t)]

            def maxima(n):
                t, g, a, h = units[n]
                nh = 4 if t == 0 else 2
                m = a_m[:, 32 + 8 * (n % 4):32 + 8 * (n % 4) + nh]
                ps = bank(("s", units[n])).rearrange("p (h k) -> p h k", h=nh)
                if n >= 4:
                    read(("s", units[n - 4]))
                v.tensor_reduce(m, ps, AX.X, ALU.max, negate=True).then_inc(S("maxima"), 1)

            def weigh(n):
                t, g, a, h = units[n]
                nh, nk = (4, P) if t == 0 else (2, T)
                w = a_m[:, 32 + 8 * (n % 4) + 4:32 + 8 * (n % 4) + 4 + nh]
                h0 = 4 * g + h * nh
                read(("s", units[n]))
                after(v.reciprocal(w, w))
                after(v.tensor_tensor(w, w, gates[:, t, h0:h0 + nh, 1 + a], ALU.mult))
                s = a_S[:, n % 3, :].rearrange("p (h k) -> p h k", h=nh)
                v.tensor_tensor(s, s, w.unsqueeze(2).broadcast_to([P, nh, nk]), ALU.mult).then_inc(S("probs"), 1)

            for n in range(len(units) + 1):
                if n < len(units):
                    maxima(n)
                if n:
                    weigh(n - 1)
            for t in range(TT):
                ve.wait_ge(S("attn_hi"), t + 1)
                ps = bank(("o", t)).rearrange("p (i q) -> p i q", i=4)
                c = slice(t * P, (t + 1) * P)
                evacuated(v.tensor_tensor(o_lo[:, 0:4, c], ps, o_hi[:, 0:4, c].bitcast(F32), ALU.subtract), ("o", t))
            read(("o", 1))
            v.memset(cst[:, 2:3], 0.0).then_inc(S("o_split"), TT)
            for j in range(2):
                read(("ap", j))
                split_operand(a_ps[:, j], 4 + 2 * j)
            layer_norm(0, ALPHA1)

            def feed_forward(l, ln):
                features(ln)
                for c in range(NFF):
                    read((f"f{l}w1", c))
                    h, k = f_h[:, c % 4], 2 * (c % 4)
                    after(v.tensor_tensor(h, h, h, ALU.mult))
                    hi, lo = flat(o_hi[:, k:k + 2]), flat(o_lo[:, k:k + 2])
                    after(v.tensor_copy(hi, h))
                    v.tensor_tensor(lo, h, hi.bitcast(F32), ALU.subtract).then_inc(S("hidden"), 1)
                layer_norm(ln + 1, ALPHA1)

            feed_forward(0, 0)

            features(1)
            ve.wait_ge(S("x_split"), 12)
            after(v.memset(c_a, 1.0))
            ps = bank("ga")
            evacuated(v.tensor_copy(c_a[0:16, :], ps[0:16, 0:T]), "ga")
            for t in range(TT):
                ps = bank(("gz", t))
                ve.wait_ge(S("softplus"), t + 1)
                evacuated(v.scalar_tensor_tensor(c_la[:, t, :], ps, 0.0, c_t1[:, t, :], ALU.min, ALU.subtract), ("gz", t))
            for j in range(2):
                read(("gq", j))
                read(("gk", j))
            for t in range(TT):
                read(("gb", t))
                ts = slice(t * P, (t + 1) * P)
                v.tensor_tensor(c_k[:, :, ts], c_k[:, :, ts], c_en[:, t], ALU.mult)
                ins = v.tensor_tensor(c_q[:, :, ts], c_q[:, :, ts], c_eb[:, t], ALU.mult)
            ins.then_inc(S("gla_scaled"), 1)
            ve.wait_ge(S("gla_scaled"), 1)
            for t in range(TT):
                last = c_eb[:, t].rearrange("p h (c x) -> p h c x", x=CH)[:, :, :, CH - 1:CH].broadcast_to([P, 4, 2, CH])
                ins = v.tensor_tensor(c_k2T[:, t].rearrange("p h (c x) -> p h c x", x=CH),
                                      c_k[:, :, t * P:(t + 1) * P].rearrange("p h (c x) -> p h c x", x=CH), last, ALU.mult)
            ins.then_inc(S("gla_scaled"), 1)
            for t in range(TT):
                ps = bank(("gatt", t)).rearrange("p (h c) -> p h c", h=4)
                evacuated(v.tensor_tensor(c_at[:, t], ps, tri[:].unsqueeze(1).broadcast_to([P, 4, P]), ALU.mult), ("gatt", t))
            for n in range(NCH - 1):
                for j in range(2):
                    ps = bank(("gu", n, j))
                    if n == 0:
                        ins = v.tensor_copy(c_S[:, 0, 2 * j:2 * j + 2].rearrange("p a b -> p (a b)"), ps)
                    else:
                        read(("gu", n - 1, j))
                        for h in (2 * j, 2 * j + 1):
                            last = (n % 2) * CH + CH - 1
                            ins = v.scalar_tensor_tensor(c_S[:, n, h], c_S[:, n - 1, h], c_eb[:, n // 2, h, last:last + 1],
                                                         ps[:, (h - 2 * j) * T:(h - 2 * j + 1) * T], ALU.mult, ALU.add)
                    evacuated(ins, ("gu", n, j))
            for h in range(4):
                if h % 2 == 0:
                    ve.wait_ge(S("gla_rstd"), h // 2 + 1)
                for e in range(2):
                    ins = v.scalar_tensor_tensor(c_o[:, 2 * h + e], c_o[:, 2 * h + e], col("norm_g", e), c_rs[:, h], ALU.mult, ALU.mult)
                read(("gr", h))
                after(ins)
                o = flat(c_o[:, 2 * h:2 * h + 2])
                after(v.tensor_tensor(o, o, flat(c_r[:, 2 * h:2 * h + 2]), ALU.mult))
                split_operand(o, 2 * h)
            layer_norm(2, ALPHA1)
            feed_forward(1, 2)

            features(3)
            beta, g_, gcum, glast, f_kd, e_g, f_kb, y_ = (s_sc[:, i] for i in range(8))
            ps = bank("ab")
            evacuated(v.tensor_copy(s_ab[:], ps[:, 0:32].rearrange("p (t c) -> p t c", t=TT)), "ab")
            read("ab")
            v.tensor_tensor(y_, s_ab[:, :, 0:8], adt[:, 1:2].broadcast_to([P, TT, 8]), ALU.add).then_inc(S("ab_ready"), 1)
            ve.wait_ge(S("ab_act"), 1)
            ve.wait_ge(S("ab_ready"), 1)
            v.tensor_scalar(beta, beta, 1.0, None, ALU.add)
            after(v.scalar_tensor_tensor(y_, y_, 0.0, f_kb, ALU.max, ALU.add))
            v.reciprocal(beta, beta)
            v.scalar_tensor_tensor(g_, y_, -1.0, adt[:, 0:1].broadcast_to([P, TT, 8]), ALU.mult, ALU.mult).then_inc(S("dn_gates"), 1)
            ps = bank("gc")
            evacuated(v.tensor_copy(s_sc[:, 2:4].rearrange("p a t h -> p (a t h)"), ps[:, 0:32]), "gc")
            read("gc")
            v.tensor_tensor(f_kd, glast, gcum, ALU.subtract).then_inc(S("gate_diff"), 1)
            ve.wait_ge(S("gate_exp"), 1)
            v.tensor_tensor(f_kb, e_g, beta, ALU.mult)
            for hb in range(2):
                hs = slice(4 * hb, 4 * hb + 4)
                if hb:
                    ve.wait_ge(S("o_split"), TT + 2 + 4 + 2)
                v.memset(s_raw[:, :, :, 0:3], 0.0).then_inc(S("raw_pad"), 1)
                for n in range(6):
                    name = ("qkv"[n // 2], 2 * hb + n % 2)
                    read(name)
                    ve.wait_ge(S("raw_pad"), hb + 1)
                    if n >= 2:
                        ve.wait_ge(S("qkv_done"), 6 * hb + n - 1)
                    first = (n // 2) * 8 + 4 * hb + 2 * (n % 2)
                    for tap in range(3, -1, -1):
                        for m in range(2):
                            o, x = s_acc[:, n % 2, m], s_raw[:, n % 2, m, tap:tap + T]
                            wt = cw[:, tap * 24 + first + m:tap * 24 + first + m + 1]
                            if tap == 3:
                                ins = v.tensor_scalar(o, x, wt, None, ALU.mult)
                            else:
                                ins = v.scalar_tensor_tensor(o, x, wt, o, ALU.mult, ALU.add)
                        if tap:
                            after(ins)
                    ins.then_inc(S("convolved"), 1)
                def per_head(ap, t):
                    return ap[:, t, hs].unsqueeze(2).broadcast_to([P, 4, P])

                for t in range(TT):
                    v.tensor_tensor(s_M[:, 4 * t:4 * t + 4], tri[:].unsqueeze(1).broadcast_to([P, 4, P]), per_head(g_, t), ALU.mult)\
                        .then_inc(S("gate_rows"), 1)
                ve.wait_ge(S("qkv_done"), 6 * hb + 6)
                for t in range(TT):
                    ps = bank(("GB", hb, t))
                    for h in range(4):
                        o, gc = slice(h * P, (h + 1) * P), gcum[:, t, 4 * hb + h:4 * hb + h + 1]
                        v.tensor_scalar(s_DT[:, t, h], ps[:, o], gc, 0.0, ALU.subtract, ALU.min)
                        ins = v.tensor_scalar(s_D[:, t, h], ps[:, o], gc, 0.0, ALU.subtract, ALU.max)
                    ins.then_inc(S("decay_args"), 1)
                for n in range(4):
                    ve.wait_ge(S("qk_rnorm"), 4 * hb + n + 1)
                    x = flat((s_q if n < 2 else s_k)[:, 2 * (n % 2):2 * (n % 2) + 2])
                    v.scalar_tensor_tensor(x, x, float(P) ** -0.5 if n < 2 else 1.0, s_rn[:, n * BANK:(n + 1) * BANK],
                                           ALU.mult, ALU.mult).then_inc(S("qk_normed"), 1)
                ve.wait_ge(S("qk_normed"), 4 * hb + 4)

                for t in range(TT):
                    ve.wait_ge(S("decay_rows"), hb * TT + t + 1)
                    after(v.tensor_copy(s_el[:, :, 2 * t:2 * t + 2], s_qd[:, t].rearrange("p h (c x) -> p h c x", x=CH)[:, :, :, CH - 1]))
                    ins = v.tensor_tensor(s_qd[:, t], s_qd[:, t], s_q[:, :, t * P:(t + 1) * P], ALU.mult)
                    ins.then_inc(S("q_decayed"), 1)
                for t in range(TT):
                    ps = bank(("kk", hb, t))
                    ve.wait_ge(S("decay_masked"), hb * TT + t + 1)
                    for h in range(4):
                        ins = v.scalar_tensor_tensor(s_A[:, t, h], ps[:, h * P:(h + 1) * P], beta[:, t, 4 * hb + h:4 * hb + h + 1], s_D[:, t, h],
                                                     ALU.mult, ALU.mult)
                    evacuated(ins, ("kk", hb, t))
                    ps = bank(("kq", hb, t))
                    evacuated(v.tensor_tensor(s_QK[:, t].rearrange("p h t -> p (h t)"), ps, s_DT[:, t].rearrange("p h t -> p (h t)"), ALU.mult),
                              ("kq", hb, t))
                    ps = bank(("kt", hb, t)).rearrange("p (h d) -> p h d", h=4)
                    v.tensor_tensor(s_Kb[:, t], ps, per_head(f_kb, t), ALU.mult)
                    evacuated(v.tensor_tensor(s_Kd[:, t], ps, per_head(f_kd, t), ALU.mult), ("kt", hb, t))
                    ps = bank(("vt", hb, t)).rearrange("p (h d) -> p h d", h=4)
                    evacuated(v.tensor_tensor(s_Vb[:, t], ps, per_head(beta, t), ALU.mult), ("vt", hb, t))
                for t in range(TT):
                    read(("at", hb, t))
                    for o, x, m in ((s_Ti, s_A, lvl0[:]), (s_R, s_B, lvl[:, 0])):
                        ins = v.tensor_tensor(o[:, t], x[:, t], m.unsqueeze(1).broadcast_to([P, 4, P]), ALU.mult)
                    after(ins)
                    for o in (s_Ti, s_R):
                        ins = v.scalar_tensor_tensor(o[:, t], o[:, t], -1.0, ident[:].unsqueeze(1).broadcast_to([P, 4, P]), ALU.mult, ALU.add)
                    ins.then_inc(S("inv_start"), 1)
                    ve.wait_ge(S("inv_start"), hb * TT + t + 1)
                for l in range(1, LEVELS):
                    for t in range(TT):
                        for name, o in (("Tl", s_Ti), ("Rl", s_R)):
                            if name == "Tl" and l == LEVELS - 1:
                                continue
                            if l > 1:
                                read((name, hb, l - 1, t))
                            ps = bank((name, hb, l, t))
                            if name == "Tl":
                                bank(("Rl", hb, l, t))
                            x = o[:, t].rearrange("p h t -> p (h t)")
                            evacuated(v.tensor_tensor(x, x, ps, ALU.subtract), (name, hb, l, t))
                for n in range(NCH):
                    t, r = n // 2, CH * (n % 2)
                    cc = slice(r, r + CH)
                    u = s_U[cc, t].rearrange("p h t -> p (h t)")
                    read(("U", hb, t))
                    if n == 0:
                        v.tensor_copy(s_vn[cc].rearrange("p h t -> p (h t)"), u).then_inc(S("v_first"), 1)
                    else:
                        ps = bank(("vn", hb, n))
                        evacuated(v.tensor_tensor(s_vn[cc].rearrange("p h t -> p (h t)"), u, ps[cc, :], ALU.subtract), ("vn", hb, n))
                    if n < NCH - 1:
                        ps = bank(("su", hb, n))
                        if n == 0:
                            ins = v.tensor_copy(s_S[:, 1].rearrange("p h t -> p (h t)"), ps)
                        else:
                            read(("su", hb, n - 1))
                            for h in range(4):
                                ins = v.scalar_tensor_tensor(s_S[:, (n + 1) % 2, h], s_S[:, n % 2, h], s_el[:, h, n:n + 1], ps[:, h * P:(h + 1) * P],
                                                             ALU.mult, ALU.add)
                        evacuated(ins, ("su", hb, n))
                for j in range(2):
                    ve.wait_ge(S("dn_rstd"), 2 * hb + j + 1)
                    o = flat(s_on[:, 2 * j:2 * j + 2])
                    after(v.scalar_tensor_tensor(o, flat(s_o[:, 2 * j:2 * j + 2]), col("dn_g"), s_rn[:, j * BANK:(j + 1) * BANK], ALU.mult, ALU.mult))
                    read(("z", 2 * hb + j))
                    after(v.tensor_tensor(o, o, flat(s_z[:, 4 * hb + 2 * j:4 * hb + 2 * j + 2]), ALU.mult))
                    split_operand(o, 4 * hb + 2 * j)
            for i in range(4):
                ps = bank(("yd", i))
                read(("gd", i))
                evacuated(v.tensor_tensor(flat(s_y[:, 2 * i:2 * i + 2]), ps, flat(s_sg[:, 2 * i:2 * i + 2]), ALU.mult), ("yd", i))
            for i in range(4, 8):
                read(("uv", i))
            for t in range(TT):
                for i in range(2):
                    ins = v.bn_stats(st[:, 16 * t + 6 * i:16 * t + 6 * i + 6], u_v[:, t, i * BANK:(i + 1) * BANK])
                after(ins)
                v.bn_aggr(st[:, 16 * t + 12:16 * t + 14], st[:, 16 * t:16 * t + 12]).then_inc(S("variance"), 1)
            for t in range(TT):
                ve.wait_ge(S("deviation"), n_norm[0] * TT + t + 1)
                after(v.reciprocal(st[:, 16 * t + 15:16 * t + 16], st[:, 16 * t + 14:16 * t + 15]))
                v.tensor_scalar(u_v[:, t, :], u_v[:, t, :], st[:, 16 * t + 12:16 * t + 13], st[:, 16 * t + 15:16 * t + 16],
                                ALU.subtract, ALU.mult).then_inc(S("sgu_normed"), 1)
            n_norm[0] += 1
            for t in range(TT):
                for j in range(2):
                    for i in range(2):
                        read(("uv", 2 * j + i))
                    ps = bank(("sp", t, j))
                    for g in range(4):
                        u = u_u[:, t, (4 * j + g) * P:(4 * j + g + 1) * P]
                        ins = v.scalar_tensor_tensor(u, ps[:, g * P:(g + 1) * P], col("sp_b", 4 * j + g), u, ALU.add, ALU.mult)
                    evacuated(ins, ("sp", t, j))
            for j in range(4):
                ve.wait_ge(S("gated_hi"), j + 1)
                ps = bank(("gT", j))
                evacuated(v.tensor_tensor(flat(o_lo[:, 2 * j:2 * j + 2]), ps, flat(o_hi[:, 2 * j:2 * j + 2]).bitcast(F32), ALU.subtract), ("gT", j))
            read(("gT", 3))
            v.memset(cst[:, 2:3], 0.0).then_inc(S("o_split"), 4)
            for i in range(4):
                sg, y = flat(s_sg[:, 2 * i:2 * i + 2]), flat(s_y[:, 2 * i:2 * i + 2])
                ps = bank(("yg", i))
                read(("gs", i))
                evacuated(v.tensor_tensor(sg, ps, sg, ALU.mult), ("yg", i))
                read(("yg", i))
                after(v.tensor_tensor(y, y, sg, ALU.add))
            for i in range(4):
                split_operand(flat(s_y[:, 2 * i:2 * i + 2]), 2 * i)
            layer_norm(4, ALPHA2)

            features(4)
            lg, el = e_lg[:, :, 0:4], e_lg[:, :, 4:20].rearrange("p t (g j) -> p t g j", g=4)
            ps = bank("rl").rearrange("p (t c) -> p t c", c=32)[:, 0:TT, 0:20]
            evacuated(v.tensor_tensor(e_lg, ps, brt[:].unsqueeze(1).broadcast_to([P, TT, 20]), ALU.add), "rl")
            read("rl")

            def sm(i, n=4):
                return e_sm[:, i, :, 0:n]

            def one(i):
                return e_sm[:, i, :, 0:1].broadcast_to([P, TT, 4])

            first4 = e_sm[:, 14, :, 0:4]
            for i in range(4):
                ins = v.memset(e_sm[:, 14, :, i:i + 1], 4.0 - i)
            after(ins)

            def arg_max(x, m, tmp, o):
                after(v.tensor_reduce(sm(m, 1), x, AX.X, ALU.max))
                after(v.tensor_tensor(sm(tmp), x, one(m), ALU.is_equal))
                after(v.tensor_tensor(sm(tmp), sm(tmp), first4, ALU.mult))
                after(v.tensor_reduce(sm(13, 1), sm(tmp), AX.X, ALU.max))
                after(v.tensor_tensor(sm(o), sm(tmp), one(13), ALU.is_equal))

            arg_max(lg, 0, 1, 2)
            v.tensor_tensor(sm(3), lg, one(0), ALU.subtract).then_inc(S("router_arg"), 1)
            grp = e_sm[:, 15].rearrange("p t (g j) -> p t g j", g=4)
            after(v.tensor_tensor(grp, el, sm(2).unsqueeze(3).broadcast_to([P, TT, 4, 4]), ALU.mult))
            after(v.tensor_reduce(sm(5), e_sm[:, 15].rearrange("p t (g j) -> p t j g", g=4), AX.X, ALU.add))
            after(v.tensor_reduce(sm(6, 1), sm(5), AX.X, ALU.max))
            v.tensor_tensor(sm(7), sm(5), one(6), ALU.subtract).then_inc(S("router_arg"), 1)
            ve.wait_ge(S("router_exp"), 2)
            v.tensor_reduce(sm(4, 1), sm(3), AX.X, ALU.add)
            after(v.tensor_reduce(sm(8, 1), sm(7), AX.X, ALU.add))
            v.reciprocal(sm(4, 1), sm(4, 1))
            after(v.reciprocal(sm(8, 1), sm(8, 1)))
            after(v.tensor_tensor(sm(7), sm(7), one(8), ALU.mult))
            arg_max(sm(7), 9, 1, 10)
            after(v.scalar_tensor_tensor(sm(5), sm(10), -2.0, sm(7), ALU.mult, ALU.add))
            arg_max(sm(5), 11, 1, 12)
            v.tensor_tensor(sm(9, 1), sm(9, 1), sm(11, 1), ALU.add)
            after(v.tensor_tensor(sm(10), sm(10), sm(12), ALU.add))
            v.reciprocal(sm(9, 1), sm(9, 1))
            after(v.tensor_tensor(sm(7), sm(7), sm(10), ALU.mult))
            after(v.tensor_tensor(sm(7), sm(7), one(9), ALU.mult))
            after(v.tensor_tensor(sm(7), sm(7), one(4), ALU.mult))
            v.tensor_tensor(grp, sm(2).unsqueeze(3).broadcast_to([P, TT, 4, 4]), sm(7).unsqueeze(2).broadcast_to([P, TT, 4, 4]), ALU.mult)\
                .then_inc(S("combined"), 1)
            ps = bank("ct")
            evacuated(v.tensor_copy(e_cT, ps[0:NEXP, 0:T]), "ct")
            for e in range(NEXP):
                if e % 2 == 0:
                    read(("cb", e // 2))
                ps = bank(("eu", e)).rearrange("p (m t) -> p m t", m=2)
                evacuated(v.tensor_tensor(e_uc[:, e % 2], ps, e_cb[:, e:e + 1].broadcast_to([P, 2, T]), ALU.mult), ("eu", e))
                read(("eu", e))
                read(("eg", e))
                k = 2 * (e % 4)
                after(v.tensor_tensor(e_h[:, e % 2], e_uc[:, e % 2], e_sg[:, e % 2], ALU.mult))
                hi, lo = flat(o_hi[:, k:k + 2]), flat(o_lo[:, k:k + 2])
                after(v.tensor_copy(hi, flat(e_h[:, e % 2])))
                v.tensor_tensor(lo, flat(e_h[:, e % 2]), hi.bitcast(F32), ALU.subtract).then_inc(S("expert_h"), 1)
            layer_norm(5, ALPHA2)

        @block.scalar
        def _(act):
            a = nc.scalar.activation
            steps = [0]

            def after(ins):
                steps[0] += 1
                ins.then_inc(S("act_step"), 1)
                act.wait_ge(S("act_step"), steps[0])

            pieces = [0]

            def split_ahead(n):
                while pieces[0] < min(n + PARTS - 1, len(split)):
                    m = pieces[0]
                    pieces[0] += 1
                    arrived(act, split[m])
                    if m >= PARTS:
                        sem, value = release[split[m - PARTS]]
                        act.wait_ge(S(sem), value)
                    a(w_hi[:, m % PARTS], ring[:, index[split[m]] % RING], ACT.Copy).then_inc(S("hi_split"), 1)

            def bank(name):
                split_ahead(pieces_for[name])
                return full(act, name)

            def read(name):
                split_ahead(pieces_for[name])
                read_out(act, name)

            def copy(name, out, in_=None, scale=1.0, func=ACT.Copy):
                ps = bank(name)
                evacuated(a(out, ps if in_ is None else in_(ps), func, scale=scale), name)

            def flat(ap):
                return ap.rearrange("p a b -> p (a b)")

            n_norm = [0]

            def deviations(name):
                split_ahead(pieces_for[name])
                a(cst[:, 3:4], cst[:, 0:1], ACT.Sqrt)
                for t in range(TT):
                    act.wait_ge(S("variance"), n_norm[0] * TT + t + 1)
                    a(st[:, 16 * t + 14:16 * t + 15], st[:, 16 * t + 13:16 * t + 14], ACT.Sqrt, bias=cst[:, 0:1]).then_inc(S("deviation"), 1)
                n_norm[0] += 1

            def features(l):
                for j in (0, 2):
                    ps = bank((f"nT{l}", j))
                    for k in (2 * j, 2 * j + 1):
                        o = slice((k - 2 * j) * T, (k - 2 * j + 1) * T)
                        ins = a(n_v[:, j, o], ps[:, o], ACT.Identity, scale=col(f"g{l}", k), bias=col(f"b{l}", k))
                    evacuated(ins, (f"nT{l}", j))
                    read((f"nT{l}", j))
                    a(flat(x_hi[:, 2 * j:2 * j + 2]), n_v[:, j], ACT.Copy).then_inc(S("x_hi"), 1)

            for j in range(4):
                ps = bank(("xT", j))
                a(flat(x_hi[:, 2 * j:2 * j + 2]), ps, ACT.Copy).then_inc(S("x0_hi"), 1)
            for j in range(2):
                ps = bank(("aq", j)).rearrange("p (m t) -> p m t", m=2)
                for half in range(2):
                    ins = a(a_q[64 * j:64 * j + 64, half::2], ps[64 * half:64 * half + 64], ACT.Copy, scale=64.0 ** -0.5)
                evacuated(ins, ("aq", j))
            for i in range(2):
                copy(("ak", i), a_kk[:, i], lambda ps: ps[:, 0:T])
                copy(("av", i), a_v[:, :, i, :], lambda ps: ps[:, 0:T].rearrange("p (t n) -> p t n", t=TT))
            copy("ag", a_g, lambda ps: ps[:, 0:TT * 24].rearrange("p (t n) -> p t n", t=TT), func=ACT.Sigmoid)
            ps = bank("ac1")
            act.wait_ge(S("vec_consts"), 1)
            read("vec")
            a(a_g1, ps[0:64, 0:30], ACT.Gelu_apprx_tanh, bias=col("cmp_b1", 0)[0:64])
            for g in range(2):
                ins = a(a_g1v[:, g, :, 0:NCMP], ps[0:64, 32 + g * NCMP:32 + (g + 1) * NCMP].unsqueeze(1).broadcast_to([64, 4, NCMP]),
                        ACT.Gelu_apprx_tanh, bias=col("cmp_b1", 1)[0:64])
            evacuated(ins, "ac1")
            for j in range(2):
                copy(("au", j), a_u[0][:, 2 * j:2 * j + 2, 16:16 + T], lambda ps: ps.rearrange("p (a b) -> p a b", a=2))
            act.wait_ge(S("c_shifted"), 1)
            a(a_sc[:, :, :, 0:NCMP], a_sc[:, :, :, 0:NCMP], ACT.Exp).then_inc(S("c_exp"), 1)
            units = [(t, g, a_, h) for t in range(TT) for g in range(2) for a_ in range(2) for h in range(1 + t)]

            def exps(n):
                t, g, a_, h = units[n]
                nh, nk = (4, P) if t == 0 else (2, T)
                act.wait_ge(S("maxima"), n + 1)
                if n >= 3:
                    bank(("t", units[n - 3]))
                ps = bank(("s", units[n]))
                m = 32 + 8 * (n % 4)
                for i in range(nh):
                    ins = a(a_S[:, n % 3, i * nk:(i + 1) * nk], ps[:, i * nk:(i + 1) * nk], ACT.Exp, bias=a_m[:, m + i:m + i + 1],
                            accum_out=a_m[:, m + 4 + i:m + 5 + i])
                evacuated(ins, ("s", units[n]))

            for n in range(len(units) + 1):
                if n < len(units):
                    exps(n)
                if n == 1:
                    copy("apct", a_pcT.rearrange("p a b c -> p (a b c)"))
                if n:
                    copy(("t", units[n - 1]), a_T[:, (n - 1) % 3])
            for t in range(TT):
                ps = bank(("o", t)).rearrange("p (i q) -> p i q", i=4)
                a(o_hi[:, 0:4, t * P:(t + 1) * P], ps, ACT.Copy).then_inc(S("attn_hi"), 1)
            for j in range(2):
                ps = bank(("ap", j))
                for g in (2 * j, 2 * j + 1):
                    o = slice((g - 2 * j) * T, (g - 2 * j + 1) * T)
                    ins = a(a_ps[:, j, o], ps[:, o], ACT.Copy, scale=col("pool_scale", g))
                evacuated(ins, ("ap", j))
            deviations(("m0", 1, 1))

            def feed_forward(l, ln):
                features(ln)
                for c in range(NFF):
                    copy((f"f{l}w1", c), f_h[:, c % 4], func=ACT.Relu)
                deviations((f"m{ln + 1}", 1, 1))

            feed_forward(0, 0)

            features(1)
            for j in range(2):
                copy(("gq", j), flat(c_q[:, 2 * j:2 * j + 2]), scale=float(P) ** -0.5)
            for t in range(TT):
                ps = bank(("gz", t))
                after(a(c_t1[:, t, :], ps, ACT.Abs))
            for t in range(TT):
                ins = a(c_t1[:, t, :], c_t1[:, t, :], ACT.Exp, scale=-1.0)
            after(ins)
            for t in range(TT):
                a(c_t1[:, t, :], c_t1[:, t, :], ACT.Ln, bias=1.0).then_inc(S("softplus"), 1)
            for j in range(2):
                copy(("gk", j), flat(c_k[:, 2 * j:2 * j + 2]))
            for t in range(TT):
                ps = bank(("gb", t))
                a(flat(c_eb[:, t]), ps, ACT.Exp, scale=1.0 / 16)
                evacuated(a(flat(c_en[:, t]), ps, ACT.Exp, scale=-1.0 / 16), ("gb", t))
            for i in range(4):
                copy(("gv", i), c_v[:, :, i * W:(i + 1) * W], lambda ps: ps.rearrange("p (t n) -> p t n", t=TT))
            act.wait_ge(S("xt_ready"), 2 * TT)
            for i in range(4):
                copy(("gr", i), flat(c_r[:, 2 * i:2 * i + 2]), func=ACT.Silu)
            for t in range(TT):
                copy(("gk2", t), flat(c_k2[:, t]))
            for h in range(4):
                ps = bank(("go", h))
                a(flat(c_o[:, 2 * h:2 * h + 2]), ps, ACT.Copy)
                evacuated(a(flat(c_sq[:, 2 * h:2 * h + 2]), ps, ACT.Square), ("go", h))
            for j in range(2):
                ps = bank(("gn", j))
                evacuated(a(flat(c_rs[:, 2 * j:2 * j + 2]), ps, ACT.Ln, scale=1.0 / T, bias=cst[:, 0:1]), ("gn", j))
            for j in range(2):
                read(("gn", j))
                r = flat(c_rs[:, 2 * j:2 * j + 2])
                a(r, r, ACT.Exp, scale=-0.5).then_inc(S("gla_rstd"), 1)
            deviations(("m2", 1, 1))
            feed_forward(1, 2)

            features(3)
            beta, g_, gcum, glast, f_kd, e_g, f_kb, y_ = (s_sc[:, i] for i in range(8))
            split_ahead(pieces_for["ab"])
            act.wait_ge(S("ab_ready"), 1)
            after(a(f_kb, y_, ACT.Abs))
            after(a(f_kb, f_kb, ACT.Exp, scale=-1.0))
            a(f_kb, f_kb, ACT.Ln, bias=1.0)
            a(adt[:, 0], adt[:, 0], ACT.Exp)
            a(beta, s_ab[:, :, 8:16], ACT.Exp, scale=-1.0).then_inc(S("ab_act"), 1)
            split_ahead(pieces_for["gc"])
            act.wait_ge(S("gate_diff"), 1)
            a(e_g, gcum, ACT.Exp)
            a(f_kd, f_kd, ACT.Exp).then_inc(S("gate_exp"), 1)

            def silu(hb, n):
                act.wait_ge(S("convolved"), 6 * hb + n + 1)
                dst = (s_q, s_k, s_v)[n // 2]
                a(flat(dst[:, 2 * (n % 2):2 * (n % 2) + 2]), flat(s_acc[:, n % 2]), ACT.Silu).then_inc(S("qkv_done"), 1)

            def rnorm(what, hb, N, src, scale, sums, out):
                def r(m):
                    return s_rn[:, m * BANK:(m + 1) * BANK]

                for n in range(N + 1):
                    if n < N:
                        if n >= 2:
                            bank((what, hb, n - 2))
                        a(flat(s_sq[:, n % 2]), flat(src(n)), ACT.Square).then_inc(S(sums), 1)
                    if n:
                        ps = bank((what, hb, n - 1))
                        evacuated(a(r(n - 1), ps, ACT.Ln, scale=scale, bias=cst[:, 1:2]), (what, hb, n - 1))
                for m in range(N):
                    read((what, hb, m))
                    a(r(m), r(m), ACT.Exp, scale=-0.5).then_inc(S(out), 1)

            for hb in range(2):
                if hb:
                    act.wait_ge(S("o_split"), TT + 2 + 4 + 2)
                act.wait_ge(S("raw_pad"), hb + 1)
                for n in range(6):
                    if n >= 2:
                        silu(hb, n - 2)
                    copy(("qkv"[n // 2], 2 * hb + n % 2), s_raw[:, n % 2, :, 3:3 + T], lambda ps: ps.rearrange("p (a b) -> p a b", a=2))
                silu(hb, 4)
                silu(hb, 5)
                act.wait_ge(S("qkv_done"), 6 * hb + 6)
                rnorm("qn", hb, 4, lambda n: (s_q if n < 2 else s_k)[:, 2 * (n % 2):2 * (n % 2) + 2], 1.0, "qk_squares", "qk_rnorm")
                if hb == 0:
                    act.wait_ge(S("xt_ready"), 4 * TT)
                    copy(("z", 0), flat(s_z[:, 0:2]), func=ACT.Silu)
                for t in range(TT):
                    ps = bank(("GB", hb, t))
                    act.wait_ge(S("decay_args"), hb * TT + t + 1)
                    evacuated(a(flat(s_qd[:, t]), ps, ACT.Exp), ("GB", hb, t))
                    a(flat(s_DT[:, t]), flat(s_DT[:, t]), ACT.Exp).then_inc(S("decay_rows"), 1)
                    a(flat(s_D[:, t]), flat(s_D[:, t]), ACT.Exp, scale=-1.0).then_inc(S("decay_exp"), 1)
                for t in range(TT):
                    copy(("at", hb, t), flat(s_B[:, t]))
                for l in range(1, LEVELS):
                    for t in range(TT):
                        copy(("Yl", hb, l, t), flat(s_Y[:, t]))
                    if l in (1, 3, 5) and hb == 0:
                        i = (l + 1) // 2
                        copy(("z", i), flat(s_z[:, 2 * i:2 * i + 2]), func=ACT.Silu)
                for t in range(TT):
                    copy(("U", hb, t), flat(s_U[:, t]))
                    copy(("W", hb, t), flat(s_WT[:, t]))
                for n in range(NCH):
                    copy(("ot", hb, n), s_o[:, :, n * CH:(n + 1) * CH], lambda ps: ps[:, 0:T].rearrange("p (h t) -> p h t", h=4))
                read(("ot", hb, NCH - 1))
                rnorm("dn", hb, 2, lambda n: s_o[:, 2 * n:2 * n + 2], 1.0 / P, "dn_squares", "dn_rstd")
            act.wait_ge(S("o_split"), TT + 2 + 4 + 4)
            for i in range(4):
                copy(("gd", i), flat(s_sg[:, 2 * i:2 * i + 2]), func=ACT.Sigmoid)
            for i in (4, 5, 6, 7, 0, 1, 2, 3):
                copy(("uv", i), (u_u if i < 4 else u_v)[:, :, (i % 4) * W:(i % 4 + 1) * W], lambda ps: ps.rearrange("p (t n) -> p t n", t=TT), func=ACT.Gelu)
                if i == 7:
                    deviations(("uv", 7))
            for j in range(2):
                copy(("uw", j), flat(u_wT[:, 4 * j:4 * j + 4]))
            read(("yd", 3))
            for i in range(4):
                copy(("gs", i), flat(s_sg[:, 2 * i:2 * i + 2]), func=ACT.Sigmoid)
            for j in range(4):
                ps = bank(("gT", j))
                a(flat(o_hi[:, 2 * j:2 * j + 2]), ps, ACT.Copy).then_inc(S("gated_hi"), 1)
            deviations(("m4", 1, 1))

            features(4)
            split_ahead(pieces_for["rl"])
            for i, k in enumerate((3, 7)):
                act.wait_ge(S("router_arg"), i + 1)
                a(e_sm[:, k, :, 0:4], e_sm[:, k, :, 0:4], ACT.Exp).then_inc(S("router_exp"), 1)
            for j in range(NEXP // 2):
                copy(("cb", j), flat(e_cb[:, 2 * j:2 * j + 2]))
            for e in range(NEXP):
                if e >= 2:
                    act.wait_ge(S("expert_h"), e - 1)
                copy(("eg", e), flat(e_sg[:, e % 2]), func=ACT.Silu)
            deviations(("m5", 1, 1))

        @block.gpsimd
        def _(pool):
            gp = nc.gpsimd
            steps = [0]

            def after(ins):
                steps[0] += 1
                ins.then_inc(S("pool_step"), 1)
                pool.wait_ge(S("pool_step"), steps[0])

            AFF = [(A["ln1_g"][0], A["ln1_b"][0]), (A["ln2_g"][0], A["ln2_b"][0]), (A["ln1_g"][1], A["ln1_b"][1]),
                   (A["ln2_g"][1], A["ln2_b"][1]), (A["sgu_ln_g_2"][0], A["sgu_ln_b_2"][0]),
                   (A["ln1_g_2"][0], A["ln1_b_2"][0]), (A["ln2_g_2"][0], A["ln2_b_2"][0])]

            def load_affine(n):
                for i in range(2):
                    gp.dma_start(gb[:, i, :], AFF[n][i].unsqueeze(0).broadcast_to([P, D])).then_inc(S("affine"), 16)

            def keep(ap, pattern, base, mult, fill=0.0):
                after(gp.affine_select(out=ap, in_=ap, compare_op=ALU.is_ge, fill=fill, base=base, pattern=pattern, channel_multiplier=mult))

            def grid(ap, b):
                return ap.rearrange("p (k b) -> p k b", b=b)

            after(gp.memset(ident[:], 1.0))
            keep(ident[:], [[-1, P]], 0, 1)
            keep(ident[:], [[1, P]], 0, -1)
            gp.tensor_copy(identb[:], ident[:]).then_inc(S("identity"), 1)
            for ap in (tri[:], tril[:], blk[:], lvl0[:], cmk[:], hmask[:], lvl[:]):
                ins = gp.memset(ap, 1.0)
            gp.memset(caus, 0.0)
            after(gp.iota(a_ci.bitcast(mybir.dt.int32), pattern=[[1, T]], base=1, channel_multiplier=0))
            keep(caus, [[-1, P]], 0, 1, NEG)
            gp.tensor_copy(maskb[:], caus)
            for ap in (tri[:], tril[:], blk[:]):
                keep(grid(ap, CH), [[-CH, P // CH], [0, CH]], 0, 1)
                keep(grid(ap, CH), [[CH, P // CH], [0, CH]], CH - 1, -1)
            keep(tri[:], [[1, P]], 0, -1)
            keep(tril[:], [[-1, P]], -1, 1)
            for l in range(LEVELS):
                b = 1 << l
                ap = grid(lvl[:, l], 2 * b)
                keep(ap, [[-2 * b, P // 2 // b], [0, 2 * b]], 0, 1)
                keep(ap, [[2 * b, P // 2 // b], [0, 2 * b]], b - 1, -1)
                keep(ap, [[0, P // 2 // b], [1, 2 * b]], -b, 0)
            keep(grid(lvl0[:], 2), [[-2, P // 2], [0, 2]], -1, 1)
            keep(grid(lvl0[:], 2), [[2, P // 2], [0, 2]], 1, -1)
            keep(grid(lvl0[:], 2), [[0, P // 2], [-1, 2]], 0, 0)
            load_affine(0)
            keep(cmk[:], [[P, TT], [-16, 16]], -31, 1)
            keep(hmask[:], [[-32, 4]], 0, 1)
            keep(hmask[:], [[32, 4]], 31, -1)
            gp.tensor_scalar(cma[:], cmk[:], -1.0, -NEG, ALU.add, ALU.mult).then_inc(S("consts"), 1)
            after(gp.tensor_copy(a_rc[:, 0], a_ci.bitcast(mybir.dt.int32)))
            for g in range(3, -1, -1):
                ins = gp.tensor_scalar(a_rc[:, g], a_rc[:, 0], float(2 << g), None, ALU.min)
            ins.then_inc(S("win_counts"), 1)
            pool.wait_ge(S("win_recip"), 1)
            ua, ub, uc = a_u
            pool.wait_ge(S("vec_consts"), 1)
            for j in range(2):
                read_out(pool, ("au", j))
            E = 16 + T
            after(gp.tensor_tensor(ub[:, :, 1:E], ua[:, :, 1:E], ua[:, :, 0:E - 1], ALU.add))
            after(gp.tensor_tensor(uc[:, 1:4, 3:E], ub[:, 1:4, 3:E], ub[:, 1:4, 1:E - 2], ALU.add))
            after(gp.tensor_tensor(ub[:, 2:4, 7:E], uc[:, 2:4, 7:E], uc[:, 2:4, 3:E - 4], ALU.add))
            after(gp.tensor_tensor(uc[:, 3:4, 15:E], ub[:, 3:4, 15:E], ub[:, 3:4, 7:E - 8], ALU.add))
            for g, src in enumerate((ub, uc, ub, uc)):
                ins = gp.tensor_tensor(a_r[:, g], src[:, g, 16:E], a_rc[:, g], ALU.mult)
            after(ins)
            gp.tensor_tensor(a_r, a_r, ua[:, :, 16:E], ALU.subtract).then_inc(S("pooled"), 1)
            def affine(n, l):
                for t in range(TT):
                    pool.wait_ge(S("affine"), 32 * (n + 1))
                    pool.wait_ge(S("normed"), 2 * (l * TT + t + 1))
                    after(gp.tensor_tensor(xt[:, t, :], res[:, t, :], gb[:, 0, :], ALU.mult))
                    gp.tensor_tensor(xt[:, t, :], xt[:, t, :], gb[:, 1, :], ALU.add).then_inc(S("xt_ready"), 1)
                if n + 1 < len(AFF):
                    pool.wait_ge(S("xt_ready"), (l + 1) * TT)
                    load_affine(n + 1)

            for l in range(2):
                affine(l, l)
            pool.wait_ge(S("x_split"), 12)
            gp.dma_start(gw2[0:16, :], A["c_gate_w2"][0]).then_inc(S("gate_w"), 16)
            gp.dma_start(gw2[16:17, :], A["c_gate_b"]).then_inc(S("gate_w"), 16)
            for l in range(2, 4):
                affine(l, l)
            def bmask(ap):
                return ap.unsqueeze(1).broadcast_to([P, 4, P])

            for hb in range(2):
                for t in range(TT):
                    pool.wait_ge(S("decay_exp"), hb * TT + t + 1)
                    gp.tensor_tensor(s_DT[:, t], s_DT[:, t], bmask(tri[:]), ALU.mult)
                    gp.tensor_tensor(s_D[:, t], s_D[:, t], bmask(tril[:]), ALU.mult).then_inc(S("decay_masked"), 1)
                for l in range(1, LEVELS):
                    for t in range(TT):
                        read_out(pool, ("at", hb, t))
                        if l > 1:
                            full(pool, ("Yl", hb, l - 1, t))
                        gp.tensor_tensor(s_Bl[:, t], s_B[:, t], bmask(lvl[:, l]), ALU.mult).then_inc(S("level_mask"), 1)
            pool.wait_ge(S("o_split"), TT + 2 + 4 + 4)
            gp.dma_start(u_w, A["spatial_w_2"][0].rearrange("g t s -> t g s")).then_inc(S("sp_w"), 16)
            pool.wait_ge(S("sp_w"), 16)
            gp.affine_select(out=u_w, in_=u_w, compare_op=ALU.is_ge, fill=0.0, base=0, pattern=[[0, 8], [-1, P]],
                             channel_multiplier=1).then_inc(S("sp_w_masked"), 1)
            for t in range(TT):
                pool.wait_ge(S("affine"), 32 * 5)
                pool.wait_ge(S("sgu_normed"), t + 1)
                after(gp.tensor_tensor(u_v[:, t, :], u_v[:, t, :], gb[:, 0, :], ALU.mult))
                gp.tensor_tensor(u_v[:, t, :], u_v[:, t, :], gb[:, 1, :], ALU.add).then_inc(S("sgu_v"), 1)
            pool.wait_ge(S("sgu_v"), TT)
            load_affine(5)

            affine(5, 4)
            affine(6, 5)

        @block.sync
        def _(sp):
            sp.dma_start(xt[:], A["x"][0].rearrange("(t p) d -> p t d", p=P)).then_inc(S("x_in"), 16)

            def load_vectors():
                sp.wait_ge(S("rows_zero"), 1)
                loads = []

                def load(dst, src):
                    loads.append(sp.dma_start(dst, src).then_inc(S("vectors"), 16))

                for name, layers in (("ln1_g", 2), ("ln1_b", 2), ("ln2_g", 2), ("ln2_b", 2), ("ln1_g_2", 1), ("ln1_b_2", 1), ("ln2_g_2", 1), ("ln2_b_2", 1)):
                    r0 = VEC[name[4] + str((0 if layers == 2 else 4) + int(name[2]) - 1)][0]
                    load(rows[r0:r0 + 8 * layers, :], A[name].rearrange("l (a p) -> (l a) p", p=P))
                for name, src in (("pool_scale", A["a_pool_scale"][0]), ("norm_g", A["c_norm_g"][0]), ("dn_g", A["dn_norm_g_2"][0])):
                    r0, n = VEC[name]
                    load(rows[r0:r0 + n, :], src.rearrange("(a p) -> a p", p=P))
                load(rows[VEC["sp_b"][0]:VEC["sp_b"][0] + 8, :], A["spatial_b_2"][0])
                load(rows[VEC["cmp_b1"][0]:VEC["cmp_b1"][0] + 2, 0:64], A["a_cmp_b1"][0])
                load(rowc[0:96, :], A["conv_w_2"][0].rearrange("j (m p) -> (j m) p", p=P))
                load(rowc[96:P, :], A["a_cmp_pos"][0].rearrange("v (k e) d -> (v k) (e d)", e=2))
                assert 16 * len(loads) == VECTORS

            def load_small():
                loads = []

                def load(dst, src):
                    loads.append(sp.dma_start(dst, src).then_inc(S("small"), 16))

                load(wga[:], A["a_w_in"][0][:, 1280:1304].rearrange("(k p) n -> p k n", p=P))
                load(w2c[:], A["a_cmp_w2"][0].rearrange("v j d -> j v d"))
                load(poolw, A["a_pool_w"][0].rearrange("g c d -> c g d"))
                load(wsm[:], A["c_w_in"][0][:, 3072:3088].rearrange("(k p) n -> p k n", p=P))
                load(wsm2[:], A["w_in_2"][0][:, 4096:4112].rearrange("(k p) n -> p k n", p=P))
                load(wrt[:, :, 0:4], A["router_group_w_2"][0].rearrange("(k p) n -> p k n", p=P))
                load(wrt[:, :, 4:20], A["router_expert_w_2"][0].rearrange("(k p) n -> p k n", p=P))
                load(brt[:, 0:4], A["router_group_b_2"].broadcast_to([P, 4]))
                load(brt[:, 4:20], A["router_expert_b_2"].broadcast_to([P, 16]))
                load(adt[:, 0], A["a_log_2"].broadcast_to([P, 8]))
                load(adt[:, 1], A["dt_bias_2"].broadcast_to([P, 8]))
                assert 16 * len(loads) == SMALL

            for n, (name, parts) in enumerate(chunks):
                if n == 2:
                    load_vectors()
                if n == RING:
                    load_small()
                if n >= RING:
                    before = chunks[n - RING][0]
                    if before in part:
                        sp.wait_ge(S("pieces_split"), part[before] + 1)
                    else:
                        sp.wait_ge(S(f"full{cmp_used[0]}"), cmp_used[1] + 1)
                for (p0, pn), src, (k, c) in parts:
                    dst = ring[p0:p0 + pn, n % RING]
                    if len(src.shape) == 4:
                        dst = dst.rearrange("p (v k n) -> p v k n", v=2, n=c)
                    else:
                        dst = dst.rearrange("p (k n) -> p k n", n=c)
                    sp.dma_start(dst, src).then_inc(S(f"weights{n % RING}"), 16)
            for t in range(TT):
                sp.wait_ge(S("xt_ready"), 5 * TT + t + 1)
                sp.dma_start(out[0, t * P:(t + 1) * P, :], xt[:, t, :]).then_inc(S("stored"), 16)
            sp.wait_ge(S("stored"), 16 * TT)


NAMES = ["x", "a_w_in", "a_cmp_pos", "a_cmp_w1", "a_cmp_b1", "a_cmp_w2", "a_pool_w", "a_pool_scale", "a_w_out", "c_w_in",
         "c_gate_w2", "c_gate_b", "c_norm_g", "c_w_out", "ln1_g", "ln1_b", "ln2_g", "ln2_b", "mlp_w1", "mlp_w2", "w_in_2",
         "conv_w_2", "a_log_2", "dt_bias_2", "dn_norm_g_2", "w_dn_out_2", "sgu_ln_g_2", "sgu_ln_b_2", "spatial_w_2",
         "spatial_b_2", "w_sgu_out_2", "w_out_2", "ln1_g_2", "ln1_b_2", "router_group_w_2", "router_group_b_2",
         "router_expert_w_2", "router_expert_b_2", "expert_w_gate_2", "expert_w_up_2", "expert_w_down_2", "ln2_g_2", "ln2_b_2"]


def kernel(**inputs):
    import numpy as np
    import concourse.bacc as bacc
    from concourse.bass_utils import run_bass_kernel_spmd

    nc = bacc.Bacc("TRN2", target_bir_lowering=False, num_devices=1)
    arrays, aps = {}, {}
    for name in NAMES:
        a = np.ascontiguousarray(inputs[name])
        arrays[f"in_{name}"] = a
        aps[name] = nc.dram_tensor(f"in_{name}", a.shape, mybir.dt.from_np(a.dtype), kind="ExternalInput").ap()
    out = nc.dram_tensor("out_x", (1, T, D), F32, kind="ExternalOutput").ap()
    build(nc, aps, out)
    r = run_bass_kernel_spmd(nc, [arrays], core_ids=[0])
    return r.results[0]["out_x"]
```
